# Optimizing a Trainium2 kernel written in Bass

```python
import jax
import jax.numpy as jnp
from jax import lax
import numpy as np
import jax, jax.numpy as jnp

D_MODEL = 2048
BATCH = 1
SEQ = 256
DEPTH = 2

N_MIXERS = 2
N_RET_LAYERS = (DEPTH + 1) // 2
N_MLA_LAYERS = DEPTH // 2
EPS = 1e-6
ROPE_BASE = 10000.0
BLOCK = 128

RET_HEADS = 8
RET_DK = D_MODEL // RET_HEADS
RET_DV = 2 * RET_DK
RET_WIDTH = RET_HEADS * RET_DV
RET_QK = RET_HEADS * RET_DK
RET_IN = 2 * RET_QK + 2 * RET_WIDTH

MLA_HEADS = 16
MLA_NOPE = 128
MLA_ROPE = 64
MLA_V = 128
MLA_Q_RANK = 512
MLA_KV_RANK = 512
MLA_WIDTH = MLA_HEADS * MLA_V
MLA_IN = MLA_Q_RANK + MLA_KV_RANK + MLA_ROPE + MLA_WIDTH


def rmsnorm(x, g):
    xf = x.astype(jnp.float32)
    y = xf * lax.rsqrt(jnp.mean(xf * xf, axis=-1, keepdims=True) + EPS)
    return (y * g.astype(jnp.float32)).astype(x.dtype)

def rope(x, pos):
    d = x.shape[-1]
    inv_freq = ROPE_BASE ** (-jnp.arange(0, d, 2, dtype=jnp.float32) / d)
    ang = pos.astype(jnp.float32)[:, :, None, None] * inv_freq
    cos = jnp.cos(ang).astype(x.dtype)
    sin = jnp.sin(ang).astype(x.dtype)
    x1, x2 = x[..., : d // 2], x[..., d // 2:]
    return jnp.concatenate([x1 * cos - x2 * sin, x2 * cos + x1 * sin], axis=-1)

def chunkwise_retention(q, k, v):
    B, S, H, _ = q.shape
    nc = S // BLOCK
    log_gamma = jnp.log1p(-jnp.exp2(-5.0 - jnp.arange(H, dtype=jnp.float32)))
    idx = jnp.arange(BLOCK, dtype=jnp.float32)
    diff = idx[:, None] - idx[None, :]
    d_intra = jnp.where(diff >= 0, jnp.exp(log_gamma[:, None, None] * jnp.maximum(diff, 0.0)), 0.0)
    xi = jnp.exp(log_gamma[:, None] * (idx + 1.0))[None, :, :, None]
    zeta = jnp.exp(log_gamma[:, None] * (BLOCK - 1.0 - idx))[None, :, :, None]
    chunk_decay = jnp.exp(log_gamma * BLOCK)[None, :, None, None]

    def to_chunks(t):
        return t.astype(jnp.float32).reshape(B, nc, BLOCK, H, t.shape[-1]).transpose(1, 0, 3, 2, 4)

    def step(state, inp):
        qi, ki, vi = inp
        scores = jnp.einsum('bhnd,bhmd->bhnm', qi, ki) * d_intra
        inner = jnp.einsum('bhnm,bhmv->bhnv', scores, vi)
        cross = jnp.einsum('bhnd,bhdv->bhnv', qi, state) * xi
        state = state * chunk_decay + jnp.einsum('bhmd,bhmv->bhdv', ki, vi * zeta)
        return state, inner + cross

    state0 = jnp.zeros((B, H, q.shape[-1], v.shape[-1]), jnp.float32)
    _, out = lax.scan(step, state0, (to_chunks(q), to_chunks(k), to_chunks(v)))
    return out.transpose(1, 0, 3, 2, 4).reshape(B, S, H, v.shape[-1])

def retention_branch(h, pos, w_in, gn_g, w_out):
    B, S, _ = h.shape
    proj = h @ w_in
    q, k, v, g = jnp.split(proj, [RET_QK, 2 * RET_QK, 2 * RET_QK + RET_WIDTH], axis=-1)
    q = rope(q.reshape(B, S, RET_HEADS, RET_DK), pos)
    k = rope(k.reshape(B, S, RET_HEADS, RET_DK), pos) * (RET_DK ** -0.5)
    v = v.reshape(B, S, RET_HEADS, RET_DV)
    y = chunkwise_retention(q, k, v)
    mu = jnp.mean(y, axis=-1, keepdims=True)
    var = jnp.mean(jnp.square(y - mu), axis=-1, keepdims=True)
    y = (y - mu) * lax.rsqrt(var + EPS)
    y = (y.reshape(B, S, RET_WIDTH) * gn_g.astype(jnp.float32)).astype(h.dtype)
    return (jax.nn.silu(g) * y) @ w_out

def causal_block_attention(q, k, v):
    B, S, H, dq = q.shape
    nb = S // BLOCK
    scale = dq ** -0.5
    qb = q.reshape(B, nb, BLOCK, H, dq).transpose(1, 0, 3, 2, 4)
    kt = k.transpose(0, 2, 1, 3)
    vt = v.transpose(0, 2, 1, 3)
    key_pos = jnp.arange(S)

    def one_block(args):
        i, qi = args
        s = jnp.einsum('bhqd,bhkd->bhqk', qi, kt).astype(jnp.float32) * scale
        qpos = i * BLOCK + jnp.arange(BLOCK)
        s = jnp.where(key_pos[None, :] <= qpos[:, None], s, -1e30)
        p = jax.nn.softmax(s, axis=-1).astype(vt.dtype)
        return jnp.einsum('bhqk,bhkd->bhqd', p, vt)

    o = lax.map(one_block, (jnp.arange(nb), qb))
    return o.transpose(1, 0, 3, 2, 4).reshape(B, S, H, v.shape[-1])

def mla_branch(h, pos, w_in, q_norm_g, w_uq, kv_norm_g, w_ukv, w_out):
    B, S, _ = h.shape
    proj = h @ w_in
    cq, ckv, k_rope, g = jnp.split(
        proj, [MLA_Q_RANK, MLA_Q_RANK + MLA_KV_RANK, MLA_Q_RANK + MLA_KV_RANK + MLA_ROPE], axis=-1)
    q = (rmsnorm(cq, q_norm_g) @ w_uq).reshape(B, S, MLA_HEADS, MLA_NOPE + MLA_ROPE)
    q = jnp.concatenate([q[..., :MLA_NOPE], rope(q[..., MLA_NOPE:], pos)], axis=-1)
    kv = (rmsnorm(ckv, kv_norm_g) @ w_ukv).reshape(B, S, MLA_HEADS, MLA_NOPE + MLA_V)
    k_nope, v = kv[..., :MLA_NOPE], kv[..., MLA_NOPE:]
    k_rope = rope(k_rope[:, :, None, :], pos)
    k = jnp.concatenate([k_nope, jnp.broadcast_to(k_rope, (B, S, MLA_HEADS, MLA_ROPE))], axis=-1)
    o = causal_block_attention(q, k, v).reshape(B, S, MLA_WIDTH)
    return (jax.nn.silu(g) * o) @ w_out

def first_inputs(seed: int = 0) -> dict:
    key = jax.random.key(seed)
    ks = jax.random.split(key, 18)

    def w(k, shape, fan_in, gain=1.0):
        return jax.random.normal(k, shape, jnp.float32) * (gain * fan_in ** -0.5)

    def gain(k, shape):
        return 1.0 + 0.05 * jax.random.normal(k, shape, jnp.float32)

    x = jax.random.normal(ks[0], (BATCH, SEQ, D_MODEL), jnp.float32)
    c = jax.random.normal(ks[1], (BATCH, D_MODEL), jnp.float32)
    start = jax.random.randint(ks[2], (BATCH, 1), 0, 1024, dtype=jnp.int32)
    positions = start + jnp.arange(SEQ, dtype=jnp.int32)[None, :]
    return {
        "x": x,
        "c": c,
        "positions": positions,
        "ada_w": w(ks[3], (DEPTH, D_MODEL, 3 * D_MODEL), D_MODEL, 0.5),
        "ada_b": 0.01 * jax.random.normal(ks[4], (DEPTH, 3 * D_MODEL), jnp.float32),
        "norm_g": gain(ks[5], (DEPTH, D_MODEL)),
        "ret_w_in": w(ks[6], (N_RET_LAYERS, D_MODEL, RET_IN), D_MODEL),
        "ret_gn_g": gain(ks[7], (N_RET_LAYERS, RET_WIDTH)),
        "ret_w_out": w(ks[8], (N_RET_LAYERS, RET_WIDTH, D_MODEL), RET_WIDTH),
        "mla_w_in": w(ks[9], (N_MLA_LAYERS, D_MODEL, MLA_IN), D_MODEL),
        "mla_q_norm_g": gain(ks[10], (N_MLA_LAYERS, MLA_Q_RANK)),
        "mla_w_uq": w(ks[11], (N_MLA_LAYERS, MLA_Q_RANK, MLA_HEADS * (MLA_NOPE + MLA_ROPE)), MLA_Q_RANK),
        "mla_kv_norm_g": gain(ks[12], (N_MLA_LAYERS, MLA_KV_RANK)),
        "mla_w_ukv": w(ks[13], (N_MLA_LAYERS, MLA_KV_RANK, MLA_HEADS * (MLA_NOPE + MLA_V)), MLA_KV_RANK),
        "mla_w_out": w(ks[14], (N_MLA_LAYERS, MLA_WIDTH, D_MODEL), MLA_WIDTH),
        "final_norm_g": gain(ks[15], (D_MODEL,)),
    }

def first_block(x, c, positions, ada_w, ada_b, norm_g, ret_w_in, ret_gn_g, ret_w_out,
              mla_w_in, mla_q_norm_g, mla_w_uq, mla_kv_norm_g, mla_w_ukv, mla_w_out,
              final_norm_g):
    c_act = jax.nn.silu(c)
    for i in range(DEPTH):
        mod = (c_act @ ada_w[i] + ada_b[i])[:, None, :]
        shift, scale, gate = jnp.split(mod, 3, axis=-1)
        h = rmsnorm(x, norm_g[i]) * (1.0 + scale) + shift
        j = i // N_MIXERS
        if i % N_MIXERS == 0:
            y = retention_branch(h, positions, ret_w_in[j], ret_gn_g[j], ret_w_out[j])
        else:
            y = mla_branch(h, positions, mla_w_in[j], mla_q_norm_g[j], mla_w_uq[j],
                           mla_kv_norm_g[j], mla_w_ukv[j], mla_w_out[j])
        x = x + gate * y
    return rmsnorm(x, final_norm_g)


DEPTH_2 = 1

HEAD_DIM = 64
A_HEADS = 8
A_WIDTH = A_HEADS * HEAD_DIM
CHUNK = 128
B_WIDTH = 768
CONV_WIDTH = 3
DILATION_PATTERNS = ((128, 1), (512, 4), (2048, 16))
C_HEADS_PER_PATTERN = 4
C_HEADS = C_HEADS_PER_PATTERN * len(DILATION_PATTERNS)
C_WIDTH = C_HEADS * HEAD_DIM
D_MIX = A_WIDTH + B_WIDTH + C_WIDTH
PROJ_SIZES = (A_WIDTH, A_WIDTH, B_WIDTH, B_WIDTH, B_WIDTH, C_WIDTH, C_WIDTH, C_WIDTH)
PROJ_SPLITS = tuple(int(s) for s in np.cumsum(PROJ_SIZES)[:-1])
D_IN_PROJ = sum(PROJ_SIZES)
D_FF = 4 * D_MODEL


def rms_norm(x, g):
    x32 = x.astype(jnp.float32)
    y = x32 * lax.rsqrt(jnp.mean(x32 * x32, axis=-1, keepdims=True) + EPS)
    return (y * g.astype(jnp.float32)).astype(x.dtype)

def spatial_gating(u, v, w_s, b_s):
    bsz, s = u.shape[:2]
    n_chunks = s // CHUNK
    vc = v.reshape(bsz, n_chunks, CHUNK, A_HEADS, HEAD_DIM)
    w_causal = jnp.tril(w_s)
    mixed = jnp.einsum('hij,bcjhd->bcihd', w_causal, vc) + b_s.T[None, None, :, :, None]
    return u * mixed.reshape(bsz, s, A_WIDTH)

def short_gated_conv(b_gate, c_gate, xb, w_conv):
    z = c_gate * xb
    zp = jnp.pad(z, ((0, 0), (CONV_WIDTH - 1, 0), (0, 0)))
    s = z.shape[1]
    conv = sum(w_conv[i] * zp[:, i:i + s] for i in range(CONV_WIDTH))
    return b_gate * conv

def head_rms_norm(x, g):
    x32 = x.astype(jnp.float32)
    return x32 * lax.rsqrt(jnp.mean(x32 * x32, axis=-1, keepdims=True) + EPS) * g.astype(jnp.float32)

def dilated_window_attention(q, k, v, window, dilation):
    bsz, s, h, d = q.shape
    length = s // dilation
    blk = window // dilation
    nb = -(-length // blk)
    lp = nb * blk

    def to_sub(t):
        t = t.reshape(bsz, length, dilation, h, d).transpose(0, 2, 1, 3, 4)
        t = jnp.pad(t, ((0, 0), (0, 0), (0, lp - length), (0, 0), (0, 0)))
        return t.reshape(bsz, dilation, nb, blk, h, d)

    qb = to_sub(q)
    kb = to_sub(k)
    vb = to_sub(v.astype(jnp.float32))
    pad_prev = ((0, 0), (0, 0), (1, 0), (0, 0), (0, 0), (0, 0))
    kcat = jnp.concatenate([jnp.pad(kb, pad_prev)[:, :, :-1], kb], axis=3)
    vcat = jnp.concatenate([jnp.pad(vb, pad_prev)[:, :, :-1], vb], axis=3)

    scores = jnp.einsum('brnqhd,brnkhd->brnhqk', qb, kcat) * (HEAD_DIM ** -0.5)
    qi = jnp.arange(blk)[:, None]
    kj = jnp.arange(2 * blk)[None, :]
    band = (kj >= qi) & (kj <= qi + blk)
    has_prev = jnp.arange(nb)[:, None, None] > 0
    mask = band[None] & (has_prev | (kj >= blk)[None])
    scores = jnp.where(mask[None, None, :, None], scores, -jnp.inf)
    m = jnp.max(scores, axis=-1, keepdims=True)
    e = jnp.exp(scores - m)
    den = jnp.sum(e, axis=-1, keepdims=True)
    o = jnp.einsum('brnhqk,brnkhd->brnhqd', e, vcat) / den
    lse = (m + jnp.log(den))[..., 0]

    o = o.transpose(0, 1, 2, 4, 3, 5).reshape(bsz, dilation, lp, h, d)[:, :, :length]
    o = o.transpose(0, 2, 1, 3, 4).reshape(bsz, s, h, d)
    lse = lse.transpose(0, 1, 2, 4, 3).reshape(bsz, dilation, lp, h)[:, :, :length]
    lse = lse.transpose(0, 2, 1, 3).reshape(bsz, s, h)
    return o, lse

def dilated_mixture(q, k, v, q_g, k_g):
    bsz, s = q.shape[:2]
    q = head_rms_norm(q.reshape(bsz, s, C_HEADS, HEAD_DIM), q_g)
    k = head_rms_norm(k.reshape(bsz, s, C_HEADS, HEAD_DIM), k_g)
    v = v.reshape(bsz, s, C_HEADS, HEAD_DIM)
    outs, lses = [], []
    for g, (window, dilation) in enumerate(DILATION_PATTERNS):
        sl = slice(g * C_HEADS_PER_PATTERN, (g + 1) * C_HEADS_PER_PATTERN)
        o, lse = dilated_window_attention(q[:, :, sl], k[:, :, sl], v[:, :, sl], window, dilation)
        outs.append(o)
        lses.append(lse)
    alpha = jax.nn.softmax(jnp.stack(lses, axis=0), axis=0)
    y = jnp.stack(outs, axis=0) * alpha[..., None]
    return y.transpose(1, 2, 0, 3, 4).reshape(bsz, s, C_WIDTH).astype(v.dtype)

def second_inputs(seed: int = 0) -> dict:
    key = jax.random.key(seed)
    ks = jax.random.split(key, 12)
    n = jax.random.normal
    f32 = jnp.float32
    return {
        'x': n(ks[0], (BATCH, SEQ, D_MODEL), f32),
        'attn_norm': 1.0 + 0.02 * n(ks[1], (DEPTH_2, D_MODEL), f32),
        'w_in': n(ks[2], (DEPTH_2, D_MODEL, D_IN_PROJ), f32) * D_MODEL ** -0.5,
        'sgu_w': n(ks[3], (DEPTH_2, A_HEADS, CHUNK, CHUNK), f32) * CHUNK ** -0.5,
        'sgu_b': 1.0 + 0.1 * n(ks[4], (DEPTH_2, A_HEADS, CHUNK), f32),
        'conv_w': n(ks[5], (DEPTH_2, CONV_WIDTH, B_WIDTH), f32) * CONV_WIDTH ** -0.5,
        'q_norm': 1.0 + 0.02 * n(ks[6], (DEPTH_2, HEAD_DIM), f32),
        'k_norm': 1.0 + 0.02 * n(ks[7], (DEPTH_2, HEAD_DIM), f32),
        'w_out': n(ks[8], (DEPTH_2, D_MIX, D_MODEL), f32) * D_MIX ** -0.5,
        'mlp_norm': 1.0 + 0.02 * n(ks[9], (DEPTH_2, D_MODEL), f32),
        'w_mlp_in': n(ks[10], (DEPTH_2, D_MODEL, D_FF), f32) * D_MODEL ** -0.5,
        'w_mlp_out': n(ks[11], (DEPTH_2, D_FF, D_MODEL), f32) * D_FF ** -0.5,
    }

def second_block(x, attn_norm, w_in, sgu_w, sgu_b, conv_w, q_norm, k_norm, w_out,
              mlp_norm, w_mlp_in, w_mlp_out):
    for l in range(DEPTH_2):
        h = rms_norm(x, attn_norm[l])
        p = h @ w_in[l]
        a_u, a_v, b_b, b_c, b_x, q, k, v = jnp.split(p, PROJ_SPLITS, axis=-1)
        y_a = spatial_gating(a_u, a_v, sgu_w[l], sgu_b[l])
        y_b = short_gated_conv(b_b, b_c, b_x, conv_w[l])
        y_c = dilated_mixture(q, k, v, q_norm[l], k_norm[l])
        x = x + jnp.concatenate([y_a, y_b, y_c], axis=-1) @ w_out[l]
        h = rms_norm(x, mlp_norm[l])
        x = x + jnp.square(jax.nn.relu(h @ w_mlp_in[l])) @ w_mlp_out[l]
    return x


def setup_inputs(seed=0):
    out = dict(first_inputs(seed))
    for name, value in second_inputs(seed + 1).items():
        if name != "x":
            out[name + "_2"] = value
    return out


def reference(
    x, c, positions, ada_w, ada_b, norm_g, ret_w_in, ret_gn_g, ret_w_out, mla_w_in,
    mla_q_norm_g, mla_w_uq, mla_kv_norm_g, mla_w_ukv, mla_w_out, final_norm_g, attn_norm_2,
    w_in_2, sgu_w_2, sgu_b_2, conv_w_2, q_norm_2, k_norm_2, w_out_2, mlp_norm_2, w_mlp_in_2,
    w_mlp_out_2,
):
    x = first_block(
        x, c, positions, ada_w, ada_b, norm_g, ret_w_in, ret_gn_g, ret_w_out, mla_w_in,
        mla_q_norm_g, mla_w_uq, mla_kv_norm_g, mla_w_ukv, mla_w_out, final_norm_g,
    )
    return second_block(
        x, attn_norm_2, w_in_2, sgu_w_2, sgu_b_2, conv_w_2, q_norm_2, k_norm_2, w_out_2,
        mlp_norm_2, w_mlp_in_2, w_mlp_out_2,
    )


_drawn_inputs = setup_inputs


def setup_inputs(seed=0):
    import zlib

    import numpy as np

    out = dict(_drawn_inputs(seed))
    spreads = {}
    factors = {'ada_b': 4.454,
     'ret_gn_g': 4.329,
     'mla_q_norm_g': 8.0,
     'mla_kv_norm_g': 8.0,
     'attn_norm_2': 2.737,
     'q_norm_2': 41.705,
     'k_norm_2': 38.638,
     'mlp_norm_2': 11.439,
     'sgu_b_2': 4.865}
    for name, (base, spread) in spreads.items():
        noise = np.random.default_rng([zlib.crc32(name.encode()), seed]).standard_normal(out[name].shape)
        drawn = base * np.exp(spread * noise) if base else spread * noise
        out[name] = jnp.asarray(drawn.astype(out[name].dtype))
    for name, factor in factors.items():
        out[name] = (out[name] * factor).astype(out[name].dtype)
    return out
```

```python
from collections import deque
from contextlib import ExitStack

import numpy as np
import concourse.bass as bass
from concourse import mybir

F32 = mybir.dt.float32
F32R = mybir.dt.float32r
I32 = mybir.dt.int32
ALU = mybir.AluOpType
ACT = mybir.ActivationFunctionType
AX_X = mybir.AxisListType.X

P = 128
D = 2048
EPS = 1e-6
RAW = 6
RING = 4
NEG = -1e30
PI = float(np.pi)
PI_IN = 3.1415925
MAGIC = 12582912.0
C1 = 6.28125
C2 = float(np.float32(2.0 * np.pi - C1))
C2 = float((np.array([C2], np.float32).view(np.uint32) & np.uint32(0xFFFFF000)).view(np.float32)[0])
C3 = float(np.float32(2.0 * np.pi - C1 - C2))

COLS = {}
_at = 0
for _name, _n in (("c", 16), ("ada_b", 96), ("norm_g", 32), ("gn_g", 32), ("qn_g", 4), ("kvn_g", 4),
                  ("attn_g", 16), ("mlp_g", 16), ("conv", 18), ("sgu_b", 8), ("q_g", 1), ("k_g", 1)):
    COLS[_name] = (_at, _at + _n)
    _at += _n
NCOL = _at
K_ID, K_MLA, K_FREQ, K_D, K_B2 = 0, 128, 384, 544, 544 + 2048
NCONST = K_B2 + 3 * 384


class Count:

    def __init__(self, handle, step=1):
        self.handle, self.step, self.n = handle, step, 0


class Line:

    def __init__(self, count, steps=False):
        self.count, self.items, self.steps = count, [], steps

    def __call__(self, fn, *waits, inc=True, count=None, free=False):
        tok = None
        if self.steps and not free and self.count.n:
            waits += ((self.count, self.count.n),)
        c = (count or self.count) if inc else None
        if c is not None:
            c.n += c.step
            tok = (c, c.n)
        self.items.append((fn, [w for w in waits if w is not None], c))
        return tok

    def play(self, eng):
        seen = {}
        for fn, waits, c in self.items:
            for s, v in waits:
                if seen.get(s, 0) < v:
                    eng.wait_ge(s.handle, v)
                    seen[s] = v
            ins = fn(eng)
            if c is not None:
                ins.then_inc(c.handle, c.step)


def stream_plan():
    w = []
    for p in range(4):
        w += [("w", "ret_in", p * 48 + i, 1024) for i in range(48)]
        if p >= 2:
            w += [("w", "ret_out", (p - 2) * 32 + i, 1024) for i in range(32)]
    n0 = len(w)
    w += [("w", "mla_in", i, 1024) for i in range(16)]
    w += [("w", "mla_kr", 0, 1024)]
    w += [("w", "mla_in", 16 + i, 1024) for i in range(16)]

    def half(h):
        return ([("w", "uq_n", h * 4 + i, 1024) for i in range(4)] + [("w", "uq_r", h * 4 + i, 512) for i in range(4)]
                + [("w", "ukv_k", h * 4 + i, 1024) for i in range(4)] + [("w", "ukv_v", h * 4 + i, 1024) for i in range(4)])
    w += half(0)
    w += [("w", "mla_in", 32 + i, 1024) for i in range(16)]
    w += half(1)
    w += [("w", "mla_out", i, 1024) for i in range(32)]
    w += [("w", "in2", i, 1024) for i in range(48)]
    w += [("w", "in2h", i, 512) for i in range(16)]
    w += [("w", "in2", 48 + i, 1024) for i in range(32)]
    w += [("w", "out2", i, 1024) for i in range(32)]
    one = [("w", "mlp1", i, 1024) for i in range(128)]
    two = [("w", "mlp2", i, 1024) for i in range(128)]
    w += one[0:16]
    for g in range(1, 8):
        w += one[g * 16:g * 16 + 16] + two[(g - 1) * 16:g * 16]
    w += two[112:128]
    plan = [("ada", 0, g, k) for g in (0, 2, 1, 3) for k in range(16)]
    ada = [("ada", 0, g, k) for g in (4, 5) for k in range(16)]
    ada += [("ada", 1, g, k) for g in (0, 2, 1, 3, 4, 5) for k in range(16)]
    for i, item in enumerate(w):
        plan.append(item)
        if i % 2 == 1 and i < n0:
            plan.append(ada.pop(0))
    assert not ada
    return plan


def fused_blocks(nc, ins, out):
    with ExitStack() as ctx:
        def sb(name, shape, dt=F32):
            return ctx.enter_context(nc.sbuf_tensor(name, shape, dt))

        def sem(name, step=1):
            return Count(ctx.enter_context(nc.semaphore(name)), step)

        raw = sb("raw", [P, RAW, 1024])
        whi = sb("whi", [P, RING, 1024], F32R)
        wlo = sb("wlo", [P, RING, 1024], F32R)
        ahi = sb("ahi", [P, 2, 16, 256], F32R)
        alo = sb("alo", [P, 2, 16, 256], F32R)
        x = sb("x", [P, 2, D])
        cols = sb("cols", [P, NCOL])
        ident = sb("ident", [P, P])
        mmask = sb("mmask", [P, 256])
        ones = sb("ones", [P, P])
        cact = sb("cact", [P, 16])
        mod = sb("mod", [P, 2, 3, 16])
        gsc = sb("gsc", [P, 2, P])
        modt = sb("modt", [P, 8])
        stat = sb("stat", [P, 64])
        mhalf = sb("mhalf", [P, 64])
        NA = 17100
        arena = sb("arena", [P, NA])
        ps = [ctx.enter_context(nc.psum_tensor(f"ps{i}", [P, 512], F32)) for i in range(8)]

        s_raw = [sem(f"s_raw{i}", 16) for i in range(RAW)]
        s_in = [sem(f"s_in{i}", 16) for i in range(12)]
        s_out = sem("s_out", 16)
        pe = Line(sem("s_pe"))
        act = Line(sem("s_act"))
        dve = Line(sem("s_dve"), steps=True)
        pool = Line(sem("s_pool"), steps=True)
        sp = Line(None)

        class Region:
            def __init__(self):
                self.off = 0

            def __call__(self, *shape):
                n = int(np.prod(shape))
                a = arena[:, self.off:self.off + n]
                self.off += n
                assert self.off <= NA, self.off
                if len(shape) == 2:
                    a = a.rearrange("p (a b) -> p a b", a=shape[0])
                if len(shape) == 3:
                    a = a.rearrange("p (a b c) -> p a b c", a=shape[0], b=shape[1])
                return a

        def col(name, i=0, n=1):
            a = COLS[name][0] + i
            return cols[:, a:a + n]

        def load(i, dst, src, *waits):
            return sp(lambda e: e.dma_start(dst, src), *waits, count=s_in[i])

        free = deque((b, None) for b in range(8))

        def take():
            return free.popleft()

        def release(b, tok):
            free.append((b, tok))

        plan = stream_plan()
        state = {"next": 0, "w": 0, "used": 0}
        raw_read = [()] * RAW
        ring_read = [None] * RING
        ready = {}
        acc = {}
        side = deque()
        urgent = deque()

        def pump(upto):
            while state["next"] < len(plan) and state["w"] <= upto:
                n = state["next"]
                state["next"] += 1
                kind = plan[n][0]
                slot = n % RAW
                if kind == "w":
                    _, name, idx, ncol = plan[n]
                    r = raw[:, slot, 0:ncol]
                    t_in = sp(lambda e, r=r, s=ins[name][idx]: e.dma_start(r, s), *raw_read[slot], count=s_raw[slot])
                    i = state["w"]
                    state["w"] += 1
                    q = i % RING
                    hi, lo = whi[:, q, 0:ncol], wlo[:, q, 0:ncol]
                    t_hi = act(lambda e, hi=hi, r=r: e.activation(hi, r, ACT.Copy), t_in, ring_read[q])
                    t_lo = dve(lambda e, hi=hi, lo=lo, r=r: e.tensor_tensor(lo, r, hi.bitcast(F32), ALU.subtract),
                               t_hi, ring_read[q], free=True)
                    ready[i] = (q, t_hi, t_lo)
                    raw_read[slot] = (t_hi, t_lo)
                else:
                    _, layer, g, k = plan[n]
                    r = raw[:, slot, :]
                    t_in = sp(lambda e, r=r, s=ins["ada"][layer, g, k]: e.dma_start(r, s), *raw_read[slot], count=s_raw[slot])
                    raw_read[slot] = (ada_block(layer, g, k, r, t_in),)

        def ada_block(layer, g, k, r, t_in):
            while k == 0 and urgent:
                urgent.popleft()()
            a = accs[acc.get("n", 0) % 2]
            ck = cact[:, k:k + 1]
            if k == 0:
                t = dve(lambda e: e.tensor_scalar(a, r, ck, None, ALU.mult), t_in, t_cact, acc.get(acc.get("n", 0) % 2))
            else:
                t = dve(lambda e: e.scalar_tensor_tensor(out=a, in0=r, scalar=ck, in1=a, op0=ALU.mult, op1=ALU.add),
                        t_in, acc["t"])
            acc["t"] = t
            if k == 15:
                urgent.append(lambda m=acc.get("n", 0): ada_done(layer, g, a, t, m))
                acc["n"] = acc.get("n", 0) + 1
            return t

        def ada_done(layer, g, a, t, m):
            b, w = take()
            for j in range(8):
                tm = pe(lambda e, j=j: e.matmul(ps[b][:, j:j + 1], a[:, j * P:(j + 1) * P], ones[:, 0:1],
                                                start=True, stop=True), t, w, t_ones, inc=(j == 7))
            bc = col("ada_b", layer * 48 + g * 8, 8)
            o = mod[:, layer, g // 2, (g % 2) * 8:(g % 2) * 8 + 8]
            tb = dve(lambda e: e.tensor_tensor(o, ps[b][:, 0:8], bc, ALU.add), tm, t_cols)
            release(b, tb)
            if g // 2 == 1:
                ng = col("norm_g", layer * 16 + (g - 2) * 8, 8)
                tb = dve(lambda e: e.scalar_tensor_tensor(out=o, in0=o, scalar=1.0, in1=ng, op0=ALU.add, op1=ALU.mult), tb)
            mod_tok[layer, g // 2, g % 2] = tb
            acc[m % 2] = tm

        def gate_rows(layer, j, *waits):
            b, w = take()
            for i in range(4):
                gs = gsc[:, i % 2, :]
                t = dve(lambda e, gs=gs, i=i: e.tensor_scalar(gs, ones[:, :], mod[:, layer, 2, 4 * j + i:4 * j + i + 1], None, ALU.mult),
                        mod_tok[layer, 2, j // 2], acc.get(("g", i % 2)))
                acc["g", i % 2] = tm = pe(lambda e, gs=gs, i=i: e.matmul(ps[b][:, i * P:(i + 1) * P], gs, ident[:, :], start=True, stop=True), t, w)
            gate_tok[layer] = act(lambda e: e.activation(gate[:, j * 512:j * 512 + 512], ps[b][:, :], ACT.Copy), tm, *waits)
            release(b, gate_tok[layer])

        at_tok = [[None] * 16 for _ in range(2)]
        at_read = [[None] * 16 for _ in range(2)]

        def step_jobs():
            if urgent:
                urgent.popleft()()
            elif side:
                side.popleft()()

        def drain():
            while urgent:
                urgent.popleft()()
            while side:
                side.popleft()()

        def next_block():
            i = state["used"]
            state["used"] += 1
            pump(i + RING - 1)
            return (i,) + ready.pop(i)

        def gemm(slot, kbs, ncol, evac, jobs=True):
            nt = ncol // 512
            got = {(n, tb): take() for tb in range(2) for n in range(nt)}
            last = len(kbs) - 1
            for i, kb in enumerate(kbs):
                _, q, t_hi, t_lo = next_block()
                for tb in range(2):
                    xh = ahi[:, slot, kb, tb * P:(tb + 1) * P]
                    xl = alo[:, slot, kb, tb * P:(tb + 1) * P]
                    for m, (xs, ws) in enumerate(((xh, whi), (xl, whi), (xh, wlo))):
                        for n in range(nt):
                            b, w = got[n, tb]
                            fin = tb == 1 and m == 2 and n == nt - 1
                            tok = pe(lambda e, b=b, xs=xs, ws=ws, n=n, m=m, i=i, q=q: e.matmul(
                                ps[b][:, :], xs, ws[:, q, n * 512:n * 512 + 512], start=(i == 0 and m == 0),
                                stop=(i == last and m == 2)),
                                w if i == 0 and m == 0 else None, t_lo if m == 2 else t_hi, at_tok[slot][kb],
                                inc=fin or (i == last and m == 2 and n == nt - 1))
                            if tok and i == last:
                                t_done = tok
                                if tb == 0:
                                    t_first = tok
                ring_read[q] = tok
                at_read[slot][kb] = tok
                if jobs and i != last:
                    step_jobs()
            evac({k: v[0] for k, v in got.items()}, (t_first, t_done))
            if jobs:
                step_jobs()

        def gemm_t(slot, kbs, evac):
            got = [take() for _ in range(4)]
            last = len(kbs) - 1
            for i, kb in enumerate(kbs):
                _, q, t_hi, t_lo = next_block()
                xh, xl = ahi[:, slot, kb, :], alo[:, slot, kb, :]
                for m, (xs, ws) in enumerate(((xh, whi), (xl, whi), (xh, wlo))):
                    for c in range(8):
                        b, w = got[c // 2]
                        tok = pe(lambda e, b=b, xs=xs, ws=ws, c=c, m=m, i=i, q=q: e.matmul(
                            ps[b][:, (c % 2) * 256:(c % 2) * 256 + 256], ws[:, q, c * P:(c + 1) * P], xs,
                            start=(i == 0 and m == 0 and c % 2 == 0), stop=(i == last and m == 2), skip_group_check=True),
                            w if i == 0 and m == 0 else None, t_lo if m == 2 else t_hi, at_tok[slot][kb],
                            inc=(m == 2 and c == 7))
                ring_read[q] = tok
                at_read[slot][kb] = tok
                if i != last:
                    step_jobs()
            evac([b for b, _ in got], tok)
            step_jobs()

        def xpose(blocks, *waits):
            b, w = take()
            for i, s in enumerate(blocks):
                tok = pe(lambda e, i=i, s=s: e.transpose(ps[b][:, i * P:(i + 1) * P], s, ident[:, :]),
                         w, t_id, *waits, inc=(i == len(blocks) - 1))
            return b, tok

        def split_at(slot, kb0, nb, b, tok, scale=None):
            parts = [(0, nb)] if scale is None else [(j, 1) for j in range(nb)]
            ops = []
            for j, n in parts:
                src = ps[b][:, j * 256:(j + n) * 256]
                hi = ahi[:, slot, kb0 + j:kb0 + j + n, :].rearrange("p a b -> p (a b)")
                lo = alo[:, slot, kb0 + j:kb0 + j + n, :].rearrange("p a b -> p (a b)")
                war = [at_read[slot][kb0 + j + m] for m in range(n)]
                sc = 1.0 if scale is None else scale(j)
                t1 = act(lambda e, hi=hi, src=src, sc=sc: e.activation(hi, src, ACT.Copy, scale=sc), tok, t_cols, *war)
                ops.append((src, hi, lo, sc, [kb0 + j + m for m in range(n)]))
            for src, hi, lo, sc, kbs in ops:
                t2 = dve(lambda e, hi=hi, lo=lo, src=src, sc=sc: e.scalar_tensor_tensor(
                    out=lo, in0=src, scalar=sc, in1=hi.bitcast(F32), op0=ALU.mult, op1=ALU.subtract), t1, free=True)
                for kb in kbs:
                    at_tok[slot][kb] = t2
            release(b, t2)

        def rstd_of(dst, src, n, *waits):
            w = dst.shape[-1]
            t = pool(lambda e: e.tensor_scalar(dst, src, 1.0 / n, EPS, ALU.mult, ALU.add), *waits)
            return pool(lambda e: e.tensor_tensor(dst, dst, mhalf[:, 0:w], ALU.pow), t, t_mhalf)

        def norm_rows(xn, x_tok):
            t = None
            toks = {}
            for tb in range(2):
                t = act(lambda e, tb=tb: e.activation(xn[:, tb, :], x[:, tb, :], ACT.Square, accum_out=stat[:, tb:tb + 1]), x_tok)
            r = rstd_of(stat[:, 2:4], stat[:, 0:2], D, t)
            for c in range(4):
                s = slice(c * 512, c * 512 + 512)
                toks[c] = (act(lambda e, s=s: e.activation(xn[:, 0, s], x[:, 0, s], ACT.Copy, scale=stat[:, 2:3]), r),
                           dve(lambda e, s=s: e.tensor_scalar(xn[:, 1, s], x[:, 1, s], stat[:, 3:4], None, ALU.mult), r))
            return toks

        def rows_to_at(slot, xn, toks, layer=None, scale=None, tmp=None):
            last = None
            for k2 in range(8):
                blocks = [xn[:, tb, (2 * k2 + j) * P:(2 * k2 + j + 1) * P] for j in range(2) for tb in range(2)]
                b, tok = xpose(blocks, *toks[k2 // 2])
                if layer is None:
                    split_at(slot, 2 * k2, 2, b, tok, lambda j: col(scale, 2 * k2 + j))
                    continue
                for j in range(2):
                    kb = 2 * k2 + j
                    tt = tmp[:, kb % 4, :]
                    t0 = dve(lambda e, b=b, j=j, kb=kb, tt=tt: e.tensor_scalar(
                        tt, ps[b][:, j * 256:j * 256 + 256], mod[:, layer, 1, kb:kb + 1], mod[:, layer, 0, kb:kb + 1],
                        ALU.mult, ALU.add), tok, mod_tok[layer, 0, kb // 8], mod_tok[layer, 1, kb // 8])
                    hi, lo = ahi[:, slot, kb, :], alo[:, slot, kb, :]
                    t1 = act(lambda e, hi=hi, tt=tt: e.activation(hi, tt, ACT.Copy), t0, at_read[slot][kb])
                    t2 = dve(lambda e, hi=hi, lo=lo, tt=tt: e.tensor_tensor(lo, tt, hi.bitcast(F32), ALU.subtract), t1)
                    at_tok[slot][kb] = t2
                release(b, t0)

        def rope(dst, b, tok, heads, half, tabs, tb, scr, war=None):
            n = heads * half
            v = ps[b][:, 0:2 * n].rearrange("p (h c d) -> p h c d", h=heads, c=2)
            d = dst.rearrange("p (h c d) -> p h c d", h=heads, c=2)
            cs, sn = (t[:, tb, :].unsqueeze(1).to_broadcast([P, heads, half]) for t in tabs)
            s = [scr[:, i, 0:n].rearrange("p (h d) -> p h d", h=heads) for i in range(4)]
            ts = []
            for o, a, f in ((s[0], v[:, :, 0, :], cs), (s[1], v[:, :, 1, :], sn), (s[2], v[:, :, 1, :], cs), (s[3], v[:, :, 0, :], sn)):
                ts.append(dve(lambda e, o=o, a=a, f=f: e.tensor_tensor(o, a, f, ALU.mult), tok, t_rope))
            dve(lambda e: e.tensor_tensor(d[:, :, 0, :], s[0], s[1], ALU.subtract), ts[1], war)
            t = dve(lambda e: e.tensor_tensor(d[:, :, 1, :], s[2], s[3], ALU.add), ts[3], war)
            return ts[3], t

        def attend(heads, masks, scale, nm, dn, S, ET, st, scores, values):
            def stage1():
                for third in range(3):
                    b, w = take()
                    hs = heads if third == 0 else heads[2 * third - 2:2 * third]
                    nk = P if third == 0 else 256
                    qs = slice(0, P) if third == 0 else slice(P, 256)
                    for i, h in enumerate(hs):
                        ops = scores(h, qs, slice(0, nk))
                        for j, (l, r, rdy) in enumerate(ops):
                            tok = pe(lambda e, b=b, i=i, j=j, l=l, r=r, nk=nk, m=len(ops): e.matmul(
                                ps[b][:, i * nk:(i + 1) * nk], l, r, start=(j == 0), stop=(j == m - 1)),
                                w, *rdy, inc=(i == len(hs) - 1 and j == len(ops) - 1))
                    n = len(hs)
                    sv = S[:, third, :].rearrange("p (h k) -> p h k", h=n)
                    mk = masks[0 if third == 0 else 1].unsqueeze(1).to_broadcast([P, n, nk])
                    tb, o = (0, 0) if third == 0 else (1, 2 * third - 2)
                    nmx, den = nm[:, tb, o:o + n], dn[:, tb, o:o + n]
                    t0 = dve(lambda e, sv=sv, b=b, mk=mk, n=n: e.tensor_tensor(
                        sv, ps[b][:, :].rearrange("p (h k) -> p h k", h=n), mk, ALU.add), tok, t_mask[0], st.get(("S", third)))
                    release(b, t0)
                    t1 = dve(lambda e, sv=sv, nmx=nmx: e.tensor_reduce(nmx, sv, AX_X, ALU.max), t0)
                    t2 = dve(lambda e, nmx=nmx: e.tensor_scalar(nmx, nmx, -scale, None, ALU.mult), t1)
                    for i in range(n):
                        t3 = act(lambda e, sv=sv, i=i, nmx=nmx, den=den: e.activation(
                            sv[:, i, :], sv[:, i, :], ACT.Exp, bias=nmx[:, i:i + 1], scale=scale, accum_out=den[:, i:i + 1]), t2)
                    st["E", third] = t3
            def stage2():
                for third in range(3):
                    b, tok = xpose([S[:, third, i * P:(i + 1) * P] for i in range(4)], st["E", third])
                    st["S", third] = tok
                    t = act(lambda e, b=b, third=third: e.activation(ET[:, third, :], ps[b][:, :], ACT.Copy), tok, st.get(("ET", third)))
                    st["T", third] = t
                    release(b, t)
            def stage3():
                values(lambda tb, i: ([(ET[:, 0, i * P:(i + 1) * P], 0)] if tb == 0 else
                                      [(ET[:, 1 + i // 2, (i % 2) * 256 + m * P:(i % 2) * 256 + (m + 1) * P], m) for m in range(2)]),
                       [st["T", i] for i in range(3)])
            return [stage1, stage2, stage3]

        K = ins["consts"]
        t_cols = load(0, cols[:, :], ins["cols"])
        t_x = load(1, x[:, :, :], ins["x"].rearrange("o (t p) d -> p (o t) d", p=P))
        t_id = load(2, ident[:, :], K[:, K_ID:K_ID + P])
        R0 = Region()
        accs = [R0(1024), R0(1024)]
        gate = R0(D)
        cos128, sin128, cos32, sin32 = R0(2, P), R0(2, P), R0(2, 32), R0(2, 32)
        base = R0.off
        dtab = R0(8, 256)
        rp = R0(2, 2, 512)
        scr = R0(4, 256)
        qT, kT = R0(4, 256), R0(4, 256)
        v = R0(2, 1024)
        sg = R0(2, 1024)
        sT = R0(2, 384)
        yn = scr.rearrange("p a b -> p (a b)").rearrange("p (a b) -> p a b", a=2)
        bn = R0(2, 16)
        R0b = Region()
        R0b.off = base + 2048
        xn = R0b(2, D)
        htmp = R0b(4, 256)
        pos = R0b(2).bitcast(I32)
        posf = R0b(2)
        freq, ang, kk, rr, rc, mm_ = R0b(160), R0b(2, 160), R0b(2, 160), R0b(2, 160), R0b(2, 160), R0b(2, 160)
        t_pos = load(3, pos, ins["pos"])
        t_freq = load(4, freq, K[:, K_FREQ:K_FREQ + 160])
        t_D = load(6, dtab, K[:, K_D:K_D + 2048].rearrange("p (a b) -> p a b", a=8))
        t_mask = [load(7, mmask[:, :], K[:, K_MLA:K_MLA + 256])]
        t_ones = pool(lambda e: e.memset(ones[:, :], 1.0))
        t_mhalf = pool(lambda e: e.memset(mhalf[:, :], -0.5))
        mod_tok, gate_tok = {}, {}
        t_cact = act(lambda e: e.activation(cact[:, :], col("c", 0, 16), ACT.Silu), t_cols)
        toks = norm_rows(xn, t_x)

        t = dve(lambda e: e.tensor_copy(posf, pos), t_pos)
        for tb in range(2):
            t1 = dve(lambda e, tb=tb: e.tensor_scalar(ang[:, tb, :], freq, posf[:, tb:tb + 1], None, ALU.mult), t, t_freq)
        t = dve(lambda e: e.tensor_scalar(kk, ang, 1.0 / (2.0 * PI), MAGIC, ALU.mult, ALU.add), t1)
        t = dve(lambda e: e.tensor_scalar(kk, kk, MAGIC, None, ALU.subtract), t)
        for i, cc in enumerate((C1, C2, C3)):
            src = ang if i == 0 else rr
            t = dve(lambda e, cc=cc, src=src: e.scalar_tensor_tensor(out=rr, in0=kk, scalar=-cc, in1=src, op0=ALU.mult, op1=ALU.add), t)
        t = dve(lambda e: e.tensor_scalar(mm_, rr, PI / 2, -2.0 * PI, ALU.is_gt, ALU.mult), t)
        t = dve(lambda e: e.scalar_tensor_tensor(out=rc, in0=rr, scalar=PI / 2, in1=mm_, op0=ALU.add, op1=ALU.add), t)
        t = dve(lambda e: e.tensor_scalar(rc, rc, PI_IN, -PI_IN, ALU.min, ALU.max), t)
        t = dve(lambda e: e.tensor_scalar(rr, rr, PI_IN, -PI_IN, ALU.min, ALU.max), t)
        for o, s, a in ((cos128, rc, 0), (sin128, rr, 0), (cos32, rc, 128), (sin32, rr, 128)):
            w = o.shape[-1]
            t_rope = act(lambda e, o=o, s=s, a=a, w=w: e.activation(o, s[:, :, a:a + w], ACT.Sin), t)

        pump(RING - 1)
        drain()
        rows_to_at(0, xn, toks, layer=0, tmp=htmp)

        L = {}

        def qk_evac(banks, toks):
            for n in range(2):
                for tb in range(2):
                    b = banks[n, tb]
                    t_b, L["rp", n] = rope(rp[:, n, tb, :], b, toks[tb], 2, 128, (cos128, sin128), tb, scr, L.get(("rpT", n)))
                    release(b, t_b)

        def qk_turn(n, j):
            blocks = [rp[:, n, tb, (2 * j + i) * P:(2 * j + i + 1) * P] for i in range(2) for tb in range(2)]
            b, tok = xpose(blocks, L["rp", n])
            L["rpT", n] = tok
            dst = (qT, kT)[n][:, 2 * j:2 * j + 2, :].rearrange("p a b -> p (a b)")
            L["qkT", n, j] = act(lambda e: e.activation(dst, ps[b][:, :], ACT.Copy), tok, L.get("scores"))
            release(b, L["qkT", n, j])

        def v_evac(banks, toks):
            for tb in range(2):
                for n in range(2):
                    b = banks[n, tb]
                    L["v"] = act(lambda e, b=b, n=n, tb=tb: e.activation(v[:, tb, n * 512:n * 512 + 512], ps[b][:, :], ACT.Copy),
                                 toks[tb], L.get("pv"))
                    release(b, L["v"])

        def g_evac(banks, toks):
            for tb in range(2):
                for n in range(2):
                    b = banks[n, tb]
                    L["sg"] = act(lambda e, b=b, n=n, tb=tb: e.activation(sg[:, tb, n * 512:n * 512 + 512], ps[b][:, :], ACT.Silu),
                                  toks[tb], L.get("zT"))
                    release(b, L["sg"])

        def ret_scores(p, h):
            b, w = take()
            for lo_, n, q0 in ((0, 256, 0), (256, 128, 128)):
                for c in range(2):
                    tok = pe(lambda e, lo_=lo_, n=n, q0=q0, c=c: e.matmul(
                        ps[b][:, lo_:lo_ + n], kT[:, 2 * h + c, q0:q0 + P], qT[:, 2 * h + c, q0:q0 + n],
                        start=(c == 0), stop=(c == 1)), w, L["qkT", 0, h], L["qkT", 1, h], inc=(q0 == 128 and c == 1))
            L["scores"] = tok
            dt = dtab[:, 2 * p + h, :]
            t = dve(lambda e: e.tensor_tensor(sT[:, h, 0:256], ps[b][:, 0:256], dt, ALU.mult), tok, t_D, L.get(("sTr", h)))
            L["sT", h] = dve(lambda e: e.tensor_tensor(sT[:, h, 256:384], ps[b][:, 256:384], dt[:, 0:P], ALU.mult), tok)
            release(b, L["sT", h])

        def ret_values(p, h):
            hs = slice(h * 512, h * 512 + 512)
            for tb in range(2):
                b, w = take()
                if tb == 0:
                    tok = pe(lambda e, b=b: e.matmul(ps[b][:, :], sT[:, h, 0:P], v[:, 0, hs], start=True, stop=True), w, L["sT", h], L["v"])
                else:
                    pe(lambda e, b=b: e.matmul(ps[b][:, :], sT[:, h, P:256], v[:, 0, hs], start=True, stop=False), w, inc=False)
                    tok = pe(lambda e, b=b: e.matmul(ps[b][:, :], sT[:, h, 256:384], v[:, 1, hs], start=False, stop=True))
                L["pv"] = L["sTr", h] = tok
                bs = bn[:, tb, :]
                t = dve(lambda e, b=b, bs=bs: e.bn_stats(bs[:, 0:6], ps[b][:, :]), tok)
                t = dve(lambda e, bs=bs: e.bn_aggr(bs[:, 6:8], bs[:, 0:6]), t)
                r = rstd_of(bs[:, 8:9], bs[:, 7:8], 1, t)
                t = dve(lambda e, bs=bs: e.tensor_scalar(bs[:, 9:10], bs[:, 6:7], bs[:, 8:9], -1.0, ALU.mult, ALU.mult), r)
                t = act(lambda e, b=b, bs=bs, tb=tb: e.activation(yn[:, tb, :], ps[b][:, :], ACT.Identity, scale=bs[:, 8:9], bias=bs[:, 9:10]),
                        t, L.get(("z", tb)))
                release(b, t)
                L["z", tb] = dve(lambda e, tb=tb: e.tensor_tensor(sg[:, tb, hs], yn[:, tb, :], sg[:, tb, hs], ALU.mult), t, L["sg"])

        def ret_turn(p, j):
            blocks = [sg[:, tb, (2 * j + i) * P:(2 * j + i + 1) * P] for i in range(2) for tb in range(2)]
            b, tok = xpose(blocks, L["z", 0], L["z", 1])
            L["zT"] = tok
            split_at(1, (p % 2) * 8 + 2 * j, 2, b, tok, lambda i: col("gn_g", p * 8 + 2 * j + i))

        ytmp = scr.rearrange("p a b -> p (a b)")
        Y = {"n": 0}

        def residual(layer, g, last=False):
            def evac(banks, toks):
                for tb in range(2):
                    for n in range(2):
                        b = banks[n, tb]
                        cs = slice(g * 1024 + n * 512, g * 1024 + n * 512 + 512)
                        tmp = Y["tmp"][:, (Y["n"] % 2) * 512:(Y["n"] % 2) * 512 + 512]
                        Y["n"] += 1
                        t = dve(lambda e, b=b, cs=cs, tmp=tmp: e.tensor_tensor(tmp, ps[b][:, :], gate[:, cs], ALU.mult),
                                toks[tb], gate_tok[layer])
                        release(b, t)
                        L["x"] = dve(lambda e, cs=cs, tb=tb, tmp=tmp: e.tensor_tensor(x[:, tb, cs], x[:, tb, cs], tmp, ALU.add), t)
                        Y["g"] = t
            return evac

        Y["tmp"] = ytmp
        for p in range(4):
            if p == 2:
                side += [lambda j=j: gate_rows(0, j) for j in range(4)]
            gemm(0, range(16), 1024, qk_evac)
            for n, j in ((0, 0), (1, 0), (0, 1), (1, 1)):
                side.append(lambda n=n, j=j: qk_turn(n, j))
            gemm(0, range(16), 1024, v_evac)
            gemm(0, range(16), 1024, g_evac)
            side += [lambda h=h, p=p: ret_scores(p, h) for h in range(2)]
            side += [lambda h=h, p=p: ret_values(p, h) for h in range(2)]
            if p == 2:
                for g in range(2):
                    gemm(1, range(16), 1024, residual(0, g))
                drain()
            side += [lambda j=j, p=p: ret_turn(p, j) for j in range(4)]
        for g in range(2):
            gemm(1, range(8), 1024, residual(0, g))
        drain()
        for g in range(2):
            gemm(1, range(8, 16), 1024, residual(0, g))
        drain()

        R1 = Region()
        R1.off = base
        sg1 = R1(2, 1024)
        rows = R1(2, 1024)
        qT1, kT1 = R1(8, 256), rows.rearrange("p a b -> p (a b)").rearrange("p (a b) -> p a b", a=8)
        v1 = R1(2, 1024)
        qr, qrT = R1(2, 512), R1(4, 256)
        kr = R1(2, P)
        ET = R1(3, 512)
        scr1 = ET.rearrange("p a b -> p (a b)")[:, 0:1024].rearrange("p (a b) -> p a b", a=4)
        R1a = Region()
        S, krE, krO = R1a(3, 512), R1a(256), R1a(256)
        nm1, dn1 = R1(2, 16), R1(2, 16)
        st1 = R1(8)
        htmp1 = S.rearrange("p a b -> p (a b)")[:, 0:1024].rearrange("p (a b) -> p a b", a=4)
        xn1 = arena[:, base:base + 2 * D].rearrange("p (a b) -> p a b", a=2)
        toks = norm_rows(xn1, L["x"])
        rows_to_at(1, xn1, toks, layer=1, tmp=htmp1)
        t_xn = at_tok[1][15]
        M = {}
        t_kr0 = pool(lambda e: e.memset(krE, 0.0), t_xn)
        t_kr0 = pool(lambda e: e.memset(krO, 0.0), t_xn)

        def c_evac(banks, toks):
            for n in range(2):
                for tb in range(2):
                    b = banks[n, tb]
                    o = rows[:, tb, n * 512:n * 512 + 512]
                    i = n * 2 + tb
                    t = act(lambda e, b=b, o=o: e.activation(o, ps[b][:, :], ACT.Copy), toks[tb], t_xn)
                    t2 = act(lambda e, b=b, i=i: e.activation(S[:, 0, :], ps[b][:, :], ACT.Square, accum_out=st1[:, i:i + 1]), M.get("sq"))
                    M["sq"] = t2
                    release(b, t2)
            M["r"] = rstd_of(st1[:, 4:8], st1[:, 0:4], 512, M["sq"])

        def c_scale(n):
            for tb in range(2):
                o = rows[:, tb, n * 512:n * 512 + 512]
                i = n * 2 + tb
                M["rows", n, tb] = dve(lambda e, o=o, i=i: e.tensor_scalar(o, o, st1[:, 4 + i:5 + i], None, ALU.mult), M["r"])

        def c_turn(n, j):
            blocks = [rows[:, tb, n * 512 + (2 * j + i) * P:n * 512 + (2 * j + i + 1) * P] for i in range(2) for tb in range(2)]
            b, tok = xpose(blocks, M["rows", n, 0], M["rows", n, 1])
            M["rowsT"] = tok
            split_at(0, 4 * n + 2 * j, 2, b, tok, lambda i: col(("qn_g", "kvn_g")[n], 2 * j + i))

        def krope():
            b, w = take()
            _, q, t_hi, t_lo = next_block()
            for tb in range(2):
                for kb in range(16):
                    xh, xl = (a[:, 1, kb, tb * P:(tb + 1) * P] for a in (ahi, alo))
                    for m, (xs, ws) in enumerate(((xh, whi), (xl, whi), (xh, wlo))):
                        tok = pe(lambda e, tb=tb, xs=xs, ws=ws, kb=kb, m=m, q=q: e.matmul(
                            ps[b][:, tb * 64:tb * 64 + 64], xs, ws[:, q, kb * 64:kb * 64 + 64],
                            start=(kb == 0 and m == 0), stop=(kb == 15 and m == 2)), w, t_hi, t_lo, at_tok[1][kb],
                            inc=(tb == 1 and kb == 15 and m == 2))
            ring_read[q] = tok
            v4 = ps[b][:, 0:128].rearrange("p (t c d) -> p t c d", t=2, c=2)
            s = [scr1[:, i, 0:64].rearrange("p (t d) -> p t d", t=2) for i in range(4)]
            ts = []
            for o, a, f in ((s[0], v4[:, :, 0, :], cos32), (s[1], v4[:, :, 1, :], sin32), (s[2], v4[:, :, 1, :], cos32), (s[3], v4[:, :, 0, :], sin32)):
                ts.append(dve(lambda e, o=o, a=a, f=f: e.tensor_tensor(o, a, f, ALU.mult), tok, t_rope))
            release(b, ts[3])
            for o in (0, 64):
                dve(lambda e, o=o: e.tensor_tensor(kr[:, :, o:o + 32], s[0], s[1], ALU.subtract), ts[1])
                M["kr"] = dve(lambda e, o=o: e.tensor_tensor(kr[:, :, o + 32:o + 64], s[2], s[3], ALU.add), ts[3])

        def kr_turn():
            b, tok = xpose([kr[:, 0, :], kr[:, 1, :]], M["kr"])
            act(lambda e: e.activation(krE[0:64, :], ps[b][0:64, 0:256], ACT.Copy), tok, t_kr0)
            M["krT"] = act(lambda e: e.activation(krO[64:128, :], ps[b][64:128, 0:256], ACT.Copy))
            release(b, M["krT"])

        def g1_evac(h):
            def evac(banks, toks):
                for tb in range(2):
                    for n in range(2):
                        b = banks[n, tb]
                        M["sg", h] = act(lambda e, b=b, n=n, tb=tb: e.activation(sg1[:, tb, n * 512:n * 512 + 512], ps[b][:, :], ACT.Silu), toks[tb], M.get("zT"))
                        release(b, M["sg", h])
            return evac

        def heads_evac(name, dst, last):
            def evac(banks, tok):
                for j, b in enumerate(banks):
                    o = dst[:, 2 * j:2 * j + 2, :].rearrange("p a b -> p (a b)")
                    if j % 2:
                        M[name, 1] = t = act(lambda e, b=b, o=o: e.activation(o, ps[b][:, :], ACT.Copy), tok, M.get(last), M["rowsT"])
                    else:
                        M[name, 0] = t = dve(lambda e, b=b, o=o: e.tensor_copy(o, ps[b][:, :]), tok, M.get(last), M["rowsT"])
                    release(b, t)
            return evac

        def qr_evac(banks, toks):
            for tb in range(2):
                b = banks[0, tb]
                t_b, M["qr"] = rope(qr[:, tb, :], b, toks[tb], 8, 32, (cos32, sin32), tb, scr1, M.get("qrT_read"))
                release(b, t_b)

        def qr_turn(j):
            blocks = [qr[:, tb, (2 * j + i) * P:(2 * j + i + 1) * P] for i in range(2) for tb in range(2)]
            b, tok = xpose(blocks, M["qr"])
            M["qrT_read"] = tok
            M["qrT"] = act(lambda e: e.activation(qrT[:, 2 * j:2 * j + 2, :].rearrange("p a b -> p (a b)"), ps[b][:, :], ACT.Copy), tok, M.get("scores"))
            release(b, M["qrT"])

        def v1_evac(banks, toks):
            for tb in range(2):
                for n in range(2):
                    b = banks[n, tb]
                    M["v"] = act(lambda e, b=b, n=n, tb=tb: e.activation(v1[:, tb, n * 512:n * 512 + 512], ps[b][:, :], ACT.Copy),
                                 toks[tb], M.get("pv"))
                    release(b, M["v"])

        A = {}

        def mla_scores(h, qs, ks):
            rdy = (M["q", 0], M["q", 1], M["k", 0], M["k", 1], M["qrT"], M["krT"])
            return [(qT1[:, h, qs], kT1[:, h, ks], rdy),
                    (qrT[:, h // 2, qs], (krE, krO)[h % 2][:, ks], ())]

        def mla_values(half, quad):
            def values(parts, rdy):
                dn = dn1[:, :, quad * 4:quad * 4 + 4]
                t_r = dve(lambda e: e.reciprocal(dn, dn), *rdy)
                M["scores"] = A["S", 2]
                for tb in range(2):
                    b, w = take()
                    for i in range(4):
                        hh = quad * 4 + i
                        ops = parts(tb, i)
                        for j, (l, m) in enumerate(ops):
                            tok = pe(lambda e, b=b, i=i, hh=hh, l=l, m=m, j=j, k=len(ops): e.matmul(
                                ps[b][:, i * P:(i + 1) * P], l, v1[:, m, hh * P:(hh + 1) * P], start=(j == 0), stop=(j == k - 1)),
                                w, M["v"], *rdy, inc=(i == 3 and j == len(ops) - 1))
                    M["pv"] = tok
                    for third in range(3):
                        A["ET", third] = tok
                    for i in range(4):
                        hh = quad * 4 + i
                        z = sg1[:, tb, hh * P:(hh + 1) * P]
                        M["z"] = dve(lambda e, b=b, i=i, tb=tb, z=z, hh=hh: e.scalar_tensor_tensor(
                            out=z, in0=ps[b][:, i * P:(i + 1) * P], scalar=dn1[:, tb, hh:hh + 1], in1=z, op0=ALU.mult, op1=ALU.mult),
                            tok, t_r, M["sg", half])
                    release(b, M["z"])
            return values

        def z_turn(half, j):
            blocks = [sg1[:, tb, (2 * j + i) * P:(2 * j + i + 1) * P] for i in range(2) for tb in range(2)]
            b, tok = xpose(blocks, M["z"])
            M["zT"] = tok
            split_at(half, (8 if half == 0 else 0) + 2 * j, 2, b, tok)

        def mla_half(half):
            jobs = []
            for quad in range(2):
                jobs += attend(list(range(4 * quad, 4 * quad + 4)), (mmask[:, P:256], mmask[:, :]), 192.0 ** -0.5,
                               nm1[:, :, quad * 4:quad * 4 + 4], dn1[:, :, quad * 4:quad * 4 + 4], S, ET, A, mla_scores, mla_values(half, quad))
                jobs += [lambda j=j: z_turn(half, 2 * quad_ + j) for quad_ in (quad,) for j in range(2)]
            return jobs

        gemm(1, range(16), 1024, c_evac)
        side += [lambda: c_scale(0), lambda: c_turn(0, 0), lambda: c_turn(0, 1), lambda: c_scale(1), lambda: c_turn(1, 0), lambda: c_turn(1, 1)]
        krope()
        side.append(kr_turn)
        side += [lambda j=j: gate_rows(1, j, Y["g"]) for j in range(4)]
        gemm(1, range(16), 1024, g1_evac(0))
        drain()
        for half in range(2):
            gemm_t(0, range(0, 4), heads_evac("q", qT1, "scores"))
            gemm(0, range(0, 4), 512, qr_evac)
            side += [lambda j=j: qr_turn(j) for j in range(2)]
            gemm_t(0, range(4, 8), heads_evac("k", kT1, "scores"))
            gemm(0, range(4, 8), 1024, v1_evac)
            drain()
            side += mla_half(half)
            if half == 0:
                gemm(1, range(16), 1024, g1_evac(1))
                drain()
        Y["tmp"] = qr.rearrange("p a b -> p (a b)")
        for half in range(2):
            for g in range(2):
                gemm(half, range(8, 16) if half == 0 else range(0, 8), 1024, residual(1, g))
            drain()

        fg = gate
        t_fg = load(9, fg, ins["final_norm_g"].unsqueeze(0).to_broadcast([P, D]), Y["g"])
        R2 = Region()
        R2.off = 2048
        R2(D)
        xn2 = R2(2, D)
        for tb in range(2):
            t = act(lambda e, tb=tb: e.activation(xn2[:, tb, :], x[:, tb, :], ACT.Square, accum_out=stat[:, tb:tb + 1]), L["x"])
        r = rstd_of(stat[:, 2:4], stat[:, 0:2], D, t)
        for tb in range(2):
            L["x"] = dve(lambda e, tb=tb: e.scalar_tensor_tensor(out=x[:, tb, :], in0=x[:, tb, :], scalar=stat[:, 2 + tb:3 + tb], in1=fg,
                                                                 op0=ALU.mult, op1=ALU.mult), r, t_fg)
        toks = norm_rows(xn2, L["x"])
        rows_to_at(0, xn2, toks, scale="attn_g")
        t_xn = at_tok[0][15]

        R2 = Region()
        qk = R2(2, 1536)
        qT2 = R2(6, 256)
        kE, kO = R2(6, 256), R2(6, 256)
        v2 = R2(2, 768)
        S2, ET2 = R2(3, 512), R2(3, 512)
        bmask = R2(3, 384)
        yc = R2(2, 768)
        nm2, dn2 = R2(2, 3, 4), R2(2, 3, 4)
        lse, cf, mx, t4 = R2(2, 3, 4), R2(2, 3, 4), R2(2, 4), R2(2, 4)
        hs_, hr = R2(2, 24), R2(2, 24)
        Rk = Region()
        Rk.off = 3072 + 1536
        av, au, wsT = Rk(2, 512), Rk(2, 512), Rk(8, P)
        sq = S2.rearrange("p a b -> p (a b)")
        Rc = Region()
        Rc.off = 3072 + 1536 + 3072 + 1536 + 1536
        bt, yb, zp = Rc(256), Rc(256), Rc(2, 258)
        qk_flat = qk.rearrange("p a b -> p (a b)")
        zz = qk_flat[:, 0:1536].rearrange("p (a b) -> p a b", a=2)
        bb = qk_flat[:, 1536:3072].rearrange("p (a b) -> p a b", a=2)
        B = {}
        t_ws = load(10, wsT, ins["sgu_wT"], t_xn)
        t_bm = load(11, bmask, K[:, K_B2:K_B2 + 3 * 384].rearrange("p (a b) -> p a b", a=3), t_xn)
        t_ws = pool(lambda e: e.affine_select(out=wsT, in_=wsT, compare_op=ALU.is_ge, fill=0.0, base=0,
                                              pattern=[[0, 8], [1, P]], channel_multiplier=-1), t_ws)

        def clear_keys():
            pool(lambda e: e.memset(kE, 0.0), B["yaT"])
            B["kz"] = pool(lambda e: e.memset(kO, 0.0))

        def copies(*moves):
            def evac(banks, toks):
                for tb in range(2):
                    for n in range(2):
                        if (n, tb) not in banks:
                            continue
                        b = banks[n, tb]
                        for mn, cs, dst, name, war in moves:
                            if mn == n:
                                B[name] = t = act(lambda e, b=b, cs=cs, d=dst(tb): e.activation(d, ps[b][:, cs], ACT.Copy),
                                                  toks[tb], t_xn, B.get(war))
                        release(b, t)
            return evac

        full = slice(0, 512)

        def head_norm(tb):
            t = dve(lambda e: e.tensor_tensor(sq, qk[:, tb, :], qk[:, tb, :], ALU.mult), B["qk0"], B["qk1"], B["qk2"], B.get("hn"))
            t = dve(lambda e: e.tensor_reduce(hs_[:, tb, :], sq.rearrange("p (h d) -> p h d", h=24), AX_X, ALU.add), t)
            B["hn"] = t
            B["hr", tb] = rstd_of(hr[:, tb, :], hs_[:, tb, :], 64, t)

        def head_scale(tb):
            q3 = qk[:, tb, :].rearrange("p (h d) -> p h d", h=24)
            B["qkn", tb] = dve(lambda e: e.tensor_tensor(q3, q3, hr[:, tb, :].unsqueeze(2).to_broadcast([P, 24, 64]), ALU.mult), B["hr", tb])

        def qk2_turn(j):
            blocks = [qk[:, tb, (2 * j + i) * P:(2 * j + i + 1) * P] for i in range(2) for tb in range(2)]
            b, tok = xpose(blocks, B["qkn", 0], B["qkn", 1])
            B["qkT"] = tok
            if j < 3:
                B["qT"] = t = act(lambda e: e.activation(qT2[:, 2 * j:2 * j + 2, :].rearrange("p a b -> p (a b)"), ps[b][:, :], ACT.Copy,
                                                         scale=col("q_g")), tok)
            else:
                for half, dst in ((slice(0, 64), kE), (slice(64, 128), kO)):
                    B["kT"] = t = act(lambda e, half=half, dst=dst: e.activation(
                        dst[half, 2 * j - 6:2 * j - 4, :].rearrange("p a b -> p (a b)"), ps[b][half, :], ACT.Copy,
                        scale=cols[half, COLS["k_g"][0]:COLS["k_g"][1]]), tok, B["kz"])
            release(b, t)

        def c_scores(h, qs, ks):
            return [(qT2[:, h // 2, qs], (kE, kO)[h % 2][:, h // 2, ks], (B["qT"], B["kT"]))]

        A2 = {}

        def c_values(g):
            def values(parts, rdy):
                b, w = take()
                for tb in range(2):
                    for i in range(4):
                        h = 4 * g + i
                        ops = parts(tb, i)
                        for j, (l, m) in enumerate(ops):
                            tok = pe(lambda e, tb=tb, i=i, l=l, m=m, j=j, k=len(ops), h=h: e.matmul(
                                ps[b][:, tb * 256 + i * 64:tb * 256 + (i + 1) * 64], l, v2[:, m, h * 64:(h + 1) * 64],
                                start=(j == 0), stop=(j == k - 1)), w, B["v0"], B["v1"], *rdy, inc=(tb == 1 and i == 3 and j == 1))
                for third in range(3):
                    A2["ET", third] = tok
                B["yc"] = act(lambda e: e.activation(yc[:, :, g * 256:(g + 1) * 256], ps[b][:, :].rearrange("p (t c) -> p t c", t=2), ACT.Copy), tok)
                release(b, B["yc"])
            return values

        def mixture():
            t = act(lambda e: e.activation(lse, dn2, ACT.Ln), B["yc"])
            t = dve(lambda e: e.tensor_tensor(lse, lse, nm2, ALU.subtract), t)
            t = dve(lambda e: e.tensor_tensor(mx, lse[:, :, 0, :], lse[:, :, 1, :], ALU.max), t)
            t = dve(lambda e: e.tensor_tensor(mx, mx, lse[:, :, 2, :], ALU.max), t)
            for g in range(3):
                t1 = dve(lambda e, g=g: e.tensor_tensor(cf[:, :, g, :], lse[:, :, g, :], mx, ALU.subtract), t)
            t = act(lambda e: e.activation(cf, cf, ACT.Exp), t1)
            t = dve(lambda e: e.tensor_tensor(t4, cf[:, :, 0, :], cf[:, :, 1, :], ALU.add), t)
            t = dve(lambda e: e.tensor_tensor(t4, t4, cf[:, :, 2, :], ALU.add), t)
            for g in range(3):
                t1 = dve(lambda e, g=g: e.tensor_tensor(lse[:, :, g, :], dn2[:, :, g, :], t4, ALU.mult), t)
            t = dve(lambda e: e.reciprocal(lse, lse), t1)
            t = dve(lambda e: e.tensor_tensor(cf, cf, lse, ALU.mult), t)
            for tb in range(2):
                y3 = yc[:, tb, :].rearrange("p (h d) -> p h d", h=12)
                c3 = cf[:, tb, :, :].rearrange("p g i -> p (g i)").unsqueeze(2).to_broadcast([P, 12, 64])
                B["ycn", tb] = dve(lambda e, y3=y3, c3=c3: e.tensor_tensor(y3, y3, c3, ALU.mult), t)

        def yc_turn(j):
            blocks = [yc[:, tb, (2 * j + i) * P:(2 * j + i + 1) * P] for i in range(2) for tb in range(2)]
            b, tok = xpose(blocks, B["ycn", 0], B["ycn", 1])
            split_at(1, 10 + 2 * j, 2, b, tok)

        def gating(tb):
            b, w = take()
            for h in range(8):
                tok = pe(lambda e, h=h: e.matmul(ps[b][:, h * 64:(h + 1) * 64], wsT[:, h, :], av[:, tb, h * 64:(h + 1) * 64], start=True, stop=True),
                         w, t_ws, B["av"], inc=(h == 7))
            a3 = av[:, tb, :].rearrange("p (h d) -> p h d", h=8)
            b3 = col("sgu_b", 0, 8).unsqueeze(2).to_broadcast([P, 8, 64])
            t = dve(lambda e: e.tensor_tensor(a3, ps[b][:, :].rearrange("p (h d) -> p h d", h=8), b3, ALU.add), tok, t_cols)
            release(b, t)
            B["ya", tb] = dve(lambda e: e.tensor_tensor(au[:, tb, :], au[:, tb, :], av[:, tb, :], ALU.mult), t, B["au"])

        def ya_turn(j):
            blocks = [au[:, tb, (2 * j + i) * P:(2 * j + i + 1) * P] for i in range(2) for tb in range(2)]
            b, tok = xpose(blocks, B["ya", 0], B["ya", 1])
            B["yaT"] = tok
            split_at(1, 2 * j, 2, b, tok)

        def cx_evac(n_c, c_cols, n_x, x_cols, dst_cols, other=None):
            def evac(banks, toks):
                for tb in range(2):
                    bc, bx = banks[n_c, tb], banks[n_x, tb]
                    z = zz[:, tb, dst_cols]
                    t = act(lambda e, bc=bc, z=z: e.activation(z, ps[bc][:, c_cols], ACT.Copy), toks[tb], B["qkT"])
                    t = dve(lambda e, bx=bx, z=z: e.tensor_tensor(z, z, ps[bx][:, x_cols], ALU.mult), t)
                    B["z", tb] = t
                    release(bx, t)
                    if n_c != n_x:
                        release(bc, t)
                    if other is not None:
                        bo = banks[1, tb]
                        B["b0"] = act(lambda e, bo=bo, tb=tb: e.activation(bb[:, tb, 0:512], ps[bo][:, :], ACT.Copy), toks[tb])
                        release(bo, B["b0"])
            return evac

        def conv_turn(f):
            blocks = [a[:, tb, f * P:(f + 1) * P] for a in (zz, bb) for tb in range(2)]
            b, tok = xpose(blocks, B["z", 0], B["z", 1], B["b0"], B["b1"])
            zq = zp[:, f % 2, :]
            t = act(lambda e: e.activation(zq[:, 2:258], ps[b][:, 0:256], ACT.Copy), tok, B["zp0"], B.get(("zp", f % 2)))
            t = dve(lambda e: e.tensor_scalar(bt, zq[:, 0:256], col("conv", 3 * f), None, ALU.mult), t)
            t = dve(lambda e: e.scalar_tensor_tensor(out=bt, in0=zq[:, 1:257], scalar=col("conv", 3 * f + 1), in1=bt, op0=ALU.mult, op1=ALU.add), t)
            t = dve(lambda e: e.scalar_tensor_tensor(out=bt, in0=zq[:, 2:258], scalar=col("conv", 3 * f + 2), in1=bt, op0=ALU.mult, op1=ALU.add), t)
            B["zp", f % 2] = t
            t = dve(lambda e: e.tensor_tensor(yb, bt, ps[b][:, 256:512], ALU.mult), t, B.get("yb"))
            release(b, t)
            hi, lo = ahi[:, 1, 4 + f, :], alo[:, 1, 4 + f, :]
            t1 = act(lambda e: e.activation(hi, yb, ACT.Copy), t, at_read[1][4 + f])
            at_tok[1][4 + f] = B["yb"] = dve(lambda e: e.tensor_tensor(lo, yb, hi.bitcast(F32), ALU.subtract), t1)

        t_mask[0] = t_bm
        gemm(0, range(16), 1024, copies((0, full, lambda tb: av[:, tb, :], "av", None), (1, full, lambda tb: au[:, tb, :], "au", None)))
        side += [lambda: gating(0), lambda: gating(1), lambda: ya_turn(0), lambda: ya_turn(1), clear_keys]
        gemm(0, range(16), 1024, copies((0, full, lambda tb: qk[:, tb, 0:512], "qk0", None), (1, full, lambda tb: qk[:, tb, 512:1024], "qk1", None)))
        gemm(0, range(16), 1024, copies((0, full, lambda tb: qk[:, tb, 1024:1536], "qk2", None), (1, full, lambda tb: v2[:, tb, 0:512], "v0", None)))
        side += [lambda: head_norm(0), lambda: head_norm(1), lambda: head_scale(0), lambda: head_scale(1)]
        side += [lambda j=j: qk2_turn(j) for j in range(6)]

        def b1_evac(banks, toks):
            drain()
            copies((0, slice(0, 256), lambda tb: bb[:, tb, 512:768], "b1", "qkT"), (0, slice(256, 512), lambda tb: v2[:, tb, 512:768], "v1", None))(banks, toks)

        gemm(0, range(16), 512, b1_evac)
        for g in range(3):
            side += attend(list(range(4 * g, 4 * g + 4)), (bmask[:, g, 0:P], bmask[:, g, P:384]), 0.125,
                           nm2[:, :, g, :], dn2[:, :, g, :], S2, ET2, A2, c_scores, c_values(g))
        side += [mixture] + [lambda j=j: yc_turn(j) for j in range(3)]
        gemm(0, range(16), 1024, cx_evac(0, full, 1, full, slice(0, 512)))
        gemm(0, range(16), 1024, cx_evac(0, slice(0, 256), 0, slice(256, 512), slice(512, 768), other=True))
        drain()
        B["zp0"] = pool(lambda e: e.memset(zp, 0.0), A2["ET", 2])
        side += [lambda f=f: conv_turn(f) for f in range(6)]

        def add_x(g, final=False):
            def evac(banks, toks):
                for tb in range(2):
                    for n in range(2):
                        b = banks[n, tb]
                        cs = slice(g * 1024 + n * 512, g * 1024 + n * 512 + 512)
                        L["x"] = dve(lambda e, b=b, cs=cs, tb=tb: e.tensor_tensor(x[:, tb, cs], ps[b][:, :], x[:, tb, cs], ALU.add), toks[tb], L["x"])
                        release(b, L["x"])
                        if final:
                            L["out"] = sp(lambda e, cs=cs, tb=tb: e.dma_start(out[0, tb * P:(tb + 1) * P, cs], x[:, tb, cs]), L["x"], count=s_out)
            return evac

        order = list(range(0, 4)) + list(range(10, 16)) + list(range(4, 10))
        for g in range(2):
            gemm(1, order, 1024, add_x(g))
        drain()

        R3 = Region()
        xn3 = R3(2, D)
        u = R3(2, 2, 1024)
        toks = norm_rows(xn3, L["x"])
        rows_to_at(0, xn3, toks, scale="mlp_g")
        U = {}

        def u_evac(g):
            def evac(banks, toks):
                for tb in range(2):
                    for n in range(2):
                        b = banks[n, tb]
                        o = u[:, g % 2, tb, n * 512:n * 512 + 512]
                        t = act(lambda e, b=b, o=o: e.activation(o, ps[b][:, :], ACT.Relu), toks[tb], U.get(("uT", g % 2)))
                        release(b, t)
                        U["u", g] = pool(lambda e, o=o: e.tensor_tensor(o, o, o, ALU.mult), t)
            return evac

        def u_turn(g, j):
            blocks = [u[:, g % 2, tb, (2 * j + i) * P:(2 * j + i + 1) * P] for i in range(2) for tb in range(2)]
            b, tok = xpose(blocks, U["u", g])
            U["uT", g % 2] = tok
            split_at(1, (g % 2) * 8 + 2 * j, 2, b, tok)

        for g in range(8):
            gemm(0, range(16), 1024, u_evac(g))
            side += [lambda g=g, j=j: u_turn(g, j) for j in range(4)]
            if g == 0:
                continue
            for n in range(2):
                gemm(1, range(((g - 1) % 2) * 8, ((g - 1) % 2) * 8 + 8), 1024, add_x(n))
        drain()
        for n in range(2):
            gemm(1, range(8, 16), 1024, add_x(n, final=True))
        assert not side and not urgent and state["used"] == state["w"] and state["next"] == len(plan)
        t_out = L["out"]

        block = ctx.enter_context(nc.Block())

        @block.sync
        def _(eng):
            sp.play(eng)
            eng.wait_ge(t_out[0].handle, t_out[1])

        @block.scalar
        def _(eng):
            act.play(eng)

        @block.vector
        def _(eng):
            dve.play(eng)

        @block.gpsimd
        def _(eng):
            pool.play(eng)

        @block.tensor
        def _(eng):
            pe.play(eng)


def constants():
    k = np.zeros((P, NCONST), np.float32)
    k[:, K_ID:K_ID + P] = np.eye(P, dtype=np.float32)
    i = np.arange(P)
    t = np.arange(256)
    k[:, K_MLA + P:K_MLA + 256] = np.where(i[None, :] <= i[:, None], 0.0, NEG)
    for d, a in ((256, 0), (64, 128)):
        f = 10000.0 ** (-np.arange(0, d, 2, dtype=np.float64) / d)
        k[:, K_FREQ + a:K_FREQ + a + d // 2] = f.astype(np.float32)[None, :]
    for h in range(8):
        lg = np.log1p(-np.exp2(-5.0 - h))
        diff = t[None, :] - i[:, None]
        k[:, K_D + h * 256:K_D + (h + 1) * 256] = np.where(diff >= 0, np.exp(lg * np.maximum(diff, 0)), 0.0) / 16.0
    for g, (w, d) in enumerate(((128, 1), (512, 4), (2048, 16))):
        def mask(q, s):
            gap = q[:, None] - s[None, :]
            return np.where((gap >= 0) & (gap <= w) & (gap % d == 0), 0.0, NEG)
        o = K_B2 + g * 384
        k[:, o:o + P] = mask(i, i)
        k[:, o + P:o + 384] = mask(i + P, t)
    return k


def tiles(w, groups, kbs=None):
    kb = w.shape[0] // P
    w3 = w.reshape(kb, P, w.shape[1])
    parts = []
    for cols in groups:
        a = np.concatenate([w3[:, :, s] for s in cols], axis=2) if len(cols) > 1 else w3[:, :, cols[0]]
        parts.append(a[list(kbs)] if kbs is not None else a)
    return np.ascontiguousarray(np.concatenate(parts, axis=0))


def layout(inp):
    a = {k: np.asarray(v) for k, v in inp.items()}
    sl = slice
    g = {}
    w = a["ret_w_in"][0]
    grp = []
    for p in range(4):
        grp += [[sl(p * 512, p * 512 + 512), sl(2048 + p * 512, 2048 + p * 512 + 512)],
                [sl(4096 + p * 1024, 4096 + (p + 1) * 1024)], [sl(8192 + p * 1024, 8192 + (p + 1) * 1024)]]
    g["ret_in"] = tiles(w, grp)
    two = [[sl(0, 1024)], [sl(1024, 2048)]]
    wo = a["ret_w_out"][0]
    g["ret_out"] = np.concatenate([tiles(wo[0:2048], two), tiles(wo[2048:3072], two), tiles(wo[3072:4096], two)])
    w = a["mla_w_in"][0]
    g["mla_in"] = tiles(w, [[sl(0, 1024)], [sl(1088, 2112)], [sl(2112, 3136)]])
    g["mla_kr"] = np.ascontiguousarray(w[:, 1024:1088].reshape(16, P, 64).transpose(1, 0, 2).reshape(1, P, 1024))
    w = a["mla_w_uq"][0].reshape(512, 16, 192)
    g["uq_n"] = tiles(np.ascontiguousarray(w[:, :, 0:128]).reshape(512, 2048), two)
    g["uq_r"] = tiles(np.ascontiguousarray(w[:, :, 128:192]).reshape(512, 1024), [[sl(0, 512)], [sl(512, 1024)]])
    w = a["mla_w_ukv"][0].reshape(512, 16, 256)
    g["ukv_k"] = tiles(np.ascontiguousarray(w[:, :, 0:128]).reshape(512, 2048), two)
    g["ukv_v"] = tiles(np.ascontiguousarray(w[:, :, 128:256]).reshape(512, 2048), two)
    w = a["mla_w_out"][0]
    g["mla_out"] = np.concatenate([tiles(w[0:1024], two), tiles(w[1024:2048], two)])
    w = a["w_in_2"][0]
    au, av, bb, bc, bx, q, k, v = 0, 512, 1024, 1792, 2560, 3328, 4096, 4864
    g["in2"] = tiles(w, [
        [sl(av, av + 512), sl(au, au + 512)],
        [sl(q, q + 768), sl(k, k + 256)], [sl(k + 256, k + 768), sl(v, v + 512)], [sl(bc, bc + 512), sl(bx, bx + 512)],
        [sl(bc + 512, bc + 768), sl(bx + 512, bx + 768), sl(bb, bb + 512)]])
    g["in2h"] = tiles(w, [[sl(bb + 512, bb + 768), sl(v + 512, v + 768)]])
    g["out2"] = tiles(a["w_out_2"][0], two, list(range(0, 4)) + list(range(10, 16)) + list(range(4, 10)))
    g["mlp1"] = tiles(a["w_mlp_in_2"][0], [[sl(i * 1024, (i + 1) * 1024)] for i in range(8)])
    w = a["w_mlp_out_2"][0]
    g["mlp2"] = np.concatenate([tiles(w[i * 1024:(i + 1) * 1024], two) for i in range(8)])
    g["ada"] = np.ascontiguousarray(a["ada_w"].reshape(2, 16, P, 6, 1024).transpose(0, 3, 1, 2, 4))
    def colm(v):
        return v.reshape(-1, P).T
    ab = a["ada_b"]
    parts = [colm(a["c"][0]), colm(ab[0]), colm(ab[1]), colm(a["norm_g"].reshape(-1)), colm(a["ret_gn_g"][0]),
             colm(a["mla_q_norm_g"][0]), colm(a["mla_kv_norm_g"][0]), colm(a["attn_norm_2"][0]), colm(a["mlp_norm_2"][0]),
             a["conv_w_2"][0].reshape(3, 6, P).transpose(2, 1, 0).reshape(P, 18), a["sgu_b_2"][0].T,
             np.concatenate([a["q_norm_2"][0]] * 2)[:, None], np.concatenate([a["k_norm_2"][0]] * 2)[:, None]]
    g["cols"] = np.ascontiguousarray(np.concatenate(parts, axis=1))
    g["pos"] = np.ascontiguousarray(a["positions"].reshape(2, P).T)
    g["x"] = a["x"]
    g["final_norm_g"] = a["final_norm_g"]
    g["sgu_wT"] = np.ascontiguousarray(a["sgu_w_2"][0].transpose(2, 0, 1))
    g["consts"] = constants()
    return g


def kernel(**inputs):
    from concourse import bacc, mybir as mb
    from concourse.bass_utils import run_bass_kernel_spmd

    nc = bacc.Bacc("TRN2", target_bir_lowering=False, num_devices=1)
    arrays, ins = {}, {}
    for name, a in layout(inputs).items():
        arrays[f"in_{name}"] = a
        ins[name] = nc.dram_tensor(f"in_{name}", a.shape, mb.dt.from_np(a.dtype), kind="ExternalInput").ap()
    out = nc.dram_tensor("out_0", (1, 256, D), mb.dt.float32, kind="ExternalOutput").ap()
    fused_blocks(nc, ins, out)
    r = run_bass_kernel_spmd(nc, [arrays], core_ids=[0])
    return r.results[0]["out_0"]
```

```python
from collections import deque
from contextlib import ExitStack

import numpy as np
import concourse.bass as bass
from concourse import mybir

F32 = mybir.dt.float32
F32R = mybir.dt.float32r
I32 = mybir.dt.int32
ALU = mybir.AluOpType
ACT = mybir.ActivationFunctionType
AX_X = mybir.AxisListType.X

P = 128
D = 2048
EPS = 1e-6
RAW = 6
RING = 4
POOLED = 256
AHEAD = 20
PHASES = [range(4 * i, 4 * i + 4) for i in range(4)]
NEG = -1e30
PI = float(np.pi)
PI_IN = 3.1415925
MAGIC = 12582912.0
C1 = 6.28125
C2 = float(np.float32(2.0 * np.pi - C1))
C2 = float((np.array([C2], np.float32).view(np.uint32) & np.uint32(0xFFFFF000)).view(np.float32)[0])
C3 = float(np.float32(2.0 * np.pi - C1 - C2))

COLS = {}
_at = 0
for _name, _n in (("c", 16), ("ada_b", 96), ("norm_g", 32), ("gn_g", 32), ("qn_g", 4), ("kvn_g", 4),
                  ("attn_g", 16), ("mlp_g", 16), ("final_g", 16), ("conv", 18), ("sgu_b", 8), ("q_g", 1), ("k_g", 1)):
    COLS[_name] = (_at, _at + _n)
    _at += _n
NCOL = _at
K_ID, K_MLA, K_FREQ, K_D, K_B2 = 0, 128, 384, 544, 544 + 2048
NCONST = K_B2 + 3 * 384


class Count:

    def __init__(self, handle, step=1):
        self.handle, self.step, self.n = handle, step, 0


class Line:

    def __init__(self, count, steps=False):
        self.count, self.items, self.steps = count, [], steps

    def __call__(self, fn, *waits, inc=True, count=None, free=False):
        tok = None
        if self.steps and not free and self.count.n:
            waits += ((self.count, self.count.n),)
        c = (count or self.count) if inc else None
        if c is not None:
            c.n += c.step
            tok = (c, c.n)
        self.items.append((fn, [w for w in waits if w is not None], c))
        return tok

    def play(self, eng):
        seen = {}
        for fn, waits, c in self.items:
            for s, v in waits:
                if seen.get(s, 0) < v:
                    eng.wait_ge(s.handle, v)
                    seen[s] = v
            ins = fn(eng)
            if c is not None:
                ins.then_inc(c.handle, c.step)


def stream_plan():
    w = [("w", "ret_in", g * 16 + kb, 1024) for kbs in PHASES for g in range(3) for kb in kbs]
    first = len(w)
    for p in range(1, 4):
        w += [("w", "ret_in", p * 48 + i, 1024) for i in range(48)]
        if p >= 2:
            w += [("w", "ret_out", (p - 2) * 32 + i, 1024) for i in range(32)]
    n0 = len(w)
    w += [("w", "mla_in", i, 1024) for i in range(16)]
    w += [("w", "mla_kr", 0, 1024)]
    w += [("w", "mla_in", 16 + i, 1024) for i in range(16)]

    def half(h):
        return ([("w", "uq_n", h * 4 + i, 1024) for i in range(4)] + [("w", "uq_r", h * 4 + i, 512) for i in range(4)]
                + [("w", "ukv_k", h * 4 + i, 1024) for i in range(4)] + [("w", "ukv_v", h * 4 + i, 1024) for i in range(4)])
    w += half(0)
    w += [("w", "mla_in", 32 + i, 1024) for i in range(16)]
    w += half(1)
    w += [("w", "mla_out", i, 1024) for i in range(32)]
    w += [("w", "in2", i, 1024) for i in range(48)]
    w += [("w", "in2h", i, 512) for i in range(16)]
    w += [("w", "in2", 48 + i, 1024) for i in range(32)]
    w += [("w", "out2", i, 1024) for i in range(32)]
    one = [("w", "mlp1", i, 1024) for i in range(128)]
    two = [("w", "mlp2", i, 1024) for i in range(128)]
    w += one[0:16]
    for g in range(1, 8):
        w += one[g * 16:g * 16 + 16] + two[(g - 1) * 16:g * 16]
    w += two[112:128]
    ada = [("ada", 0, g, k) for g in range(4) for k in range(16)]
    plan, ada = ada[:AHEAD], ada[AHEAD:]
    for i in range(first):
        plan.append(w[i])
        while ada and 64 - len(ada) < AHEAD + (i + 1) * 4 / 3:
            plan.append(ada.pop(0))
    ada = [("ada", 0, g, k) for g in (4, 5) for k in range(16)]
    ada += [("ada", 1, g, k) for g in range(6) for k in range(16)]
    total = len(ada)
    for i, item in enumerate(w[first:]):
        plan.append(item)
        while ada and total - len(ada) < (i + 1) * total // (n0 - first - 8):
            plan.append(ada.pop(0))
    assert not ada
    return plan


def fused_blocks(nc, ins, out):
    with ExitStack() as ctx:
        def sb(name, shape, dt=F32):
            return ctx.enter_context(nc.sbuf_tensor(name, shape, dt))

        def sem(name, step=1):
            return Count(ctx.enter_context(nc.semaphore(name)), step)

        raw = sb("raw", [P, RAW, 1024])
        whi = sb("whi", [P, RING, 1024], F32R)
        wlo = sb("wlo", [P, RING, 1024], F32R)
        ahi = sb("ahi", [P, 2, 16, 256], F32R)
        alo = sb("alo", [P, 2, 16, 256], F32R)
        x = sb("x", [P, 2, D])
        cols = sb("cols", [P, NCOL])
        ident = sb("ident", [P, P])
        mmask = sb("mmask", [P, 256])
        ones = sb("ones", [P, P])
        cact = sb("cact", [P, 16])
        mod = sb("mod", [P, 2, 3, 16])
        gsc = sb("gsc", [P, 2, P])
        dg = sb("dg", [P, 2, P])
        stat = sb("stat", [P, 64])
        mhalf = sb("mhalf", [P, 64])
        NA = 16860
        arena = sb("arena", [P, NA])
        ps = [ctx.enter_context(nc.psum_tensor(f"ps{i}", [P, 512], F32)) for i in range(8)]

        s_raw = [sem(f"s_raw{i}", 16) for i in range(RAW)]
        s_in = [sem(f"s_in{i}", 16) for i in range(12)]
        s_out = sem("s_out", 16)
        pe = Line(sem("s_pe"))
        act = Line(sem("s_act"))
        dve = Line(sem("s_dve"), steps=True)
        pool = Line(sem("s_pool"), steps=True)
        sp = Line(None)

        class Region:
            def __init__(self):
                self.off = 0

            def __call__(self, *shape):
                n = int(np.prod(shape))
                a = arena[:, self.off:self.off + n]
                self.off += n
                assert self.off <= NA, self.off
                if len(shape) == 2:
                    a = a.rearrange("p (a b) -> p a b", a=shape[0])
                if len(shape) == 3:
                    a = a.rearrange("p (a b c) -> p a b c", a=shape[0], b=shape[1])
                return a

        def col(name, i=0, n=1):
            a = COLS[name][0] + i
            return cols[:, a:a + n]

        def load(i, dst, src, *waits):
            return sp(lambda e: e.dma_start(dst, src), *waits, count=s_in[i])

        free = deque((b, None) for b in range(8))

        def take():
            return free.popleft()

        def release(b, tok):
            free.append((b, tok))

        plan = stream_plan()
        state = {"next": 0, "w": 0, "used": 0}
        raw_read = [()] * RAW
        ring_read = [None] * RING
        ready = {}
        acc = {}
        side = deque()
        urgent = deque()

        def pump(upto, stop=None):
            while state["next"] < (stop or len(plan)) and (stop or state["w"] <= upto):
                n = state["next"]
                state["next"] += 1
                kind = plan[n][0]
                slot = n % RAW
                if kind == "w":
                    _, name, idx, ncol = plan[n]
                    r = raw[:, slot, 0:ncol]
                    t_in = sp(lambda e, r=r, s=ins[name][idx]: e.dma_start(r, s), *raw_read[slot], count=s_raw[slot])
                    i = state["w"]
                    state["w"] += 1
                    q = i % RING
                    hi, lo = whi[:, q, 0:ncol], wlo[:, q, 0:ncol]
                    t_hi = act(lambda e, hi=hi, r=r: e.activation(hi, r, ACT.Copy), t_in, ring_read[q])
                    line = pool if i < POOLED and i % 4 == 3 else dve
                    t_lo = line(lambda e, hi=hi, lo=lo, r=r: e.tensor_tensor(lo, r, hi.bitcast(F32), ALU.subtract),
                                t_hi, ring_read[q], free=True)
                    ready[i] = (q, t_hi, t_lo)
                    raw_read[slot] = (t_hi, t_lo)
                else:
                    _, layer, g, k = plan[n]
                    r = raw[:, slot, :]
                    t_in = sp(lambda e, r=r, s=ins["ada"][layer, g, k]: e.dma_start(r, s), *raw_read[slot], count=s_raw[slot])
                    raw_read[slot] = (ada_block(layer, g, k, r, t_in),)

        def ada_block(layer, g, k, r, t_in):
            while k == 0 and urgent:
                urgent.popleft()[1]()
            m = acc.get("n", 0)
            main, other = accs[m % 2], accs[(m + 1) % 2]
            second = k > 2 and k % 2 == 1
            a = other if second else main
            ck = cact[:, k:k + 1]
            if k in (0, 3):
                t = dve(lambda e: e.tensor_scalar(a, r, ck, None, ALU.mult), t_in, t_cact, acc.get(("read", k == 3)), free=True)
            else:
                t = dve(lambda e: e.scalar_tensor_tensor(out=a, in0=r, scalar=ck, in1=a, op0=ALU.mult, op1=ALU.add),
                        t_in, acc["t", second], free=True)
            acc["t", second] = t
            if k == 15:
                ts = dve(lambda e: e.tensor_tensor(main, main, other, ALU.add), t, acc["t", False])
                acc["read", False] = ts
                urgent.append((state["used"] + (1 if layer == 0 and g < 4 else 3), lambda: ada_done(layer, g, main, ts)))
                acc["n"] = m + 1
            return t

        def ada_done(layer, g, a, t):
            if g < 4:
                o = mod[:, layer, 0:2, 4 * g:4 * g + 4]
                a0 = COLS["ada_b"][0] + layer * 48
                bc = cols[:, a0:a0 + 32].rearrange("p (c j) -> p c j", c=2)[:, :, 4 * g:4 * g + 4]
            else:
                o = mod[:, layer, 2, 8 * (g - 4):8 * g - 24]
                bc = col("ada_b", layer * 48 + 32 + 8 * (g - 4), 8)
            if layer == 0 and g < 4:
                b, w = take()
                for j in range(8):
                    tm = pe(lambda e, j=j: e.matmul(ps[b][:, j:j + 1], a[:, j * P:(j + 1) * P], ones[:, 0:1],
                                                    start=True, stop=True), t, w, t_ones, inc=(j == 7))
                acc["read", True] = tm
                tb = dve(lambda e: e.tensor_tensor(o, ps[b][:, 0:8].rearrange("p (c j) -> p c j", c=2), bc, ALU.add), tm, t_cols)
                release(b, tb)
            else:
                got = [take() for _ in range(2)]
                for j, (b, w) in enumerate(got):
                    tm = pe(lambda e, b=b, j=j: e.matmul(ps[b][:, :], ones[:, :], a[:, j * 512:j * 512 + 512], start=True, stop=True), t, w, t_ones)
                for j, (b, w) in enumerate(got):
                    tb = dve(lambda e, b=b, j=j: e.tensor_tensor(
                        a[:, j * 512:j * 512 + 512].rearrange("p (c d) -> p c d", c=4), ps[b][:, :].rearrange("p (c d) -> p c d", c=4),
                        ident[:, :].unsqueeze(1).to_broadcast([P, 4, P]), ALU.mult), tm, t_id)
                    release(b, tb)
                a4 = a.rearrange("p (c j d) -> p c j d", c=2, j=4) if g < 4 else a.rearrange("p (j d) -> p j d", j=8)
                acc["read", True] = tb = dve(lambda e: e.tensor_reduce(o, a4, AX_X, ALU.add), tb)
                tb = dve(lambda e: e.tensor_tensor(o, o, bc, ALU.add), tb, t_cols)
            if g < 4:
                oa = mod[:, layer, 1, 4 * g:4 * g + 4]
                ng = col("norm_g", layer * 16 + 4 * g, 4)
                tb = dve(lambda e: e.scalar_tensor_tensor(out=oa, in0=oa, scalar=1.0, in1=ng, op0=ALU.add, op1=ALU.mult), tb)
            mod_tok[layer, g] = tb

        def gate_rows(layer, j, *waits):
            b, w = take()
            for i in range(4):
                gs = gsc[:, i % 2, :]
                t = dve(lambda e, gs=gs, i=i: e.tensor_scalar(gs, ones[:, :], mod[:, layer, 2, 4 * j + i:4 * j + i + 1], None, ALU.mult),
                        mod_tok[layer, 4 + j // 2], acc.get(("g", i % 2)))
                acc["g", i % 2] = tm = pe(lambda e, gs=gs, i=i: e.matmul(ps[b][:, i * P:(i + 1) * P], gs, ident[:, :], start=True, stop=True), t, w)
            gate_tok[layer] = act(lambda e: e.activation(gate[:, j * 512:j * 512 + 512], ps[b][:, :], ACT.Copy), tm, *waits)
            release(b, gate_tok[layer])

        at_tok = [[None] * 16 for _ in range(2)]
        at_read = [[None] * 16 for _ in range(2)]

        def step_jobs():
            if urgent and state["used"] >= urgent[0][0]:
                urgent.popleft()[1]()
            elif side:
                job = side.popleft()
                if job:
                    job()

        def drain():
            while urgent:
                urgent.popleft()[1]()
            while side:
                job = side.popleft()
                if job:
                    job()

        def next_block():
            i = state["used"]
            state["used"] += 1
            pump(i + RING - 1)
            return (i,) + ready.pop(i)

        def gemm(slot, kbs, ncol, evac, jobs=True):
            nt = ncol // 512
            got = {(n, tb): take() for tb in range(2) for n in range(nt)}
            last = len(kbs) - 1
            for i, kb in enumerate(kbs):
                _, q, t_hi, t_lo = next_block()
                for tb in range(2):
                    xh = ahi[:, slot, kb, tb * P:(tb + 1) * P]
                    xl = alo[:, slot, kb, tb * P:(tb + 1) * P]
                    for m, (xs, ws) in enumerate(((xh, whi), (xl, whi), (xh, wlo))):
                        for n in range(nt):
                            b, w = got[n, tb]
                            fin = tb == 1 and m == 2 and n == nt - 1
                            tok = pe(lambda e, b=b, xs=xs, ws=ws, n=n, m=m, i=i, q=q: e.matmul(
                                ps[b][:, :], xs, ws[:, q, n * 512:n * 512 + 512], start=(i == 0 and m == 0),
                                stop=(i == last and m == 2)),
                                w if i == 0 and m == 0 else None, t_lo if m == 2 else t_hi, at_tok[slot][kb],
                                inc=fin or (i == last and m == 2 and n == nt - 1))
                            if tok and i == last:
                                t_done = tok
                                if tb == 0:
                                    t_first = tok
                ring_read[q] = tok
                at_read[slot][kb] = tok
                if jobs and i != last:
                    step_jobs()
            evac({k: v[0] for k, v in got.items()}, (t_first, t_done))
            if jobs:
                step_jobs()

        def gemm_t(slot, kbs, evac):
            got = [take() for _ in range(4)]
            last = len(kbs) - 1
            for i, kb in enumerate(kbs):
                _, q, t_hi, t_lo = next_block()
                xh, xl = ahi[:, slot, kb, :], alo[:, slot, kb, :]
                for m, (xs, ws) in enumerate(((xh, whi), (xl, whi), (xh, wlo))):
                    for c in range(8):
                        b, w = got[c // 2]
                        tok = pe(lambda e, b=b, xs=xs, ws=ws, c=c, m=m, i=i, q=q: e.matmul(
                            ps[b][:, (c % 2) * 256:(c % 2) * 256 + 256], ws[:, q, c * P:(c + 1) * P], xs,
                            start=(i == 0 and m == 0 and c % 2 == 0), stop=(i == last and m == 2), skip_group_check=True),
                            w if i == 0 and m == 0 else None, t_lo if m == 2 else t_hi, at_tok[slot][kb],
                            inc=(m == 2 and c == 7))
                ring_read[q] = tok
                at_read[slot][kb] = tok
                if i != last:
                    step_jobs()
            evac([b for b, _ in got], tok)
            step_jobs()

        def xpose(blocks, *waits):
            b, w = take()
            for i, s in enumerate(blocks):
                tok = pe(lambda e, i=i, s=s: e.transpose(ps[b][:, i * P:(i + 1) * P], s, ident[:, :]),
                         w, t_id, *waits, inc=(i == len(blocks) - 1))
            return b, tok

        def split_at(slot, kb0, nb, b, tok, scale=None):
            parts = [(0, nb)] if scale is None else [(j, 1) for j in range(nb)]
            ops = []
            for j, n in parts:
                src = ps[b][:, j * 256:(j + n) * 256]
                hi = ahi[:, slot, kb0 + j:kb0 + j + n, :].rearrange("p a b -> p (a b)")
                lo = alo[:, slot, kb0 + j:kb0 + j + n, :].rearrange("p a b -> p (a b)")
                war = [at_read[slot][kb0 + j + m] for m in range(n)]
                sc = 1.0 if scale is None else scale(j)
                t1 = act(lambda e, hi=hi, src=src, sc=sc: e.activation(hi, src, ACT.Copy, scale=sc), tok, t_cols, *war)
                ops.append((src, hi, lo, sc, [kb0 + j + m for m in range(n)]))
            for src, hi, lo, sc, kbs in ops:
                t2 = dve(lambda e, hi=hi, lo=lo, src=src, sc=sc: e.scalar_tensor_tensor(
                    out=lo, in0=src, scalar=sc, in1=hi.bitcast(F32), op0=ALU.mult, op1=ALU.subtract), t1, free=True)
                for kb in kbs:
                    at_tok[slot][kb] = t2
            release(b, t2)

        def rstd_of(dst, src, n, *waits):
            w = dst.shape[-1]
            t = pool(lambda e: e.tensor_scalar(dst, src, 1.0 / n, EPS, ALU.mult, ALU.add), *waits)
            return pool(lambda e: e.tensor_tensor(dst, dst, mhalf[:, 0:w], ALU.pow), t, t_mhalf)

        def square(o, tb, c, src, junk, *waits):
            N["sq", o, tb, c] = act(lambda e: e.activation(junk, src, ACT.Square, accum_out=stat[:, o + 4 * tb + c:o + 4 * tb + c + 1]), *waits)

        def mean_square(o):
            return dve(lambda e: e.tensor_reduce(stat[:, o + 8:o + 10], stat[:, o:o + 8].rearrange("p (t c) -> p t c", t=2), AX_X, ALU.add),
                       *[N["sq", o, tb, c] for tb in range(2) for c in range(4)])

        def diagonals(r, *waits):
            for tb in range(2):
                N["dg"] = dve(lambda e, tb=tb: e.tensor_scalar(dg[:, tb, :], ident[:, :], r[:, tb:tb + 1], None, ALU.mult), t_id, N.get("dgT"), *waits)

        def norm_diag(o):
            diagonals(stat[:, o + 10:o + 12], rstd_of(stat[:, o + 10:o + 12], stat[:, o + 8:o + 10], D, mean_square(o)))

        def norm_turn(k2):
            b, w = take()
            for j in range(2):
                for tb in range(2):
                    kb = 2 * k2 + j
                    tok = pe(lambda e, j=j, tb=tb, kb=kb: e.matmul(
                        ps[b][:, (2 * j + tb) * P:(2 * j + tb + 1) * P], x[:, tb, kb * P:(kb + 1) * P], dg[:, tb, :], start=True, stop=True),
                        w, N["dg"], inc=(j == 1 and tb == 1))
            N["dgT"] = tok
            return b, tok

        def norm_at(slot, k2, layer=None, scale=None, tmp=None, turned=None):
            b, tok = turned or norm_turn(k2)
            if layer is None:
                split_at(slot, 2 * k2, 2, b, tok, lambda j: scale[:, 2 * k2 + j:2 * k2 + j + 1])
                return
            tt = tmp[:, (k2 % 2) * 512:(k2 % 2) * 512 + 512]
            for j in range(2):
                kb = 2 * k2 + j
                o, src = tt[:, j * 256:j * 256 + 256], ps[b][:, j * 256:j * 256 + 256]
                a, s = mod[:, layer, 1, kb:kb + 1], mod[:, layer, 0, kb:kb + 1]
                waits = (tok, mod_tok[layer, kb // 4], N.get(("tmp", k2 % 2)))
                if k2 % 2:
                    t0 = act(lambda e, o=o, src=src, a=a, s=s: e.activation(o, src, ACT.Identity, scale=a, bias=s), *waits)
                else:
                    t0 = dve(lambda e, o=o, src=src, a=a, s=s: e.tensor_scalar(o, src, a, s, ALU.mult, ALU.add), *waits)
            release(b, t0)
            hi, lo = (a[:, slot, 2 * k2:2 * k2 + 2, :].rearrange("p a b -> p (a b)") for a in (ahi, alo))
            t1 = act(lambda e: e.activation(hi, tt, ACT.Copy), t0, at_read[slot][2 * k2], at_read[slot][2 * k2 + 1])
            t2 = dve(lambda e: e.tensor_tensor(lo, tt, hi.bitcast(F32), ALU.subtract), t1)
            N["tmp", k2 % 2] = at_tok[slot][2 * k2] = at_tok[slot][2 * k2 + 1] = t2

        def rope(dst, src, tok, heads, half, tabs, tb, scr, war=None):
            n = heads * half
            v = src[:, 0:2 * n].rearrange("p (h c d) -> p h c d", h=heads, c=2)
            d = dst.rearrange("p (h c d) -> p h c d", h=heads, c=2)
            s = [scr[:, i * 512:i * 512 + 2 * n].rearrange("p (h c d) -> p h c d", h=heads, c=2) for i in range(2)]
            for o, t in zip(s, tabs):
                f = t[:, tb, :].unsqueeze(1).unsqueeze(1).to_broadcast([P, heads, 2, half])
                t_s = dve(lambda e, o=o, f=f: e.tensor_tensor(o, v, f, ALU.mult), tok, N["rope"])
            dve(lambda e: e.tensor_tensor(d[:, :, 0, :], s[0][:, :, 0, :], s[1][:, :, 1, :], ALU.subtract), t_s, war)
            t = dve(lambda e: e.tensor_tensor(d[:, :, 1, :], s[0][:, :, 1, :], s[1][:, :, 0, :], ALU.add), t_s, war)
            return t_s, t

        def attend(heads, masks, scale, nm, dn, S, ET, st, scores, values):
            def stage1():
                for third in range(3):
                    b, w = take()
                    hs = heads if third == 0 else heads[2 * third - 2:2 * third]
                    nk = P if third == 0 else 256
                    qs = slice(0, P) if third == 0 else slice(P, 256)
                    for i, h in enumerate(hs):
                        ops = scores(h, qs, slice(0, nk))
                        for j, (l, r, rdy) in enumerate(ops):
                            tok = pe(lambda e, b=b, i=i, j=j, l=l, r=r, nk=nk, m=len(ops): e.matmul(
                                ps[b][:, i * nk:(i + 1) * nk], l, r, start=(j == 0), stop=(j == m - 1)),
                                w, *rdy, inc=(i == len(hs) - 1 and j == len(ops) - 1))
                    n = len(hs)
                    sv = S[:, third, :].rearrange("p (h k) -> p h k", h=n)
                    mk = masks[0 if third == 0 else 1].unsqueeze(1).to_broadcast([P, n, nk])
                    tb, o = (0, 0) if third == 0 else (1, 2 * third - 2)
                    nmx, den = nm[:, tb, o:o + n], dn[:, tb, o:o + n]
                    t0 = dve(lambda e, sv=sv, b=b, mk=mk, n=n: e.tensor_tensor(
                        sv, ps[b][:, :].rearrange("p (h k) -> p h k", h=n), mk, ALU.add), tok, t_mask[0], st.get(("S", third)))
                    release(b, t0)
                    t1 = dve(lambda e, sv=sv, nmx=nmx: e.tensor_reduce(nmx, sv, AX_X, ALU.max), t0)
                    t2 = dve(lambda e, nmx=nmx: e.tensor_scalar(nmx, nmx, -scale, None, ALU.mult), t1)
                    for i in range(n):
                        t3 = act(lambda e, sv=sv, i=i, nmx=nmx, den=den: e.activation(
                            sv[:, i, :], sv[:, i, :], ACT.Exp, bias=nmx[:, i:i + 1], scale=scale, accum_out=den[:, i:i + 1]), t2)
                    st["E", third] = t3
            def stage2():
                for third in range(3):
                    b, tok = xpose([S[:, third, i * P:(i + 1) * P] for i in range(4)], st["E", third])
                    st["S", third] = tok
                    t = act(lambda e, b=b, third=third: e.activation(ET[:, third, :], ps[b][:, :], ACT.Copy), tok, st.get(("ET", third)))
                    st["T", third] = t
                    release(b, t)
            def stage3():
                values(lambda tb, i: ([(ET[:, 0, i * P:(i + 1) * P], 0)] if tb == 0 else
                                      [(ET[:, 1 + i // 2, (i % 2) * 256 + m * P:(i % 2) * 256 + (m + 1) * P], m) for m in range(2)]),
                       [st["T", i] for i in range(3)])
            return [stage1, stage2, stage3]

        K = ins["consts"]
        t_cols = load(0, cols[:, :], ins["cols"])
        t_id = load(2, ident[:, :], K[:, K_ID:K_ID + P])
        R0 = Region()
        accs = [R0(1024), R0(1024)]
        gate = R0(D)
        cos128, sin128, cos32, sin32 = R0(2, P), R0(2, P), R0(2, 32), R0(2, 32)
        base = R0.off
        dtab = R0(8, 256)
        rp = R0(2, 2, 512)
        scr = R0(1024)
        qT, kT = R0(4, 256), R0(4, 256)
        v = R0(2, 1024)
        sg = R0(2, 1024)
        sT = R0(2, 384)
        yn = scr.rearrange("p (a b) -> p a b", a=2)
        bn = R0(2, 16)
        R0b = Region()
        R0b.off = base + 2048
        pos = R0b(2).bitcast(I32)
        posf = R0b(2)
        freq, ang, kk, rr, rc, mm_ = R0b(160), R0b(2, 160), R0b(2, 160), R0b(2, 160), R0b(2, 160), R0b(2, 160)
        t_pos = load(3, pos, ins["pos"])
        t_freq = load(4, freq, K[:, K_FREQ:K_FREQ + 160])
        t_ones = pool(lambda e: e.memset(ones[:, :], 1.0))
        t_mhalf = pool(lambda e: e.memset(mhalf[:, :], -0.5))
        mod_tok, gate_tok, N = {}, {}, {}
        t_cact = act(lambda e: e.activation(cact[:, :], col("c", 0, 16), ACT.Silu), t_cols)
        pump(0, 10)
        t_x = load(1, x[:, :, :], ins["x"].rearrange("o (t p) d -> p (o t) d", p=P))
        for tb in range(2):
            for c in range(4):
                junk = scr[:, (c % 2) * 512:(c % 2) * 512 + 512]
                square(0, tb, c, x[:, tb, c * 512:c * 512 + 512], junk, t_x, N.get(("junk", c % 2)))
                N["junk", c % 2] = N["sq", 0, tb, c]
        pump(0, 14)
        norm_diag(0)
        pump(0, 16)
        turned = [norm_turn(k2) for k2 in range(2)]
        drain()
        for k2 in range(2):
            norm_at(0, k2, layer=0, tmp=scr, turned=turned[k2])

        def at0(q):
            return [lambda k2=k2: norm_at(0, k2, layer=0, tmp=scr) for k2 in (2 * q, 2 * q + 1)]

        t_mask = [load(7, mmask[:, :], K[:, K_MLA:K_MLA + 256])]

        def angles():
            t = dve(lambda e: e.tensor_copy(posf, pos), t_pos)
            for tb in range(2):
                t1 = dve(lambda e, tb=tb: e.tensor_scalar(ang[:, tb, :], freq, posf[:, tb:tb + 1], None, ALU.mult), t, t_freq)
            t = dve(lambda e: e.tensor_scalar(kk, ang, 1.0 / (2.0 * PI), MAGIC, ALU.mult, ALU.add), t1)
            N["rope"] = dve(lambda e: e.tensor_scalar(kk, kk, MAGIC, None, ALU.subtract), t)

        def reduced():
            for i, cc in enumerate((C1, C2, C3)):
                src = ang if i == 0 else rr
                N["rope"] = dve(lambda e, cc=cc, src=src: e.scalar_tensor_tensor(out=rr, in0=kk, scalar=-cc, in1=src, op0=ALU.mult, op1=ALU.add), N["rope"])

        def tables():
            t = dve(lambda e: e.tensor_scalar(mm_, rr, PI / 2, -2.0 * PI, ALU.is_gt, ALU.mult), N["rope"])
            t = dve(lambda e: e.scalar_tensor_tensor(out=rc, in0=rr, scalar=PI / 2, in1=mm_, op0=ALU.add, op1=ALU.add), t)
            t = dve(lambda e: e.tensor_scalar(rc, rc, PI_IN, -PI_IN, ALU.min, ALU.max), t)
            t = dve(lambda e: e.tensor_scalar(rr, rr, PI_IN, -PI_IN, ALU.min, ALU.max), t)
            for o, s, a in ((cos128, rc, 0), (sin128, rr, 0), (cos32, rc, 128), (sin32, rr, 128)):
                w = o.shape[-1]
                N["rope"] = act(lambda e, o=o, s=s, a=a, w=w: e.activation(o, s[:, :, a:a + w], ACT.Sin), t)

        side += [angles, reduced, tables]

        L = {}

        def qk_evac(banks, toks):
            for n in range(2):
                for tb in range(2):
                    b = banks[n, tb]
                    t_b, L["rp", n] = rope(rp[:, n, tb, :], ps[b], toks[tb], 2, 128, (cos128, sin128), tb, scr, L.get(("rpT", n)))
                    release(b, t_b)

        def qk_turn(n, j):
            blocks = [rp[:, n, tb, (2 * j + i) * P:(2 * j + i + 1) * P] for i in range(2) for tb in range(2)]
            b, tok = xpose(blocks, L["rp", n])
            L["rpT", n] = tok
            dst = (qT, kT)[n][:, 2 * j:2 * j + 2, :].rearrange("p a b -> p (a b)")
            L["qkT", n, j] = act(lambda e: e.activation(dst, ps[b][:, :], ACT.Copy), tok, L.get("scores"))
            release(b, L["qkT", n, j])

        def v_evac(banks, toks):
            for tb in range(2):
                for n in range(2):
                    b = banks[n, tb]
                    L["v"] = act(lambda e, b=b, n=n, tb=tb: e.activation(v[:, tb, n * 512:n * 512 + 512], ps[b][:, :], ACT.Copy),
                                 toks[tb], L.get("pv"))
                    release(b, L["v"])

        def g_evac(banks, toks):
            for tb in range(2):
                for n in range(2):
                    b = banks[n, tb]
                    L["sg"] = act(lambda e, b=b, n=n, tb=tb: e.activation(sg[:, tb, n * 512:n * 512 + 512], ps[b][:, :], ACT.Silu),
                                  toks[tb], L.get("zT"))
                    release(b, L["sg"])

        def ret_scores(p, h):
            b, w = take()
            for lo_, n, q0 in ((0, 256, 0), (256, 128, 128)):
                for c in range(2):
                    tok = pe(lambda e, lo_=lo_, n=n, q0=q0, c=c: e.matmul(
                        ps[b][:, lo_:lo_ + n], kT[:, 2 * h + c, q0:q0 + P], qT[:, 2 * h + c, q0:q0 + n],
                        start=(c == 0), stop=(c == 1)), w, L["qkT", 0, h], L["qkT", 1, h], inc=(q0 == 128 and c == 1))
            L["scores"] = tok
            dt = dtab[:, 2 * p + h, :]
            t = dve(lambda e: e.tensor_tensor(sT[:, h, 0:256], ps[b][:, 0:256], dt, ALU.mult), tok, t_D, L.get(("sTr", h)))
            L["sT", h] = dve(lambda e: e.tensor_tensor(sT[:, h, 256:384], ps[b][:, 256:384], dt[:, 0:P], ALU.mult), tok)
            release(b, L["sT", h])

        def ret_values(p, h):
            hs = slice(h * 512, h * 512 + 512)
            for tb in range(2):
                b, w = take()
                if tb == 0:
                    tok = pe(lambda e, b=b: e.matmul(ps[b][:, :], sT[:, h, 0:P], v[:, 0, hs], start=True, stop=True), w, L["sT", h], L["v"])
                else:
                    pe(lambda e, b=b: e.matmul(ps[b][:, :], sT[:, h, P:256], v[:, 0, hs], start=True, stop=False), w, inc=False)
                    tok = pe(lambda e, b=b: e.matmul(ps[b][:, :], sT[:, h, 256:384], v[:, 1, hs], start=False, stop=True))
                L["pv"] = L["sTr", h] = tok
                bs = bn[:, tb, :]
                t = dve(lambda e, b=b, bs=bs: e.bn_stats(bs[:, 0:6], ps[b][:, :]), tok)
                t = dve(lambda e, bs=bs: e.bn_aggr(bs[:, 6:8], bs[:, 0:6]), t)
                r = rstd_of(bs[:, 8:9], bs[:, 7:8], 1, t)
                t = dve(lambda e, bs=bs: e.tensor_scalar(bs[:, 9:10], bs[:, 6:7], bs[:, 8:9], -1.0, ALU.mult, ALU.mult), r)
                t = act(lambda e, b=b, bs=bs, tb=tb: e.activation(yn[:, tb, :], ps[b][:, :], ACT.Identity, scale=bs[:, 8:9], bias=bs[:, 9:10]),
                        t, L.get(("z", tb)))
                release(b, t)
                L["z", tb] = dve(lambda e, tb=tb: e.tensor_tensor(sg[:, tb, hs], yn[:, tb, :], sg[:, tb, hs], ALU.mult), t, L["sg"])

        def ret_turn(p, j):
            blocks = [sg[:, tb, (2 * j + i) * P:(2 * j + i + 1) * P] for i in range(2) for tb in range(2)]
            b, tok = xpose(blocks, L["z", 0], L["z", 1])
            L["zT"] = tok
            split_at(1, (p % 2) * 8 + 2 * j, 2, b, tok, lambda i: col("gn_g", p * 8 + 2 * j + i))

        def parts(ph, buf, name, done):
            def evac(banks, toks):
                for tb in range(2):
                    for n in range(2):
                        b, o = banks[n, tb], buf(n, tb)
                        if ph == 0:
                            t = act(lambda e, b=b, o=o: e.activation(o, ps[b][:, :], ACT.Copy), toks[tb])
                        else:
                            t = dve(lambda e, b=b, o=o: e.tensor_tensor(o, ps[b][:, :], o, ALU.add), toks[tb], L["part", name, n, tb])
                        L["part", name, n, tb] = t
                        release(b, t)
                        if ph == 3:
                            done(n, tb, o, t)
            return evac

        def qk_done(n, tb, o, t):
            L["rp", n] = rope(rp[:, n, tb, :], o, t, 2, 128, (cos128, sin128), tb, scr)[1]

        def v_done(n, tb, o, t):
            L["v"] = t

        def g_done(n, tb, o, t):
            L["sg"] = act(lambda e: e.activation(o, o, ACT.Silu), t)

        def qk_part(n, tb):
            return (qT, kT)[n].rearrange("p a b -> p (a b)")[:, tb * 512:tb * 512 + 512]

        def cols_of(buf):
            return lambda n, tb: buf[:, tb, n * 512:n * 512 + 512]

        ytmp = scr
        Y = {"n": 0}

        def residual(layer, g, summed=None):
            def evac(banks, toks):
                for tb in range(2):
                    for n in range(2):
                        b = banks[n, tb]
                        cs = slice(g * 1024 + n * 512, g * 1024 + n * 512 + 512)
                        tmp = Y["tmp"][:, (Y["n"] % 2) * 512:(Y["n"] % 2) * 512 + 512]
                        Y["n"] += 1
                        t = dve(lambda e, b=b, cs=cs, tmp=tmp: e.tensor_tensor(tmp, ps[b][:, :], gate[:, cs], ALU.mult),
                                toks[tb], gate_tok[layer])
                        release(b, t)
                        L["x"] = dve(lambda e, cs=cs, tb=tb, tmp=tmp: e.tensor_tensor(x[:, tb, cs], x[:, tb, cs], tmp, ALU.add), t)
                        Y["g"] = t
                        if summed:
                            summed(tb, 2 * g + n, cs, L["x"])
            return evac

        def sums0(tb, c, cs, t):
            square(16, tb, c, x[:, tb, cs], qT.rearrange("p a b -> p (a b)")[:, 0:512], t, L["scores"], N.get("junk0"))
            N["junk0"] = N["sq", 16, tb, c]

        Y["tmp"] = ytmp
        for ph, kbs in enumerate(PHASES):
            for name, buf, done in (("qk", qk_part, qk_done), ("v", cols_of(v), v_done), ("g", cols_of(sg), g_done)):
                if ph < 3 and name == "g":
                    side += at0(ph + 1)
                gemm(0, kbs, 1024, parts(ph, buf, name, done))
                if ph == 3 and name == "qk":
                    side += [None] * 3 + [lambda n=n, j=j: qk_turn(n, j) for n, j in ((0, 0), (1, 0), (0, 1), (1, 1))]
            drain()
            if ph == 1:
                t_D = load(6, dtab, K[:, K_D:K_D + 2048].rearrange("p (a b) -> p a b", a=8))
        for p in range(4):
            if p:
                gemm(0, range(16), 1024, qk_evac)
                side += [None] * 3 + [lambda n=n, j=j: qk_turn(n, j) for n, j in ((0, 0), (1, 0), (0, 1), (1, 1))]
                gemm(0, range(16), 1024, v_evac)
                if p == 2:
                    side += [lambda j=j: gate_rows(0, j) for j in range(4)]
                gemm(0, range(16), 1024, g_evac)
            side += [lambda h=h, p=p: ret_scores(p, h) for h in range(2)]
            side += [None] + [lambda h=h, p=p: ret_values(p, h) for h in range(2)]
            if p == 2:
                for g in range(2):
                    gemm(1, range(16), 1024, residual(0, g))
                drain()
            side += [None] * 4 + [lambda j=j, p=p: ret_turn(p, j) for j in range(4)]
        for g in range(2):
            gemm(1, range(8), 1024, residual(0, g))
        drain()
        for g in range(2):
            gemm(1, range(8, 16), 1024, residual(0, g, sums0))
        drain()

        R1 = Region()
        R1.off = base
        sg1 = R1(2, 1024)
        rows = R1(2, 1024)
        qT1, kT1 = R1(8, 256), rows.rearrange("p a b -> p (a b)").rearrange("p (a b) -> p a b", a=8)
        v1 = R1(2, 1024)
        qr, qrT = R1(2, 512), R1(4, 256)
        kr = R1(2, P)
        ET = R1(3, 512)
        scr1 = ET.rearrange("p a b -> p (a b)")[:, 0:1024]
        R1a = Region()
        S, krE, krO = R1a(3, 512), R1a(256), R1a(256)
        nm1, dn1 = R1(2, 16), R1(2, 16)
        st1 = R1(8)
        htmp1 = S.rearrange("p a b -> p (a b)")[:, 0:1024]
        norm_diag(16)
        M = {}
        def c_evac(banks, toks):
            M["xn"] = t_xn = at_tok[1][15]
            pool(lambda e: e.memset(krE, 0.0), t_xn)
            M["kr0"] = pool(lambda e: e.memset(krO, 0.0), t_xn)
            for n in range(2):
                for tb in range(2):
                    b = banks[n, tb]
                    o = rows[:, tb, n * 512:n * 512 + 512]
                    i = n * 2 + tb
                    t = act(lambda e, b=b, o=o: e.activation(o, ps[b][:, :], ACT.Copy), toks[tb], t_xn)
                    t2 = act(lambda e, b=b, i=i: e.activation(S[:, 0, :], ps[b][:, :], ACT.Square, accum_out=st1[:, i:i + 1]), M.get("sq"))
                    M["sq"] = t2
                    release(b, t2)
            M["r"] = rstd_of(st1[:, 4:8], st1[:, 0:4], 512, M["sq"])

        def c_scale(n):
            for tb in range(2):
                o = rows[:, tb, n * 512:n * 512 + 512]
                i = n * 2 + tb
                M["rows", n, tb] = dve(lambda e, o=o, i=i: e.tensor_scalar(o, o, st1[:, 4 + i:5 + i], None, ALU.mult), M["r"])

        def c_turn(n, j):
            blocks = [rows[:, tb, n * 512 + (2 * j + i) * P:n * 512 + (2 * j + i + 1) * P] for i in range(2) for tb in range(2)]
            b, tok = xpose(blocks, M["rows", n, 0], M["rows", n, 1])
            M["rowsT"] = tok
            split_at(0, 4 * n + 2 * j, 2, b, tok, lambda i: col(("qn_g", "kvn_g")[n], 2 * j + i))

        def krope():
            b, w = take()
            _, q, t_hi, t_lo = next_block()
            for kb in range(16):
                for m, (xs, ws) in enumerate(((ahi, whi), (alo, whi), (ahi, wlo))):
                    tok = pe(lambda e, xs=xs, ws=ws, kb=kb, m=m: e.matmul(
                        ps[b][0:64, 0:256], ws[:, q, kb * 64:kb * 64 + 64], xs[:, 1, kb, :],
                        start=(kb == 0 and m == 0), stop=(kb == 15 and m == 2)), w, t_hi, t_lo, at_tok[1][kb],
                        inc=(kb == 15 and m == 2))
            ring_read[q] = tok
            M["krow"] = act(lambda e: e.activation(scr1[0:64, 0:256], ps[b][0:64, 0:256], ACT.Copy), tok, M["xn"])
            release(b, M["krow"])

        def krope_rows():
            b, w = take()
            for tb in range(2):
                tok = pe(lambda e, tb=tb: e.transpose(ps[b][:, tb * 64:tb * 64 + 64], scr1[0:64, tb * P:(tb + 1) * P], ident[0:64, 0:64]),
                         w, M["krow"], inc=(tb == 1))
            v4 = ps[b][:, 0:128].rearrange("p (t c d) -> p t c d", t=2, c=2)
            s = [scr1[:, 256 + i * 64:320 + i * 64].rearrange("p (t d) -> p t d", t=2) for i in range(4)]
            ts = []
            for o, a, f in ((s[0], v4[:, :, 0, :], cos32), (s[1], v4[:, :, 1, :], sin32), (s[2], v4[:, :, 1, :], cos32), (s[3], v4[:, :, 0, :], sin32)):
                ts.append(dve(lambda e, o=o, a=a, f=f: e.tensor_tensor(o, a, f, ALU.mult), tok, N["rope"]))
            release(b, ts[3])
            for o in (0, 64):
                dve(lambda e, o=o: e.tensor_tensor(kr[:, :, o:o + 32], s[0], s[1], ALU.subtract), ts[1])
                M["kr"] = dve(lambda e, o=o: e.tensor_tensor(kr[:, :, o + 32:o + 64], s[2], s[3], ALU.add), ts[3])

        def kr_turn():
            b, tok = xpose([kr[:, 0, :], kr[:, 1, :]], M["kr"])
            act(lambda e: e.activation(krE[0:64, :], ps[b][0:64, 0:256], ACT.Copy), tok, M["kr0"])
            M["krT"] = act(lambda e: e.activation(krO[64:128, :], ps[b][64:128, 0:256], ACT.Copy))
            release(b, M["krT"])

        def g1_evac(h):
            def evac(banks, toks):
                for tb in range(2):
                    for n in range(2):
                        b = banks[n, tb]
                        M["sg", h] = act(lambda e, b=b, n=n, tb=tb: e.activation(sg1[:, tb, n * 512:n * 512 + 512], ps[b][:, :], ACT.Silu), toks[tb], M.get("zT"))
                        release(b, M["sg", h])
            return evac

        def heads_evac(name, dst, last):
            def evac(banks, tok):
                for j, b in enumerate(banks):
                    o = dst[:, 2 * j:2 * j + 2, :].rearrange("p a b -> p (a b)")
                    if j % 2:
                        M[name, 1] = t = act(lambda e, b=b, o=o: e.activation(o, ps[b][:, :], ACT.Copy), tok, M.get(last), M["rowsT"])
                    else:
                        M[name, 0] = t = dve(lambda e, b=b, o=o: e.tensor_copy(o, ps[b][:, :]), tok, M.get(last), M["rowsT"])
                    release(b, t)
            return evac

        def qr_evac(banks, toks):
            for tb in range(2):
                b = banks[0, tb]
                t_b, M["qr"] = rope(qr[:, tb, :], ps[b], toks[tb], 8, 32, (cos32, sin32), tb, scr1, M.get("qrT_read"))
                release(b, t_b)

        def qr_turn(j):
            blocks = [qr[:, tb, (2 * j + i) * P:(2 * j + i + 1) * P] for i in range(2) for tb in range(2)]
            b, tok = xpose(blocks, M["qr"])
            M["qrT_read"] = tok
            M["qrT"] = act(lambda e: e.activation(qrT[:, 2 * j:2 * j + 2, :].rearrange("p a b -> p (a b)"), ps[b][:, :], ACT.Copy), tok, M.get("scores"))
            release(b, M["qrT"])

        def v1_evac(banks, toks):
            for tb in range(2):
                for n in range(2):
                    b = banks[n, tb]
                    M["v"] = act(lambda e, b=b, n=n, tb=tb: e.activation(v1[:, tb, n * 512:n * 512 + 512], ps[b][:, :], ACT.Copy),
                                 toks[tb], M.get("pv"))
                    release(b, M["v"])

        A = {}

        def mla_scores(h, qs, ks):
            rdy = (M["q", 0], M["q", 1], M["k", 0], M["k", 1], M["qrT"], M["krT"])
            return [(qT1[:, h, qs], kT1[:, h, ks], rdy),
                    (qrT[:, h // 2, qs], (krE, krO)[h % 2][:, ks], ())]

        def mla_values(half, quad):
            def values(parts, rdy):
                dn = dn1[:, :, quad * 4:quad * 4 + 4]
                t_r = dve(lambda e: e.reciprocal(dn, dn), *rdy)
                M["scores"] = A["S", 2]
                for tb in range(2):
                    b, w = take()
                    for i in range(4):
                        hh = quad * 4 + i
                        ops = parts(tb, i)
                        for j, (l, m) in enumerate(ops):
                            tok = pe(lambda e, b=b, i=i, hh=hh, l=l, m=m, j=j, k=len(ops): e.matmul(
                                ps[b][:, i * P:(i + 1) * P], l, v1[:, m, hh * P:(hh + 1) * P], start=(j == 0), stop=(j == k - 1)),
                                w, M["v"], *rdy, inc=(i == 3 and j == len(ops) - 1))
                    M["pv"] = tok
                    for third in range(3):
                        A["ET", third] = tok
                    for i in range(4):
                        hh = quad * 4 + i
                        z = sg1[:, tb, hh * P:(hh + 1) * P]
                        M["z"] = dve(lambda e, b=b, i=i, tb=tb, z=z, hh=hh: e.scalar_tensor_tensor(
                            out=z, in0=ps[b][:, i * P:(i + 1) * P], scalar=dn1[:, tb, hh:hh + 1], in1=z, op0=ALU.mult, op1=ALU.mult),
                            tok, t_r, M["sg", half])
                    release(b, M["z"])
            return values

        def z_turn(half, j):
            blocks = [sg1[:, tb, (2 * j + i) * P:(2 * j + i + 1) * P] for i in range(2) for tb in range(2)]
            b, tok = xpose(blocks, M["z"])
            M["zT"] = tok
            split_at(half, (8 if half == 0 else 0) + 2 * j, 2, b, tok)

        def mla_half(half):
            att = [attend(list(range(4 * quad, 4 * quad + 4)), (mmask[:, P:256], mmask[:, :]), 192.0 ** -0.5,
                          nm1[:, :, quad * 4:quad * 4 + 4], dn1[:, :, quad * 4:quad * 4 + 4], S, ET, A, mla_scores, mla_values(half, quad))
                   for quad in range(2)]
            turn = [lambda j=j: z_turn(half, j) for j in range(4)]
            return [att[0][0], None, att[0][1], None, att[0][2], att[1][0], turn[0], turn[1], att[1][1], None, att[1][2], None, None, turn[2], turn[3]]

        for k2 in range(2):
            norm_at(1, k2, layer=1, tmp=htmp1)
        side += [lambda k2=k2: norm_at(1, k2, layer=1, tmp=htmp1) for k2 in range(2, 8)]
        gemm(1, range(16), 1024, c_evac)
        side += [None, lambda: c_scale(0), lambda: c_scale(1), lambda: c_turn(0, 0), lambda: c_turn(0, 1), lambda: c_turn(1, 0), lambda: c_turn(1, 1)]
        krope()
        side += [krope_rows, None, kr_turn]
        side += [lambda j=j: gate_rows(1, j, Y["g"]) for j in range(4)]
        gemm(1, range(16), 1024, g1_evac(0))
        drain()
        for half in range(2):
            gemm_t(0, range(0, 4), heads_evac("q", qT1, "scores"))
            gemm(0, range(0, 4), 512, qr_evac)
            side += [None] * 3 + [lambda j=j: qr_turn(j) for j in range(2)]
            gemm_t(0, range(4, 8), heads_evac("k", kT1, "scores"))
            gemm(0, range(4, 8), 1024, v1_evac)
            drain()
            side += mla_half(half)
            if half == 0:
                gemm(1, range(16), 1024, g1_evac(1))
                drain()
        Y["tmp"] = qr.rearrange("p a b -> p (a b)")
        fg = qT1.rearrange("p a b -> p (a b)")
        xf = v1.rearrange("p a b -> p (a b)")

        def sums1(tb, c, cs, t):
            i = 2 * tb + c % 2
            o = xf[:, i * 512:i * 512 + 512]
            square(32, tb, c, x[:, tb, cs], S[:, 0, :], t, A["S", 2], N.get("junk1"))
            t = pool(lambda e: e.tensor_tensor(o, x[:, tb, cs], fg[:, cs], ALU.mult), t, t_fg, M["pv"], N.get(("xf", i)))
            square(48, tb, c, o, o, t)
            N["junk1"] = N["sq", 32, tb, c]
            N["xf", i] = N["sq", 48, tb, c]

        for half in range(2):
            for g in range(2):
                gemm(half, range(8, 16) if half == 0 else range(0, 8), 1024, residual(1, g, sums1 if half else None))
            drain()
            if half == 0:
                t_fg = load(9, fg, ins["final_norm_g"].unsqueeze(0).to_broadcast([P, D]), M["scores"], M["pv"])

        r1, r2 = stat[:, 42:44], stat[:, 58:60]
        t1 = mean_square(32)
        t2 = mean_square(48)
        t = t_r1 = rstd_of(r1, stat[:, 40:42], D, t1)
        t = pool(lambda e: e.tensor_tensor(r2, r1, r1, ALU.mult), t)
        t = pool(lambda e: e.tensor_tensor(r2, r2, stat[:, 56:58], ALU.mult), t, t2)
        t = rstd_of(r2, r2, D, t)
        t = pool(lambda e: e.tensor_tensor(r2, r2, r1, ALU.mult), t)
        gg = stat[:, 0:16]
        t_gg = dve(lambda e: e.tensor_tensor(gg, col("final_g", 0, 16), col("attn_g", 0, 16), ALU.mult), t_cols, N["dgT"])
        diagonals(r2, t)

        def final_x(tb, c):
            cs = slice(c * 1024, c * 1024 + 1024)
            L["x"] = dve(lambda e: e.scalar_tensor_tensor(out=x[:, tb, cs], in0=x[:, tb, cs], scalar=r1[:, tb:tb + 1], in1=fg[:, cs],
                                                          op0=ALU.mult, op1=ALU.mult), N["dgT"], t_r1, t_fg)

        R2 = Region()
        qk = R2(2, 1536)
        qT2 = R2(6, 256)
        kE, kO = R2(6, 256), R2(6, 256)
        v2 = R2(2, 768)
        S2, ET2 = R2(3, 512), R2(3, 512)
        bmask = R2(3, 384)
        yc = R2(2, 768)
        nm2, dn2 = R2(2, 3, 4), R2(2, 3, 4)
        lse, cf, mx, t4 = R2(2, 3, 4), R2(2, 3, 4), R2(2, 4), R2(2, 4)
        hs_, hr = R2(2, 24), R2(2, 24)
        av = ET2.rearrange("p a b -> p (a b)")[:, 0:1024].rearrange("p (a b) -> p a b", a=2)
        au = R2(2, 512)
        wsT = yc.rearrange("p a b -> p (a b)")[:, 0:1024].rearrange("p (a b) -> p a b", a=8)
        sq = S2.rearrange("p a b -> p (a b)")
        Rc = Region()
        Rc.off = 3072 + 1536 + 3072 + 1536 + 1536
        bt, yb, zp = Rc(256), Rc(256), Rc(2, 258)
        qk_flat = qk.rearrange("p a b -> p (a b)")
        zz = qk_flat[:, 0:1536].rearrange("p (a b) -> p a b", a=2)
        bb = qk_flat[:, 1536:3072].rearrange("p (a b) -> p a b", a=2)
        B = {}
        for k2 in range(2):
            norm_at(0, k2, scale=gg)
        side += [lambda k2=k2: norm_at(0, k2, scale=gg) for k2 in range(2, 8)]
        side += [lambda tb=tb, c=c: final_x(tb, c) for tb in range(2) for c in range(2)]

        def small_loads():
            t_ws = load(10, wsT, ins["sgu_wT"], L["x"])
            B["bm"] = t_mask[0] = load(11, bmask, K[:, K_B2:K_B2 + 3 * 384].rearrange("p (a b) -> p a b", a=3), L["x"])
            B["ws"] = pool(lambda e: e.affine_select(out=wsT, in_=wsT, compare_op=ALU.is_ge, fill=0.0, base=0,
                                                     pattern=[[0, 8], [1, P]], channel_multiplier=-1), t_ws)
            pool(lambda e: e.memset(kE, 0.0), at_tok[0][15])
            B["kz"] = pool(lambda e: e.memset(kO, 0.0), at_tok[0][15])

        side.append(small_loads)
        def copies(*moves):
            def evac(banks, toks):
                for tb in range(2):
                    for n in range(2):
                        if (n, tb) not in banks:
                            continue
                        b = banks[n, tb]
                        for mn, cs, dst, name, war in moves:
                            if mn == n:
                                B[name] = t = act(lambda e, b=b, cs=cs, d=dst(tb): e.activation(d, ps[b][:, cs], ACT.Copy),
                                                  toks[tb], L["x"], B.get(war))
                        release(b, t)
            return evac

        full = slice(0, 512)

        def head_norm(tb):
            t = dve(lambda e: e.tensor_tensor(sq, qk[:, tb, :], qk[:, tb, :], ALU.mult), B["qk0"], B["qk1"], B["qk2"], B.get("hn"))
            t = dve(lambda e: e.tensor_reduce(hs_[:, tb, :], sq.rearrange("p (h d) -> p h d", h=24), AX_X, ALU.add), t)
            B["hn"] = t
            B["hr", tb] = rstd_of(hr[:, tb, :], hs_[:, tb, :], 64, t)

        def head_scale(tb):
            q3 = qk[:, tb, :].rearrange("p (h d) -> p h d", h=24)
            B["qkn", tb] = dve(lambda e: e.tensor_tensor(q3, q3, hr[:, tb, :].unsqueeze(2).to_broadcast([P, 24, 64]), ALU.mult), B["hr", tb])

        def qk2_turn(j):
            blocks = [qk[:, tb, (2 * j + i) * P:(2 * j + i + 1) * P] for i in range(2) for tb in range(2)]
            b, tok = xpose(blocks, B["qkn", 0], B["qkn", 1])
            B["qkT"] = tok
            if j < 3:
                B["qT"] = t = act(lambda e: e.activation(qT2[:, 2 * j:2 * j + 2, :].rearrange("p a b -> p (a b)"), ps[b][:, :], ACT.Copy,
                                                         scale=col("q_g")), tok)
            else:
                for half, dst in ((slice(0, 64), kE), (slice(64, 128), kO)):
                    B["kT"] = t = act(lambda e, half=half, dst=dst: e.activation(
                        dst[half, 2 * j - 6:2 * j - 4, :].rearrange("p a b -> p (a b)"), ps[b][half, :], ACT.Copy,
                        scale=cols[half, COLS["k_g"][0]:COLS["k_g"][1]]), tok, B["kz"])
            release(b, t)

        def c_scores(h, qs, ks):
            return [(qT2[:, h // 2, qs], (kE, kO)[h % 2][:, h // 2, ks], (B["qT"], B["kT"]))]

        A2 = {}

        def c_values(g):
            def values(parts, rdy):
                b, w = take()
                for tb in range(2):
                    for i in range(4):
                        h = 4 * g + i
                        ops = parts(tb, i)
                        for j, (l, m) in enumerate(ops):
                            tok = pe(lambda e, tb=tb, i=i, l=l, m=m, j=j, k=len(ops), h=h: e.matmul(
                                ps[b][:, tb * 256 + i * 64:tb * 256 + (i + 1) * 64], l, v2[:, m, h * 64:(h + 1) * 64],
                                start=(j == 0), stop=(j == k - 1)), w, B["v0"], B["v1"], *rdy, inc=(tb == 1 and i == 3 and j == 1))
                for third in range(3):
                    A2["ET", third] = tok
                B["yc"] = act(lambda e: e.activation(yc[:, :, g * 256:(g + 1) * 256], ps[b][:, :].rearrange("p (t c) -> p t c", t=2), ACT.Copy), tok)
                release(b, B["yc"])
            return values

        def mixture():
            t = act(lambda e: e.activation(lse, dn2, ACT.Ln), B["yc"])
            t = dve(lambda e: e.tensor_tensor(lse, lse, nm2, ALU.subtract), t)
            t = dve(lambda e: e.tensor_tensor(mx, lse[:, :, 0, :], lse[:, :, 1, :], ALU.max), t)
            t = dve(lambda e: e.tensor_tensor(mx, mx, lse[:, :, 2, :], ALU.max), t)
            for g in range(3):
                t1 = dve(lambda e, g=g: e.tensor_tensor(cf[:, :, g, :], lse[:, :, g, :], mx, ALU.subtract), t)
            t = act(lambda e: e.activation(cf, cf, ACT.Exp), t1)
            t = dve(lambda e: e.tensor_tensor(t4, cf[:, :, 0, :], cf[:, :, 1, :], ALU.add), t)
            t = dve(lambda e: e.tensor_tensor(t4, t4, cf[:, :, 2, :], ALU.add), t)
            for g in range(3):
                t1 = dve(lambda e, g=g: e.tensor_tensor(lse[:, :, g, :], dn2[:, :, g, :], t4, ALU.mult), t)
            t = dve(lambda e: e.reciprocal(lse, lse), t1)
            t = dve(lambda e: e.tensor_tensor(cf, cf, lse, ALU.mult), t)
            for tb in range(2):
                y3 = yc[:, tb, :].rearrange("p (h d) -> p h d", h=12)
                c3 = cf[:, tb, :, :].rearrange("p g i -> p (g i)").unsqueeze(2).to_broadcast([P, 12, 64])
                B["ycn", tb] = dve(lambda e, y3=y3, c3=c3: e.tensor_tensor(y3, y3, c3, ALU.mult), t)

        def yc_turn(j):
            blocks = [yc[:, tb, (2 * j + i) * P:(2 * j + i + 1) * P] for i in range(2) for tb in range(2)]
            b, tok = xpose(blocks, B["ycn", 0], B["ycn", 1])
            split_at(1, 10 + 2 * j, 2, b, tok)

        def gating(tb):
            b, w = take()
            for h in range(8):
                tok = pe(lambda e, h=h: e.matmul(ps[b][:, h * 64:(h + 1) * 64], wsT[:, h, :], av[:, tb, h * 64:(h + 1) * 64], start=True, stop=True),
                         w, B["ws"], B["av"], inc=(h == 7))
            a3 = av[:, tb, :].rearrange("p (h d) -> p h d", h=8)
            b3 = col("sgu_b", 0, 8).unsqueeze(2).to_broadcast([P, 8, 64])
            t = dve(lambda e: e.tensor_tensor(a3, ps[b][:, :].rearrange("p (h d) -> p h d", h=8), b3, ALU.add), tok, t_cols)
            release(b, t)
            B["ya", tb] = dve(lambda e: e.tensor_tensor(au[:, tb, :], au[:, tb, :], av[:, tb, :], ALU.mult), t, B["au"])

        def ya_turn(j):
            blocks = [au[:, tb, (2 * j + i) * P:(2 * j + i + 1) * P] for i in range(2) for tb in range(2)]
            b, tok = xpose(blocks, B["ya", 0], B["ya", 1])
            B["yaT"] = tok
            split_at(1, 2 * j, 2, b, tok)

        def cx_evac(n_c, c_cols, n_x, x_cols, dst_cols, other=None):
            def evac(banks, toks):
                for tb in range(2):
                    bc, bx = banks[n_c, tb], banks[n_x, tb]
                    z = zz[:, tb, dst_cols]
                    t = act(lambda e, bc=bc, z=z: e.activation(z, ps[bc][:, c_cols], ACT.Copy), toks[tb], B["qkT"])
                    t = dve(lambda e, bx=bx, z=z: e.tensor_tensor(z, z, ps[bx][:, x_cols], ALU.mult), t)
                    B["z", tb] = t
                    release(bx, t)
                    if n_c != n_x:
                        release(bc, t)
                    if other is not None:
                        bo = banks[1, tb]
                        B["b0"] = act(lambda e, bo=bo, tb=tb: e.activation(bb[:, tb, 0:512], ps[bo][:, :], ACT.Copy), toks[tb])
                        release(bo, B["b0"])
            return evac

        def conv_turn(f):
            blocks = [a[:, tb, f * P:(f + 1) * P] for a in (zz, bb) for tb in range(2)]
            b, tok = xpose(blocks, B["z", 0], B["z", 1], B["b0"], B["b1"])
            zq = zp[:, f % 2, :]
            t = act(lambda e: e.activation(zq[:, 2:258], ps[b][:, 0:256], ACT.Copy), tok, B["zp0"], B.get(("zp", f % 2)))
            t = dve(lambda e: e.tensor_scalar(bt, zq[:, 0:256], col("conv", 3 * f), None, ALU.mult), t)
            t = dve(lambda e: e.scalar_tensor_tensor(out=bt, in0=zq[:, 1:257], scalar=col("conv", 3 * f + 1), in1=bt, op0=ALU.mult, op1=ALU.add), t)
            t = dve(lambda e: e.scalar_tensor_tensor(out=bt, in0=zq[:, 2:258], scalar=col("conv", 3 * f + 2), in1=bt, op0=ALU.mult, op1=ALU.add), t)
            B["zp", f % 2] = t
            t = dve(lambda e: e.tensor_tensor(yb, bt, ps[b][:, 256:512], ALU.mult), t, B.get("yb"))
            release(b, t)
            hi, lo = ahi[:, 1, 4 + f, :], alo[:, 1, 4 + f, :]
            t1 = act(lambda e: e.activation(hi, yb, ACT.Copy), t, at_read[1][4 + f])
            at_tok[1][4 + f] = B["yb"] = dve(lambda e: e.tensor_tensor(lo, yb, hi.bitcast(F32), ALU.subtract), t1)

        gemm(0, range(16), 1024, copies((0, full, lambda tb: qk[:, tb, 0:512], "qk0", None), (1, full, lambda tb: qk[:, tb, 512:1024], "qk1", None)))
        gemm(0, range(16), 1024, copies((0, full, lambda tb: qk[:, tb, 1024:1536], "qk2", None), (1, full, lambda tb: v2[:, tb, 0:512], "v0", None)))
        side += [lambda: head_norm(0), lambda: head_norm(1), lambda: head_scale(0), lambda: head_scale(1), None, None, None]
        side += [lambda j=j: qk2_turn(j) for j in range(6)]
        gemm(0, range(16), 1024, copies((0, full, lambda tb: av[:, tb, :], "av", None), (1, full, lambda tb: au[:, tb, :], "au", None)))
        side += [None, lambda: gating(0), lambda: gating(1), None, None, lambda: ya_turn(0), lambda: ya_turn(1)]
        gemm(0, range(16), 512, copies((0, slice(0, 256), lambda tb: bb[:, tb, 512:768], "b1", "qkT"),
                                       (0, slice(256, 512), lambda tb: v2[:, tb, 512:768], "v1", None)))
        drain()
        for third in range(3):
            A2["ET", third] = B["yaT"]
        B["yc"] = B["yaT"]
        for g in range(3):
            a, b, c = attend(list(range(4 * g, 4 * g + 4)), (bmask[:, g, 0:P], bmask[:, g, P:384]), 0.125,
                             nm2[:, :, g, :], dn2[:, :, g, :], S2, ET2, A2, c_scores, c_values(g))
            side += [a, None, b, None, c, None]
        side += [mixture, None, None, None] + [lambda j=j: yc_turn(j) for j in range(3)]
        gemm(0, range(16), 1024, cx_evac(0, full, 1, full, slice(0, 512)))
        gemm(0, range(16), 1024, cx_evac(0, slice(0, 256), 0, slice(256, 512), slice(512, 768), other=True))
        drain()
        B["zp0"] = pool(lambda e: e.memset(zp, 0.0), A2["ET", 2])
        side += [None] + [lambda f=f: conv_turn(f) for f in range(6)]

        def add_x(g, final=False, summed=None):
            def evac(banks, toks):
                for tb in range(2):
                    for n in range(2):
                        b = banks[n, tb]
                        cs = slice(g * 1024 + n * 512, g * 1024 + n * 512 + 512)
                        L["x"] = dve(lambda e, b=b, cs=cs, tb=tb: e.tensor_tensor(x[:, tb, cs], ps[b][:, :], x[:, tb, cs], ALU.add), toks[tb], L["x"])
                        release(b, L["x"])
                        if summed:
                            summed(tb, 2 * g + n, cs, L["x"])
                        if final:
                            L["out"] = sp(lambda e, cs=cs, tb=tb: e.dma_start(out[0, tb * P:(tb + 1) * P, cs], x[:, tb, cs]), L["x"], count=s_out)
            return evac

        def sums2(tb, c, cs, t):
            square(16, tb, c, x[:, tb, cs], S2[:, 0, :], t, A2["ET", 2], N.get("junk2"))
            N["junk2"] = N["sq", 16, tb, c]

        order = list(range(0, 4)) + list(range(10, 16)) + list(range(4, 10))
        for g in range(2):
            gemm(1, order, 1024, add_x(g, summed=sums2))
        drain()

        norm_diag(16)
        for k2 in range(2):
            norm_at(0, k2, scale=col("mlp_g", 0, 16))
        side += [lambda k2=k2: norm_at(0, k2, scale=col("mlp_g", 0, 16)) for k2 in range(2, 8)]
        R3 = Region()
        u = R3(2, 2, 1024)
        U = {}

        def u_evac(g):
            def evac(banks, toks):
                for tb in range(2):
                    for n in range(2):
                        b = banks[n, tb]
                        o = u[:, g % 2, tb, n * 512:n * 512 + 512]
                        t = act(lambda e, b=b, o=o: e.activation(o, ps[b][:, :], ACT.Relu), toks[tb], U.get(("uT", g % 2)))
                        release(b, t)
                        U["u", g] = pool(lambda e, o=o: e.tensor_tensor(o, o, o, ALU.mult), t)
            return evac

        def u_turn(g, j):
            blocks = [u[:, g % 2, tb, (2 * j + i) * P:(2 * j + i + 1) * P] for i in range(2) for tb in range(2)]
            b, tok = xpose(blocks, U["u", g])
            U["uT", g % 2] = tok
            split_at(1, (g % 2) * 8 + 2 * j, 2, b, tok)

        for g in range(8):
            gemm(0, range(16), 1024, u_evac(g))
            side += [None] * 2 + [lambda g=g, j=j: u_turn(g, j) for j in range(4)]
            if g == 0:
                continue
            for n in range(2):
                gemm(1, range(((g - 1) % 2) * 8, ((g - 1) % 2) * 8 + 8), 1024, add_x(n))
        drain()
        for n in range(2):
            gemm(1, range(8, 16), 1024, add_x(n, final=True))
        assert not side and not urgent and state["used"] == state["w"] and state["next"] == len(plan)
        t_out = L["out"]

        block = ctx.enter_context(nc.Block())

        @block.sync
        def _(eng):
            sp.play(eng)
            eng.wait_ge(t_out[0].handle, t_out[1])

        @block.scalar
        def _(eng):
            act.play(eng)

        @block.vector
        def _(eng):
            dve.play(eng)

        @block.gpsimd
        def _(eng):
            pool.play(eng)

        @block.tensor
        def _(eng):
            pe.play(eng)


def constants():
    k = np.zeros((P, NCONST), np.float32)
    k[:, K_ID:K_ID + P] = np.eye(P, dtype=np.float32)
    i = np.arange(P)
    t = np.arange(256)
    k[:, K_MLA + P:K_MLA + 256] = np.where(i[None, :] <= i[:, None], 0.0, NEG)
    for d, a in ((256, 0), (64, 128)):
        f = 10000.0 ** (-np.arange(0, d, 2, dtype=np.float64) / d)
        k[:, K_FREQ + a:K_FREQ + a + d // 2] = f.astype(np.float32)[None, :]
    for h in range(8):
        lg = np.log1p(-np.exp2(-5.0 - h))
        diff = t[None, :] - i[:, None]
        k[:, K_D + h * 256:K_D + (h + 1) * 256] = np.where(diff >= 0, np.exp(lg * np.maximum(diff, 0)), 0.0) / 16.0
    for g, (w, d) in enumerate(((128, 1), (512, 4), (2048, 16))):
        def mask(q, s):
            gap = q[:, None] - s[None, :]
            return np.where((gap >= 0) & (gap <= w) & (gap % d == 0), 0.0, NEG)
        o = K_B2 + g * 384
        k[:, o:o + P] = mask(i, i)
        k[:, o + P:o + 384] = mask(i + P, t)
    return k


def tiles(w, groups, kbs=None):
    kb = w.shape[0] // P
    w3 = w.reshape(kb, P, w.shape[1])
    parts = []
    for cols in groups:
        a = np.concatenate([w3[:, :, s] for s in cols], axis=2) if len(cols) > 1 else w3[:, :, cols[0]]
        parts.append(a[list(kbs)] if kbs is not None else a)
    return np.ascontiguousarray(np.concatenate(parts, axis=0))


def layout(inp):
    a = {k: np.asarray(v) for k, v in inp.items()}
    sl = slice
    g = {}
    w = a["ret_w_in"][0]
    grp = []
    for p in range(4):
        grp += [[sl(p * 512, p * 512 + 512), sl(2048 + p * 512, 2048 + p * 512 + 512)],
                [sl(4096 + p * 1024, 4096 + (p + 1) * 1024)], [sl(8192 + p * 1024, 8192 + (p + 1) * 1024)]]
    g["ret_in"] = tiles(w, grp)
    two = [[sl(0, 1024)], [sl(1024, 2048)]]
    wo = a["ret_w_out"][0]
    g["ret_out"] = np.concatenate([tiles(wo[0:2048], two), tiles(wo[2048:3072], two), tiles(wo[3072:4096], two)])
    w = a["mla_w_in"][0]
    g["mla_in"] = tiles(w, [[sl(0, 1024)], [sl(1088, 2112)], [sl(2112, 3136)]])
    g["mla_kr"] = np.ascontiguousarray(w[:, 1024:1088].reshape(16, P, 64).transpose(1, 0, 2).reshape(1, P, 1024))
    w = a["mla_w_uq"][0].reshape(512, 16, 192)
    g["uq_n"] = tiles(np.ascontiguousarray(w[:, :, 0:128]).reshape(512, 2048), two)
    g["uq_r"] = tiles(np.ascontiguousarray(w[:, :, 128:192]).reshape(512, 1024), [[sl(0, 512)], [sl(512, 1024)]])
    w = a["mla_w_ukv"][0].reshape(512, 16, 256)
    g["ukv_k"] = tiles(np.ascontiguousarray(w[:, :, 0:128]).reshape(512, 2048), two)
    g["ukv_v"] = tiles(np.ascontiguousarray(w[:, :, 128:256]).reshape(512, 2048), two)
    w = a["mla_w_out"][0]
    g["mla_out"] = np.concatenate([tiles(w[0:1024], two), tiles(w[1024:2048], two)])
    w = a["w_in_2"][0]
    au, av, bb, bc, bx, q, k, v = 0, 512, 1024, 1792, 2560, 3328, 4096, 4864
    g["in2"] = tiles(w, [
        [sl(q, q + 768), sl(k, k + 256)], [sl(k + 256, k + 768), sl(v, v + 512)],
        [sl(av, av + 512), sl(au, au + 512)], [sl(bc, bc + 512), sl(bx, bx + 512)],
        [sl(bc + 512, bc + 768), sl(bx + 512, bx + 768), sl(bb, bb + 512)]])
    g["in2h"] = tiles(w, [[sl(bb + 512, bb + 768), sl(v + 512, v + 768)]])
    g["out2"] = tiles(a["w_out_2"][0], two, list(range(0, 4)) + list(range(10, 16)) + list(range(4, 10)))
    g["mlp1"] = tiles(a["w_mlp_in_2"][0], [[sl(i * 1024, (i + 1) * 1024)] for i in range(8)])
    w = a["w_mlp_out_2"][0]
    g["mlp2"] = np.concatenate([tiles(w[i * 1024:(i + 1) * 1024], two) for i in range(8)])
    w = a["ada_w"].reshape(2, 16, P, 3 * D)
    grp = [[sl(q * 512, q * 512 + 512), sl(D + q * 512, D + q * 512 + 512)] for q in range(4)]
    grp += [[sl(2 * D + i * 1024, 2 * D + (i + 1) * 1024)] for i in range(2)]
    g["ada"] = np.ascontiguousarray(np.stack([np.concatenate([w[..., c] for c in cs], axis=-1) for cs in grp], axis=1))
    def colm(v):
        return v.reshape(-1, P).T
    ab = a["ada_b"]
    parts = [colm(a["c"][0]), colm(ab[0]), colm(ab[1]), colm(a["norm_g"].reshape(-1)), colm(a["ret_gn_g"][0]),
             colm(a["mla_q_norm_g"][0]), colm(a["mla_kv_norm_g"][0]), colm(a["attn_norm_2"][0]), colm(a["mlp_norm_2"][0]), colm(a["final_norm_g"]),
             a["conv_w_2"][0].reshape(3, 6, P).transpose(2, 1, 0).reshape(P, 18), a["sgu_b_2"][0].T,
             np.concatenate([a["q_norm_2"][0]] * 2)[:, None], np.concatenate([a["k_norm_2"][0]] * 2)[:, None]]
    g["cols"] = np.ascontiguousarray(np.concatenate(parts, axis=1))
    g["pos"] = np.ascontiguousarray(a["positions"].reshape(2, P).T)
    g["x"] = a["x"]
    g["final_norm_g"] = a["final_norm_g"]
    g["sgu_wT"] = np.ascontiguousarray(a["sgu_w_2"][0].transpose(2, 0, 1))
    g["consts"] = constants()
    return g


def kernel(**inputs):
    from concourse import bacc, mybir as mb
    from concourse.bass_utils import run_bass_kernel_spmd

    nc = bacc.Bacc("TRN2", target_bir_lowering=False, num_devices=1)
    arrays, ins = {}, {}
    for name, a in layout(inputs).items():
        arrays[f"in_{name}"] = a
        ins[name] = nc.dram_tensor(f"in_{name}", a.shape, mb.dt.from_np(a.dtype), kind="ExternalInput").ap()
    out = nc.dram_tensor("out_0", (1, 256, D), mb.dt.float32, kind="ExternalOutput").ap()
    fused_blocks(nc, ins, out)
    r = run_bass_kernel_spmd(nc, [arrays], core_ids=[0])
    return r.results[0]["out_0"]
```

```python
from collections import deque
from contextlib import ExitStack

import numpy as np
import concourse.bass as bass
from concourse import mybir

F32 = mybir.dt.float32
F32R = mybir.dt.float32r
I32 = mybir.dt.int32
ALU = mybir.AluOpType
ACT = mybir.ActivationFunctionType
AX_X = mybir.AxisListType.X

P = 128
D = 2048
EPS = 1e-6
RAW = 6
RING = 4
POOLED = 256
TAIL = 1
AHEAD = 20
PHASES = [range(4 * i, 4 * i + 4) for i in range(4)]
NEG = -1e30
PI = float(np.pi)
PI_IN = 3.1415925
MAGIC = 12582912.0
C1 = 6.28125
C2 = float(np.float32(2.0 * np.pi - C1))
C2 = float((np.array([C2], np.float32).view(np.uint32) & np.uint32(0xFFFFF000)).view(np.float32)[0])
C3 = float(np.float32(2.0 * np.pi - C1 - C2))

COLS = {}
_at = 0
for _name, _n in (("c", 16), ("ada_b", 64), ("norm_g", 32), ("gn_g", 32), ("qn_g", 4), ("kvn_g", 4),
                  ("attn_g", 16), ("mlp_g", 16), ("final_g", 16), ("conv", 18), ("sgu_b", 8), ("q_g", 1), ("k_g", 1)):
    COLS[_name] = (_at, _at + _n)
    _at += _n
NCOL = _at
K_ID, K_MLA, K_FREQ, K_D, K_B2 = 0, 128, 384, 544, 544 + 2048
NCONST = K_B2 + 3 * 384


class Count:

    def __init__(self, handle, step=1):
        self.handle, self.step, self.n = handle, step, 0


class Line:

    def __init__(self, count, steps=False):
        self.count, self.items, self.steps = count, [], steps

    def __call__(self, fn, *waits, inc=True, count=None, free=False):
        tok = None
        if self.steps and not free and self.count.n:
            waits += ((self.count, self.count.n),)
        c = (count or self.count) if inc else None
        if c is not None:
            c.n += c.step
            tok = (c, c.n)
        self.items.append((fn, [w for w in waits if w is not None], c))
        return tok

    def play(self, eng):
        seen = {}
        for fn, waits, c in self.items:
            for s, v in waits:
                if seen.get(s, 0) < v:
                    eng.wait_ge(s.handle, v)
                    seen[s] = v
            ins = fn(eng)
            if c is not None:
                ins.then_inc(c.handle, c.step)


def stream_plan():
    w = [("w", "ret_in", g * 16 + kb, 1024) for kbs in PHASES for g in range(5) for kb in kbs]
    first = len(w)
    for p in range(1, 4):
        w += [("w", "ret_in", p * 48 + i, 1024) for i in range(32 if p == 1 else 0, 48)]
        if p >= 2:
            w += [("w", "ret_out", (p - 2) * 32 + i, 1024) for i in range(32)]
    n0 = len(w)
    w += [("w", "mla_in", i, 1024) for i in range(16)]
    w += [("w", "mla_kr", 0, 1024)]
    w += [("w", "mla_in", 16 + i, 1024) for i in range(16)]

    def half(h):
        return ([("w", "uq_n", h * 4 + i, 1024) for i in range(4)] + [("w", "uq_r", h * 4 + i, 512) for i in range(4)]
                + [("w", "ukv_k", h * 4 + i, 1024) for i in range(4)] + [("w", "ukv_v", h * 4 + i, 1024) for i in range(4)])
    w += half(0)
    w += [("w", "mla_in", 32 + i, 1024) for i in range(16)]
    w += half(1)
    w += [("w", "mla_out", i, 1024) for i in range(32)]
    w += [("w", "in2", i, 1024) for i in range(48)]
    w += [("w", "in2h", i, 512) for i in range(16)]
    w += [("w", "in2", 48 + i, 1024) for i in range(32)]
    w += [("w", "out2", i, 1024) for i in range(32)]
    one = [("w", "mlp1", i, 1024) for i in range(128)]
    two = [("w", "mlp2", i, 1024) for i in range(128)]
    w += one[0:16]
    for g in range(1, 8):
        w += one[g * 16:g * 16 + 16] + two[(g - 1) * 16:g * 16]
    w += two[112:128]
    ada = [("ada", 0, g, k) for g in range(4) for k in range(16)]
    plan, ada = ada[:AHEAD], ada[AHEAD:]
    for i in range(first):
        plan.append(w[i])
        while ada and 64 - len(ada) < AHEAD + (i + 1) * 4 / 5:
            plan.append(ada.pop(0))
    ada = [("ada", 0, g, k) for g in (4, 5) for k in range(16)]
    ada += [("ada", 1, g, k) for g in range(4) for k in range(16)]
    gate = [("ada", 1, g, k) for g in (4, 5) for k in range(16)]
    total = len(ada)
    for i, item in enumerate(w[first:]):
        plan.append(item)
        while ada and total - len(ada) < (i + 1) * total // (n0 - first - 8):
            plan.append(ada.pop(0))
        if n0 - first + 3 < i and gate:
            plan.append(gate.pop(0))
    assert not ada
    return plan


def fused_blocks(nc, ins, out):
    with ExitStack() as ctx:
        def sb(name, shape, dt=F32):
            return ctx.enter_context(nc.sbuf_tensor(name, shape, dt))

        def sem(name, step=1):
            return Count(ctx.enter_context(nc.semaphore(name)), step)

        raw = sb("raw", [P, RAW, 1024])
        whi = sb("whi", [P, RING, 1024], F32R)
        wlo = sb("wlo", [P, RING, 1024], F32R)
        ahi = sb("ahi", [P, 2, 16, 256], F32R)
        alo = sb("alo", [P, 2, 16, 256], F32R)
        x = sb("x", [P, 2, D])
        cols = sb("cols", [P, NCOL])
        ident = sb("ident", [P, P])
        mmask = sb("mmask", [P, 256])
        ones = sb("ones", [P, P])
        cact = sb("cact", [P, 16])
        mod = sb("mod", [P, 2, 2, 16])
        dg = sb("dg", [P, 2, P])
        stat = sb("stat", [P, 64])
        mhalf = sb("mhalf", [P, 64])
        NA = 16860
        arena = sb("arena", [P, NA])
        ps = [ctx.enter_context(nc.psum_tensor(f"ps{i}", [P, 512], F32)) for i in range(8)]

        s_raw = [sem(f"s_raw{i}", 16) for i in range(RAW)]
        s_in = [sem(f"s_in{i}", 16) for i in range(16)]
        s_out = sem("s_out", 16)
        pe = Line(sem("s_pe"))
        act = Line(sem("s_act"))
        dve = Line(sem("s_dve"), steps=True)
        pool = Line(sem("s_pool"), steps=True)
        sp = Line(None)

        class Region:
            def __init__(self):
                self.off = 0

            def __call__(self, *shape):
                n = int(np.prod(shape))
                a = arena[:, self.off:self.off + n]
                self.off += n
                assert self.off <= NA, self.off
                if len(shape) == 2:
                    a = a.rearrange("p (a b) -> p a b", a=shape[0])
                if len(shape) == 3:
                    a = a.rearrange("p (a b c) -> p a b c", a=shape[0], b=shape[1])
                return a

        def col(name, i=0, n=1):
            a = COLS[name][0] + i
            return cols[:, a:a + n]

        def load(i, dst, src, *waits):
            return sp(lambda e: e.dma_start(dst, src), *waits, count=s_in[i])

        free = deque((b, None) for b in range(8))

        def take():
            return free.popleft()

        def release(b, tok):
            free.append((b, tok))

        plan = stream_plan()
        state = {"next": 0, "w": 0, "used": 0}
        raw_read = [()] * RAW
        ring_read = [None] * RING
        ready = {}
        acc = {}
        side = deque()
        urgent = deque()

        def pump(upto, stop=None):
            while state["next"] < (stop or len(plan)) and (stop or state["w"] <= upto):
                n = state["next"]
                state["next"] += 1
                kind = plan[n][0]
                slot = n % RAW
                if kind == "w":
                    _, name, idx, ncol = plan[n]
                    r = raw[:, slot, 0:ncol]
                    t_in = sp(lambda e, r=r, s=ins[name][idx]: e.dma_start(r, s), *raw_read[slot], count=s_raw[slot])
                    i = state["w"]
                    state["w"] += 1
                    q = i % RING
                    hi, lo = whi[:, q, 0:ncol], wlo[:, q, 0:ncol]
                    t_hi = act(lambda e, hi=hi, r=r: e.activation(hi, r, ACT.Copy), t_in, ring_read[q])
                    line = pool if i < POOLED and i % 4 == 3 else dve
                    t_lo = line(lambda e, hi=hi, lo=lo, r=r: e.tensor_tensor(lo, r, hi.bitcast(F32), ALU.subtract),
                                t_hi, ring_read[q], free=True)
                    ready[i] = (q, t_hi, t_lo)
                    raw_read[slot] = (t_hi, t_lo)
                else:
                    _, layer, g, k = plan[n]
                    r = raw[:, slot, :]
                    t_in = sp(lambda e, r=r, s=ins["ada"][layer, g, k]: e.dma_start(r, s), *raw_read[slot], count=s_raw[slot])
                    raw_read[slot] = (ada_block(layer, g, k, r, t_in),)

        def ada_block(layer, g, k, r, t_in):
            while k == 3 and urgent:
                urgent.popleft()[1]()
            m = acc.get("n", 0)
            bufs = late_accs if layer and g > 3 else accs
            main, other = bufs[m % 2], bufs[(m + 1) % 2]
            second = k > 2 and k % 2 == 1
            a = other if second else main
            ck = cact[:, k:k + 1]
            if k in (0, 3):
                t = dve(lambda e: e.tensor_scalar(a, r, ck, None, ALU.mult), t_in, t_cact, acc.get(("read", k == 3)), acc.get("late"), free=True)
            else:
                t = dve(lambda e: e.scalar_tensor_tensor(out=a, in0=r, scalar=ck, in1=a, op0=ALU.mult, op1=ALU.add),
                        t_in, acc["t", second], free=True)
            acc["t", second] = t
            if k == 15:
                ts = dve(lambda e: e.tensor_tensor(main, main, other, ALU.add), t, acc["t", False])
                if g > 3:
                    bias = gate[0:1, (g - 4) * 1024:(g - 3) * 1024]
                    ts = dve(lambda e: e.tensor_tensor(main[0:1, :], main[0:1, :], bias, ALU.add), ts, gate_tok["bias", layer])
                    gate_tok["bias read"] = ts
                acc["read", False] = ts
                urgent.append((state["used"] + (1 if layer == 0 and g < 4 else 3), lambda: ada_done(layer, g, main, ts)))
                acc["n"] = m + 1
            return t

        def ada_done(layer, g, a, t):
            if g < 4:
                o = mod[:, layer, :, 4 * g:4 * g + 4]
                a0 = COLS["ada_b"][0] + layer * 32
                bc = cols[:, a0:a0 + 32].rearrange("p (c j) -> p c j", c=2)[:, :, 4 * g:4 * g + 4]
            if layer == 0 and g < 4:
                b, w = take()
                for j in range(8):
                    tm = pe(lambda e, j=j: e.matmul(ps[b][:, j:j + 1], a[:, j * P:(j + 1) * P], ones[:, 0:1],
                                                    start=True, stop=True), t, w, t_ones, inc=(j == 7))
                acc["read", True] = tm
                tb = dve(lambda e: e.tensor_tensor(o, ps[b][:, 0:8].rearrange("p (c j) -> p c j", c=2), bc, ALU.add), tm, t_cols)
                release(b, tb)
            else:
                got = [take() for _ in range(2)]
                for j, (b, w) in enumerate(got):
                    tm = pe(lambda e, b=b, j=j: e.matmul(ps[b][:, :], ones[:, :], a[:, j * 512:j * 512 + 512], start=True, stop=True), t, w, t_ones)
                if g > 3:
                    acc["read", True] = tm
                    for j, (b, w) in enumerate(got):
                        o = gate[:, (g - 4) * 1024 + j * 512:(g - 4) * 1024 + j * 512 + 512]
                        gate_tok[layer] = act(lambda e, b=b, o=o: e.activation(o, ps[b][:, :], ACT.Copy), tm, gate_tok["bias", layer])
                        release(b, gate_tok[layer])
                    return
                for j, (b, w) in enumerate(got):
                    tb = dve(lambda e, b=b, j=j: e.tensor_tensor(
                        a[:, j * 512:j * 512 + 512].rearrange("p (c d) -> p c d", c=4), ps[b][:, :].rearrange("p (c d) -> p c d", c=4),
                        ident[:, :].unsqueeze(1).to_broadcast([P, 4, P]), ALU.mult), tm, t_id)
                    release(b, tb)
                a4 = a.rearrange("p (c j d) -> p c j d", c=2, j=4)
                acc["read", True] = tb = dve(lambda e: e.tensor_reduce(o, a4, AX_X, ALU.add), tb)
                tb = dve(lambda e: e.tensor_tensor(o, o, bc, ALU.add), tb, t_cols)
            oa = mod[:, layer, 1, 4 * g:4 * g + 4]
            ng = col("norm_g", layer * 16 + 4 * g, 4)
            tb = dve(lambda e: e.scalar_tensor_tensor(out=oa, in0=oa, scalar=1.0, in1=ng, op0=ALU.add, op1=ALU.mult), tb)
            mod_tok[layer, g] = tb

        at_tok = [[None] * 16 for _ in range(2)]
        at_read = [[None] * 16 for _ in range(2)]

        def step_jobs():
            if urgent and state["used"] >= urgent[0][0]:
                urgent.popleft()[1]()
            elif side:
                job = side.popleft()
                if job:
                    job()

        def drain():
            while urgent:
                urgent.popleft()[1]()
            while side:
                job = side.popleft()
                if job:
                    job()

        def next_block(held=0):
            i = state["used"]
            state["used"] += 1
            pump(i + RING - 1 - held)
            return ready.pop(i)

        def run_ahead():
            pump(state["used"] + RING - 1)

        def gemm(slot, kbs, ncol, evac, tail=TAIL):
            order = [(n, tb) for tb in range(2) for n in range(ncol // 512)]
            got = {key: take() for key in order}
            kbs = list(kbs)
            head = len(kbs) - tail
            toks = {}

            def mm(key, kb, q, m, t_w, first, last, inc):
                n, tb = key
                b, w = got[key]
                xs = (ahi, alo, ahi)[m][:, slot, kb, tb * P:(tb + 1) * P]
                ws = (whi, whi, wlo)[m][:, q, n * 512:n * 512 + 512]
                return pe(lambda e: e.matmul(ps[b][:, :], xs, ws, start=first, stop=last),
                          w if first else None, t_w, at_tok[slot][kb], inc=inc)

            for i in range(head):
                q, t_hi, t_lo = next_block()
                kb = kbs[i]
                for tb in range(2):
                    for m in range(3):
                        for key in order:
                            if key[1] == tb:
                                tok = mm(key, kb, q, m, t_lo if m == 2 else t_hi, i == 0 and m == 0, False,
                                         m == 2 and key == order[-1])
                ring_read[q] = at_read[slot][kb] = tok
                step_jobs()
            blocks = [next_block(j) for j in range(tail)]
            for c, key in enumerate(order):
                for j, (q, t_hi, t_lo) in enumerate(blocks):
                    kb = kbs[head + j]
                    for m in range(3):
                        end = j == tail - 1 and m == 2
                        tok = mm(key, kb, q, m, t_lo if m == 2 else t_hi, head + j == 0 and m == 0, end,
                                 m == 2 and (end or key == order[-1]))
                    if key == order[-1]:
                        ring_read[q] = at_read[slot][kb] = tok
                toks[key] = tok
                if 0 < c < tail:
                    step_jobs()
            evac({k: v[0] for k, v in got.items()}, toks)
            step_jobs()

        def gemm_t(slot, kbs, evac):
            got = [take() for _ in range(4)]
            last = len(kbs) - 1
            for i, kb in enumerate(kbs):
                q, t_hi, t_lo = next_block()
                xh, xl = ahi[:, slot, kb, :], alo[:, slot, kb, :]
                for m, (xs, ws) in enumerate(((xh, whi), (xl, whi), (xh, wlo))):
                    for c in range(8):
                        b, w = got[c // 2]
                        tok = pe(lambda e, b=b, xs=xs, ws=ws, c=c, m=m, i=i, q=q: e.matmul(
                            ps[b][:, (c % 2) * 256:(c % 2) * 256 + 256], ws[:, q, c * P:(c + 1) * P], xs,
                            start=(i == 0 and m == 0 and c % 2 == 0), stop=(i == last and m == 2), skip_group_check=True),
                            w if i == 0 and m == 0 else None, t_lo if m == 2 else t_hi, at_tok[slot][kb],
                            inc=(m == 2 and c == 7))
                ring_read[q] = tok
                at_read[slot][kb] = tok
                if i != last:
                    step_jobs()
            evac([b for b, _ in got], tok)
            step_jobs()

        def xpose(blocks, *waits):
            b, w = take()
            for i, s in enumerate(blocks):
                tok = pe(lambda e, i=i, s=s: e.transpose(ps[b][:, i * P:(i + 1) * P], s, ident[:, :]),
                         w, t_id, *waits, inc=(i == len(blocks) - 1))
            return b, tok

        def split_at(slot, kb0, nb, b, tok, scale=None):
            parts = [(0, nb)] if scale is None else [(j, 1) for j in range(nb)]
            ops = []
            for j, n in parts:
                src = ps[b][:, j * 256:(j + n) * 256]
                hi = ahi[:, slot, kb0 + j:kb0 + j + n, :].rearrange("p a b -> p (a b)")
                lo = alo[:, slot, kb0 + j:kb0 + j + n, :].rearrange("p a b -> p (a b)")
                war = [at_read[slot][kb0 + j + m] for m in range(n)]
                sc = 1.0 if scale is None else scale(j)
                t1 = act(lambda e, hi=hi, src=src, sc=sc: e.activation(hi, src, ACT.Copy, scale=sc), tok, t_cols, *war)
                ops.append((src, hi, lo, sc, [kb0 + j + m for m in range(n)]))
            for src, hi, lo, sc, kbs in ops:
                t2 = dve(lambda e, hi=hi, lo=lo, src=src, sc=sc: e.scalar_tensor_tensor(
                    out=lo, in0=src, scalar=sc, in1=hi.bitcast(F32), op0=ALU.mult, op1=ALU.subtract), t1, free=True)
                for kb in kbs:
                    at_tok[slot][kb] = t2
            release(b, t2)

        def rstd_of(dst, src, n, *waits):
            w = dst.shape[-1]
            t = pool(lambda e: e.tensor_scalar(dst, src, 1.0 / n, EPS, ALU.mult, ALU.add), *waits)
            return pool(lambda e: e.tensor_tensor(dst, dst, mhalf[:, 0:w], ALU.pow), t, t_mhalf)

        def square(o, tb, c, src, junk, *waits):
            N["sq", o, tb, c] = act(lambda e: e.activation(junk, src, ACT.Square, accum_out=stat[:, o + 4 * tb + c:o + 4 * tb + c + 1]), *waits)

        def mean_square(o):
            return dve(lambda e: e.tensor_reduce(stat[:, o + 8:o + 10], stat[:, o:o + 8].rearrange("p (t c) -> p t c", t=2), AX_X, ALU.add),
                       *[N["sq", o, tb, c] for tb in range(2) for c in range(4)])

        def diagonals(r, *waits):
            for tb in range(2):
                N["dg"] = dve(lambda e, tb=tb: e.tensor_scalar(dg[:, tb, :], ident[:, :], r[:, tb:tb + 1], None, ALU.mult), t_id, N.get("dgT"), *waits)

        def norm_diag(o):
            diagonals(stat[:, o + 10:o + 12], rstd_of(stat[:, o + 10:o + 12], stat[:, o + 8:o + 10], D, mean_square(o)))

        def norm_turn(k2):
            b, w = take()
            for j in range(2):
                for tb in range(2):
                    kb = 2 * k2 + j
                    tok = pe(lambda e, j=j, tb=tb, kb=kb: e.matmul(
                        ps[b][:, (2 * j + tb) * P:(2 * j + tb + 1) * P], x[:, tb, kb * P:(kb + 1) * P], dg[:, tb, :], start=True, stop=True),
                        w, N["dg"], inc=(j == 1 and tb == 1))
            N["dgT"] = tok
            return b, tok

        def norm_at(slot, k2, layer=None, scale=None, tmp=None, turned=None):
            b, tok = turned or norm_turn(k2)
            if layer is None:
                split_at(slot, 2 * k2, 2, b, tok, lambda j: scale[:, 2 * k2 + j:2 * k2 + j + 1])
                return
            tt = tmp[:, (k2 % 2) * 512:(k2 % 2) * 512 + 512]
            for j in range(2):
                kb = 2 * k2 + j
                o, src = tt[:, j * 256:j * 256 + 256], ps[b][:, j * 256:j * 256 + 256]
                a, s = mod[:, layer, 1, kb:kb + 1], mod[:, layer, 0, kb:kb + 1]
                waits = (tok, mod_tok[layer, kb // 4], N.get(("tmp", k2 % 2)))
                if k2 % 2:
                    t0 = act(lambda e, o=o, src=src, a=a, s=s: e.activation(o, src, ACT.Identity, scale=a, bias=s), *waits)
                else:
                    t0 = dve(lambda e, o=o, src=src, a=a, s=s: e.tensor_scalar(o, src, a, s, ALU.mult, ALU.add), *waits)
            release(b, t0)
            hi, lo = (a[:, slot, 2 * k2:2 * k2 + 2, :].rearrange("p a b -> p (a b)") for a in (ahi, alo))
            t1 = act(lambda e: e.activation(hi, tt, ACT.Copy), t0, at_read[slot][2 * k2], at_read[slot][2 * k2 + 1])
            t2 = dve(lambda e: e.tensor_tensor(lo, tt, hi.bitcast(F32), ALU.subtract), t1)
            N["tmp", k2 % 2] = at_tok[slot][2 * k2] = at_tok[slot][2 * k2 + 1] = t2

        def rope(dst, src, tok, heads, half, tabs, tb, scr, war=None):
            n = heads * half
            v = src[:, 0:2 * n].rearrange("p (h c d) -> p h c d", h=heads, c=2)
            d = dst.rearrange("p (h c d) -> p h c d", h=heads, c=2)
            s = [scr[:, i * 512:i * 512 + 2 * n].rearrange("p (h c d) -> p h c d", h=heads, c=2) for i in range(2)]
            for i, (o, t) in enumerate(zip(s, tabs)):
                f = t[:, tb, :].unsqueeze(1).unsqueeze(1).to_broadcast([P, heads, 2, half])
                t_s = dve(lambda e, o=o, f=f: e.tensor_tensor(o, v, f, ALU.mult), tok, N["rope"], free=i == 1)
            dve(lambda e: e.tensor_tensor(d[:, :, 0, :], s[0][:, :, 0, :], s[1][:, :, 1, :], ALU.subtract), t_s, war)
            t = dve(lambda e: e.tensor_tensor(d[:, :, 1, :], s[0][:, :, 1, :], s[1][:, :, 0, :], ALU.add), t_s, war, free=True)
            return t_s, t

        def attend(heads, masks, scale, nm, dn, S, ET, st, scores, values):
            def stage1():
                for third in range(3):
                    b, w = take()
                    hs = heads if third == 0 else heads[2 * third - 2:2 * third]
                    nk = P if third == 0 else 256
                    qs = slice(0, P) if third == 0 else slice(P, 256)
                    for i, h in enumerate(hs):
                        ops = scores(h, qs, slice(0, nk))
                        for j, (l, r, rdy) in enumerate(ops):
                            tok = pe(lambda e, b=b, i=i, j=j, l=l, r=r, nk=nk, m=len(ops): e.matmul(
                                ps[b][:, i * nk:(i + 1) * nk], l, r, start=(j == 0), stop=(j == m - 1)),
                                w, *rdy, inc=(i == len(hs) - 1 and j == len(ops) - 1))
                    n = len(hs)
                    sv = S[:, third, :].rearrange("p (h k) -> p h k", h=n)
                    mk = masks[0 if third == 0 else 1].unsqueeze(1).to_broadcast([P, n, nk])
                    tb, o = (0, 0) if third == 0 else (1, 2 * third - 2)
                    nmx, den = nm[:, tb, o:o + n], dn[:, tb, o:o + n]
                    t0 = dve(lambda e, sv=sv, b=b, mk=mk, n=n: e.tensor_tensor(
                        sv, ps[b][:, :].rearrange("p (h k) -> p h k", h=n), mk, ALU.add), tok, t_mask[0], st.get(("S", third)))
                    release(b, t0)
                    t1 = dve(lambda e, sv=sv, nmx=nmx: e.tensor_reduce(nmx, sv, AX_X, ALU.max), t0)
                    t2 = dve(lambda e, nmx=nmx: e.tensor_scalar(nmx, nmx, -scale, None, ALU.mult), t1)
                    for i in range(n):
                        t3 = act(lambda e, sv=sv, i=i, nmx=nmx, den=den: e.activation(
                            sv[:, i, :], sv[:, i, :], ACT.Exp, bias=nmx[:, i:i + 1], scale=scale, accum_out=den[:, i:i + 1]), t2)
                    st["E", third] = t3
            def stage2():
                for third in range(3):
                    b, tok = xpose([S[:, third, i * P:(i + 1) * P] for i in range(4)], st["E", third])
                    st["S", third] = tok
                    t = act(lambda e, b=b, third=third: e.activation(ET[:, third, :], ps[b][:, :], ACT.Copy), tok, st.get(("ET", third)))
                    st["T", third] = t
                    release(b, t)
            def stage3():
                values(lambda tb, i: ([(ET[:, 0, i * P:(i + 1) * P], 0)] if tb == 0 else
                                      [(ET[:, 1 + i // 2, (i % 2) * 256 + m * P:(i % 2) * 256 + (m + 1) * P], m) for m in range(2)]),
                       [st["T", i] for i in range(3)])
            return [stage1, stage2, stage3]

        K = ins["consts"]
        t_cols = load(0, cols[:, :], ins["cols"])
        t_id = load(2, ident[:, :], K[:, K_ID:K_ID + P])
        R0 = Region()
        accs = [R0(1024), R0(1024)]
        gate = R0(D)
        cos128, sin128, cos32, sin32 = R0(2, P), R0(2, P), R0(2, 32), R0(2, 32)
        base = R0.off
        dtab = R0(8, 256)
        rp = R0(2, 2, 512)
        scr = R0(1024)
        qT, kT = R0(4, 256), R0(4, 256)
        v = R0(2, 1024)
        sg = R0(2, 1024)
        sT = R0(2, 384)
        yn = qT.rearrange("p a b -> p (a b)").rearrange("p (a b) -> p a b", a=2)
        bn = R0(4, 16)
        R0b = Region()
        R0b.off = base + 2048
        pos = R0b(2).bitcast(I32)
        posf = R0b(2)
        freq, ang, kk, rr, rc, mm_ = R0b(160), R0b(2, 160), R0b(2, 160), R0b(2, 160), R0b(2, 160), R0b(2, 160)
        t_pos = load(3, pos, ins["pos"])
        t_freq = load(4, freq, K[:, K_FREQ:K_FREQ + 160])
        t_ones = pool(lambda e: e.memset(ones[:, :], 1.0))
        t_mhalf = pool(lambda e: e.memset(mhalf[:, :], -0.5))
        mod_tok, gate_tok, N = {}, {}, {}
        t_cact = act(lambda e: e.activation(cact[:, :], col("c", 0, 16), ACT.Silu), t_cols)
        pump(0, 10)
        t_x = load(1, x[:, :, :], ins["x"].rearrange("o (t p) d -> p (o t) d", p=P))
        for tb in range(2):
            for c in range(4):
                junk = scr[:, (c % 2) * 512:(c % 2) * 512 + 512]
                square(0, tb, c, x[:, tb, c * 512:c * 512 + 512], junk, t_x, N.get(("junk", c % 2)))
                N["junk", c % 2] = N["sq", 0, tb, c]
        pump(0, 14)
        norm_diag(0)
        pump(0, 16)
        turned = [norm_turn(k2) for k2 in range(2)]
        drain()
        for k2 in range(2):
            norm_at(0, k2, layer=0, tmp=scr, turned=turned[k2])

        def at0(q):
            return [lambda k2=k2: norm_at(0, k2, layer=0, tmp=scr) for k2 in (2 * q, 2 * q + 1)]

        t_mask = [load(7, mmask[:, :], K[:, K_MLA:K_MLA + 256])]

        def angles():
            t = dve(lambda e: e.tensor_copy(posf, pos), t_pos)
            for tb in range(2):
                t1 = dve(lambda e, tb=tb: e.tensor_scalar(ang[:, tb, :], freq, posf[:, tb:tb + 1], None, ALU.mult), t, t_freq)
            t = dve(lambda e: e.tensor_scalar(kk, ang, 1.0 / (2.0 * PI), MAGIC, ALU.mult, ALU.add), t1)
            N["rope"] = dve(lambda e: e.tensor_scalar(kk, kk, MAGIC, None, ALU.subtract), t)

        def reduced():
            for i, cc in enumerate((C1, C2, C3)):
                src = ang if i == 0 else rr
                N["rope"] = dve(lambda e, cc=cc, src=src: e.scalar_tensor_tensor(out=rr, in0=kk, scalar=-cc, in1=src, op0=ALU.mult, op1=ALU.add), N["rope"])

        def tables():
            t = dve(lambda e: e.tensor_scalar(mm_, rr, PI / 2, -2.0 * PI, ALU.is_gt, ALU.mult), N["rope"])
            t = dve(lambda e: e.scalar_tensor_tensor(out=rc, in0=rr, scalar=PI / 2, in1=mm_, op0=ALU.add, op1=ALU.add), t)
            t = dve(lambda e: e.tensor_scalar(rc, rc, PI_IN, -PI_IN, ALU.min, ALU.max), t)
            t = dve(lambda e: e.tensor_scalar(rr, rr, PI_IN, -PI_IN, ALU.min, ALU.max), t)
            for o, s, a in ((cos128, rc, 0), (sin128, rr, 0), (cos32, rc, 128), (sin32, rr, 128)):
                w = o.shape[-1]
                N["rope"] = act(lambda e, o=o, s=s, a=a, w=w: e.activation(o, s[:, :, a:a + w], ACT.Sin), t)

        side += [angles, reduced, tables]

        L = {}

        def qk_evac(banks, toks):
            for tb in range(2):
                for n in range(2):
                    b = banks[n, tb]
                    L["part", "qk", n, tb] = act(lambda e, b=b, o=qk_part(n, tb): e.activation(o, ps[b][:, :], ACT.Copy),
                                                 toks[n, tb], L["scores"], L["z", 0], L["z", 1])
                    release(b, L["part", "qk", n, tb])

        def qk_rope(name, part, n, tb):
            L["rp", n] = rope(rp[:, n, tb, :], part(n, tb), L["part", name, n, tb], 2, 128, (cos128, sin128), tb, scr, L.get(("rpT", n)))[1]

        def qk_ropes(name, part):
            return [lambda n=n, tb=tb: qk_rope(name, part, n, tb) for n in range(2) for tb in range(2)]

        def qk_turn(n, j):
            blocks = [rp[:, n, tb, (2 * j + i) * P:(2 * j + i + 1) * P] for i in range(2) for tb in range(2)]
            b, tok = xpose(blocks, L["rp", n])
            L["rpT", n] = tok
            dst = (qT, kT)[n][:, 2 * j:2 * j + 2, :].rearrange("p a b -> p (a b)")
            L["qkT", n, j] = act(lambda e: e.activation(dst, ps[b][:, :], ACT.Copy), tok, L.get("scores"), L.get(("z", 0)), L.get(("z", 1)))
            release(b, L["qkT", n, j])

        def v_evac(banks, toks):
            for tb in range(2):
                for n in range(2):
                    b = banks[n, tb]
                    L["v"] = act(lambda e, b=b, n=n, tb=tb: e.activation(v[:, tb, n * 512:n * 512 + 512], ps[b][:, :], ACT.Copy),
                                 toks[n, tb], L.get("pv"))
                    release(b, L["v"])

        def g_evac(banks, toks):
            for tb in range(2):
                for n in range(2):
                    b = banks[n, tb]
                    L["sg"] = act(lambda e, b=b, n=n, tb=tb: e.activation(sg[:, tb, n * 512:n * 512 + 512], ps[b][:, :], ACT.Silu),
                                  toks[n, tb], L.get("zT"))
                    release(b, L["sg"])

        def ret_scores(p, h):
            b, w = take()
            for lo_, n, q0 in ((0, 256, 0), (256, 128, 128)):
                for c in range(2):
                    tok = pe(lambda e, lo_=lo_, n=n, q0=q0, c=c: e.matmul(
                        ps[b][:, lo_:lo_ + n], kT[:, 2 * h + c, q0:q0 + P], qT[:, 2 * h + c, q0:q0 + n],
                        start=(c == 0), stop=(c == 1)), w, L["qkT", 0, h], L["qkT", 1, h], inc=(q0 == 128 and c == 1))
            L["scores"] = tok
            dt = dtab[:, 2 * p + h, :]
            t = dve(lambda e: e.tensor_tensor(sT[:, h, 0:256], ps[b][:, 0:256], dt, ALU.mult), tok, t_D[p], L.get(("sTr", h)))
            L["sT", h] = dve(lambda e: e.tensor_tensor(sT[:, h, 256:384], ps[b][:, 256:384], dt[:, 0:P], ALU.mult), tok)
            release(b, L["sT", h])

        def ret_values(p, h):
            hs = slice(h * 512, h * 512 + 512)
            bs = bn[:, 2 * h:2 * h + 2, :]
            for tb in range(2):
                L["bank", h, tb] = b, w = take()
                if tb == 0:
                    tok = pe(lambda e, b=b: e.matmul(ps[b][:, :], sT[:, h, 0:P], v[:, 0, hs], start=True, stop=True), w, L["sT", h], L["v"])
                else:
                    pe(lambda e, b=b: e.matmul(ps[b][:, :], sT[:, h, P:256], v[:, 0, hs], start=True, stop=False), w, inc=False)
                    tok = pe(lambda e, b=b: e.matmul(ps[b][:, :], sT[:, h, 256:384], v[:, 1, hs], start=False, stop=True))
                L["pv"] = L["sTr", h] = tok
                t = dve(lambda e, b=b, tb=tb: e.bn_stats(bs[:, tb, 0:6], ps[b][:, :]), tok)
                t = dve(lambda e, tb=tb: e.bn_aggr(bs[:, tb, 6:8], bs[:, tb, 0:6]), t)
            L["rstd", h] = rstd_of(bs[:, :, 8], bs[:, :, 7], 1, t)

        def ret_norm(h):
            bs = bn[:, 2 * h:2 * h + 2, :]
            t = dve(lambda e: e.scalar_tensor_tensor(out=bs[:, :, 9], in0=bs[:, :, 6], scalar=-1.0, in1=bs[:, :, 8], op0=ALU.mult, op1=ALU.mult), L["rstd", h])
            for tb in range(2):
                b = L["bank", h, tb][0]
                L["yn", tb] = act(lambda e, b=b, tb=tb: e.activation(yn[:, tb, :], ps[b][:, :], ACT.Identity, scale=bs[:, tb, 8:9], bias=bs[:, tb, 9:10]),
                                  t, L["scores"], L.get(("z", tb)))
                release(b, L["yn", tb])

        def ret_gate(h):
            hs = slice(h * 512, h * 512 + 512)
            for tb in range(2):
                L["z", tb] = dve(lambda e, tb=tb: e.tensor_tensor(sg[:, tb, hs], yn[:, tb, :], sg[:, tb, hs], ALU.mult), L["yn", tb], L["sg"], free=tb == 1)

        def ret_jobs(p):
            jobs = [lambda h=h: ret_scores(p, h) for h in range(2)]
            for f in (lambda h: ret_values(p, h), ret_norm, ret_gate):
                jobs += [lambda h=h, f=f: f(h) for h in range(2)]
            return jobs[:4] + [jobs[4], jobs[6], jobs[5], jobs[7]]

        def ret_turn(p, j):
            blocks = [sg[:, tb, (2 * j + i) * P:(2 * j + i + 1) * P] for i in range(2) for tb in range(2)]
            b, tok = xpose(blocks, L["z", 0], L["z", 1])
            L["zT"] = tok
            split_at(1, (p % 2) * 8 + 2 * j, 2, b, tok, lambda i: col("gn_g", p * 8 + 2 * j + i))

        def parts(ph, buf, name, done):
            def evac(banks, toks):
                for tb in range(2):
                    for n in range(2):
                        b, o = banks[n, tb], buf(n, tb)
                        if ph == 0:
                            t = act(lambda e, b=b, o=o: e.activation(o, ps[b][:, :], ACT.Copy), toks[n, tb])
                        else:
                            t = dve(lambda e, b=b, o=o: e.tensor_tensor(o, ps[b][:, :], o, ALU.add), toks[n, tb], L["part", name, n, tb], free=True)
                        L["part", name, n, tb] = t
                        release(b, t)
                        if ph == 3:
                            done(n, tb, o, t)
                        if ph and n == 1 and tb == 0:
                            run_ahead()
            return evac

        def qk_done(n, tb, o, t):
            pass

        def v_done(n, tb, o, t):
            L["v"] = t

        def v_next_done(n, tb, o, t):
            L["v next"] = t

        def v_copy():
            for tb in range(2):
                L["v"] = L["v copied"] = act(lambda e, tb=tb: e.activation(v[:, tb, :], v_next[:, tb, :], ACT.Copy), L["v next"], L["pv"])

        def g_done(n, tb, o, t):
            L["sg"] = act(lambda e: e.activation(o, o, ACT.Silu), t)

        def qk_part(n, tb):
            return (qT, kT)[n].rearrange("p a b -> p (a b)")[:, tb * 512:tb * 512 + 512]

        v_next = gate.rearrange("p (a b) -> p a b", a=2)

        def qk_next(n, tb):
            return dtab.rearrange("p a b -> p (a b)")[:, (2 * n + tb) * 512:(2 * n + tb) * 512 + 512]

        qk_turns = [lambda n=n, j=j: qk_turn(n, j) for n, j in ((0, 0), (1, 0), (0, 1), (1, 1))]

        def cols_of(buf):
            return lambda n, tb: buf[:, tb, n * 512:n * 512 + 512]

        ytmp = scr
        Y = {}

        def residual(layer, g, summed=None):
            def evac(banks, toks):
                adds = []

                def add():
                    tb, c, cs, tmp, t = adds.pop(0)
                    Y["x", tb, c] = Y["add", c % 2] = L["x"] = dve(
                        lambda e: e.tensor_tensor(x[:, tb, cs], x[:, tb, cs], tmp, ALU.add), t, Y.get(("x", tb, c)), free=True)
                    if summed:
                        summed(tb, c, cs, L["x"])

                for tb in range(2):
                    for n in range(2):
                        b, c = banks[n, tb], 2 * g + n
                        cs = slice(c * 512, c * 512 + 512)
                        tmp = Y["tmp"][:, n * 512:n * 512 + 512]
                        if len(adds) == 2:
                            add()
                        t = dve(lambda e, b=b, cs=cs, tmp=tmp: e.tensor_tensor(tmp, ps[b][:, :], gate[:, cs], ALU.mult),
                                toks[n, tb], gate_tok[layer], Y.get(("add", n)), free=(tb, n) != (0, 0))
                        release(b, t)
                        adds.append((tb, c, cs, tmp, t))
                        Y["g"] = t
                while adds:
                    add()
            return evac

        def sums0(tb, c, cs, t):
            square(16, tb, c, x[:, tb, cs], qT.rearrange("p a b -> p (a b)")[:, 0:512], t, L["scores"], N.get("junk0"))
            N["junk0"] = N["sq", 16, tb, c]

        Y["tmp"] = ytmp
        for ph, kbs in enumerate(PHASES):
            for name, buf, done in (("qk", qk_part, qk_done), ("v", cols_of(v), v_done), ("g", cols_of(sg), g_done),
                                    ("qk next", qk_next, qk_done), ("v next", cols_of(v_next), v_next_done)):
                if ph < 3 and name == "v next":
                    side += at0(ph + 1)
                gemm(0, kbs, 1024, parts(ph, buf, name, done))
                if ph == 3 and name == "qk":
                    side += qk_ropes(name, qk_part) + qk_turns
                if ph == 3 and name == "qk next":
                    side += qk_ropes(name, qk_next)
            drain()
        t_D = {}

        def load_decays(p):
            t_D[p] = load((6, 12, 13, 14)[p], dtab[:, 2 * p:2 * p + 2, :],
                          K[:, K_D + p * 512:K_D + p * 512 + 512].rearrange("p (a b) -> p a b", a=2), L["rp", 0], L["rp", 1])

        load_decays(0)

        def load_gate(layer, i, *waits):
            gate_tok["bias", layer] = load(i, gate[0:1, :], ins["ada_b"][layer:layer + 1, 2 * D:3 * D], *waits)

        for p in range(4):
            if p >= 2:
                gemm(0, range(16), 1024, qk_evac)
                side += [None] + qk_ropes("qk", qk_part) + [None] + qk_turns
                gemm(0, range(16), 1024, v_evac)
            if p:
                load_decays(p)
                gemm(0, range(16), 1024, g_evac)
            if p == 1:
                load_gate(0, 5, L["v copied"])
            side += ret_jobs(p)
            if p == 0:
                side += [v_copy] + qk_turns[:2]
            if p == 2:
                for g in range(2):
                    gemm(1, range(16), 1024, residual(0, g))
                drain()
            side += [None] * (0, 1, 0, 2)[p] + [lambda j=j, p=p: ret_turn(p, j) for j in range(4)]
            if p == 0:
                side += qk_turns[2:]
        for g in range(2):
            gemm(1, range(8), 1024, residual(0, g))
        drain()
        for g in range(2):
            gemm(1, range(8, 16), 1024, residual(0, g, sums0), 1 + g)
        drain()

        R1 = Region()
        R1.off = base
        sg1 = R1(2, 1024)
        rows = R1(2, 1024)
        qT1, kT1 = R1(8, 256), rows.rearrange("p a b -> p (a b)").rearrange("p (a b) -> p a b", a=8)
        v1 = R1(2, 1024)
        qr, qrT = R1(2, 512), R1(4, 256)
        kr = R1(2, P)
        ET = R1(3, 512)
        scr1 = ET.rearrange("p a b -> p (a b)")[:, 0:1024]
        R1a = Region()
        S, krE, krO = R1a(3, 512), R1a(256), R1a(256)
        nm1, dn1 = R1(2, 16), R1(2, 16)
        st1 = R1(8)
        htmp1 = S.rearrange("p a b -> p (a b)")[:, 0:1024]
        norm_diag(16)
        M = {}
        late_accs = [v1.rearrange("p a b -> p (a b)")[:, i * 1024:i * 1024 + 1024] for i in range(2)]
        acc["late"] = acc["read", True]
        load_gate(1, 8, Y["g"])
        def c_evac(banks, toks):
            M["xn"] = t_xn = at_tok[1][15]
            pool(lambda e: e.memset(krE, 0.0), t_xn)
            M["kr0"] = pool(lambda e: e.memset(krO, 0.0), t_xn)
            for n in range(2):
                for tb in range(2):
                    b = banks[n, tb]
                    o = rows[:, tb, n * 512:n * 512 + 512]
                    i = n * 2 + tb
                    t = act(lambda e, b=b, o=o: e.activation(o, ps[b][:, :], ACT.Copy), toks[n, tb], t_xn)
                    t2 = act(lambda e, b=b, i=i: e.activation(S[:, 0, :], ps[b][:, :], ACT.Square, accum_out=st1[:, i:i + 1]), M.get("sq"))
                    M["sq"] = t2
                    release(b, t2)
            M["r"] = rstd_of(st1[:, 4:8], st1[:, 0:4], 512, M["sq"])

        def c_scale(n):
            for tb in range(2):
                o = rows[:, tb, n * 512:n * 512 + 512]
                i = n * 2 + tb
                M["rows", n, tb] = dve(lambda e, o=o, i=i: e.tensor_scalar(o, o, st1[:, 4 + i:5 + i], None, ALU.mult), M["r"])

        def c_turn(n, j):
            blocks = [rows[:, tb, n * 512 + (2 * j + i) * P:n * 512 + (2 * j + i + 1) * P] for i in range(2) for tb in range(2)]
            b, tok = xpose(blocks, M["rows", n, 0], M["rows", n, 1])
            M["rowsT"] = tok
            split_at(0, 4 * n + 2 * j, 2, b, tok, lambda i: col(("qn_g", "kvn_g")[n], 2 * j + i))

        def krope():
            b, w = take()
            q, t_hi, t_lo = next_block()
            for kb in range(16):
                for m, (xs, ws) in enumerate(((ahi, whi), (alo, whi), (ahi, wlo))):
                    tok = pe(lambda e, xs=xs, ws=ws, kb=kb, m=m: e.matmul(
                        ps[b][0:64, 0:256], ws[:, q, kb * 64:kb * 64 + 64], xs[:, 1, kb, :],
                        start=(kb == 0 and m == 0), stop=(kb == 15 and m == 2)), w, t_hi, t_lo, at_tok[1][kb],
                        inc=(kb == 15 and m == 2))
            ring_read[q] = tok
            M["krow"] = act(lambda e: e.activation(scr1[0:64, 0:256], ps[b][0:64, 0:256], ACT.Copy), tok, M["xn"])
            release(b, M["krow"])

        def krope_rows():
            b, w = take()
            for tb in range(2):
                tok = pe(lambda e, tb=tb: e.transpose(ps[b][:, tb * 64:tb * 64 + 64], scr1[0:64, tb * P:(tb + 1) * P], ident[0:64, 0:64]),
                         w, M["krow"], inc=(tb == 1))
            v4 = ps[b][:, 0:128].rearrange("p (t c d) -> p t c d", t=2, c=2)
            s = [scr1[:, 256 + i * 64:320 + i * 64].rearrange("p (t d) -> p t d", t=2) for i in range(4)]
            ts = []
            for o, a, f in ((s[0], v4[:, :, 0, :], cos32), (s[1], v4[:, :, 1, :], sin32), (s[2], v4[:, :, 1, :], cos32), (s[3], v4[:, :, 0, :], sin32)):
                ts.append(dve(lambda e, o=o, a=a, f=f: e.tensor_tensor(o, a, f, ALU.mult), tok, N["rope"]))
            release(b, ts[3])
            for o in (0, 64):
                dve(lambda e, o=o: e.tensor_tensor(kr[:, :, o:o + 32], s[0], s[1], ALU.subtract), ts[1])
                M["kr"] = dve(lambda e, o=o: e.tensor_tensor(kr[:, :, o + 32:o + 64], s[2], s[3], ALU.add), ts[3])

        def kr_turn():
            b, tok = xpose([kr[:, 0, :], kr[:, 1, :]], M["kr"])
            act(lambda e: e.activation(krE[0:64, :], ps[b][0:64, 0:256], ACT.Copy), tok, M["kr0"])
            M["krT"] = act(lambda e: e.activation(krO[64:128, :], ps[b][64:128, 0:256], ACT.Copy))
            release(b, M["krT"])

        def g1_evac(h):
            def evac(banks, toks):
                for tb in range(2):
                    for n in range(2):
                        b = banks[n, tb]
                        M["sg", h] = act(lambda e, b=b, n=n, tb=tb: e.activation(sg1[:, tb, n * 512:n * 512 + 512], ps[b][:, :], ACT.Silu), toks[n, tb], M.get("zT"))
                        release(b, M["sg", h])
            return evac

        def heads_evac(name, dst, last):
            def evac(banks, tok):
                for j, b in enumerate(banks):
                    o = dst[:, 2 * j:2 * j + 2, :].rearrange("p a b -> p (a b)")
                    if j % 2:
                        M[name, 1] = t = act(lambda e, b=b, o=o: e.activation(o, ps[b][:, :], ACT.Copy), tok, M.get(last), M["rowsT"])
                    else:
                        M[name, 0] = t = dve(lambda e, b=b, o=o: e.tensor_copy(o, ps[b][:, :]), tok, M.get(last), M["rowsT"])
                    release(b, t)
            return evac

        def qr_evac(banks, toks):
            for tb in range(2):
                b = banks[0, tb]
                t_b, M["qr"] = rope(qr[:, tb, :], ps[b], toks[0, tb], 8, 32, (cos32, sin32), tb, scr1, M.get("qrT_read"))
                release(b, t_b)

        def qr_turn(j):
            blocks = [qr[:, tb, (2 * j + i) * P:(2 * j + i + 1) * P] for i in range(2) for tb in range(2)]
            b, tok = xpose(blocks, M["qr"])
            M["qrT_read"] = tok
            M["qrT"] = act(lambda e: e.activation(qrT[:, 2 * j:2 * j + 2, :].rearrange("p a b -> p (a b)"), ps[b][:, :], ACT.Copy), tok, M.get("scores"))
            release(b, M["qrT"])

        def v1_evac(banks, toks):
            for tb in range(2):
                for n in range(2):
                    b = banks[n, tb]
                    M["v"] = act(lambda e, b=b, n=n, tb=tb: e.activation(v1[:, tb, n * 512:n * 512 + 512], ps[b][:, :], ACT.Copy),
                                 toks[n, tb], M.get("pv"))
                    release(b, M["v"])

        A = {}

        def mla_scores(h, qs, ks):
            rdy = (M["q", 0], M["q", 1], M["k", 0], M["k", 1], M["qrT"], M["krT"])
            return [(qT1[:, h, qs], kT1[:, h, ks], rdy),
                    (qrT[:, h // 2, qs], (krE, krO)[h % 2][:, ks], ())]

        def mla_values(half, quad):
            def values(parts, rdy):
                dn = dn1[:, :, quad * 4:quad * 4 + 4]
                t_r = dve(lambda e: e.reciprocal(dn, dn), *rdy)
                M["scores"] = A["S", 2]
                for tb in range(2):
                    b, w = take()
                    for i in range(4):
                        hh = quad * 4 + i
                        ops = parts(tb, i)
                        for j, (l, m) in enumerate(ops):
                            tok = pe(lambda e, b=b, i=i, hh=hh, l=l, m=m, j=j, k=len(ops): e.matmul(
                                ps[b][:, i * P:(i + 1) * P], l, v1[:, m, hh * P:(hh + 1) * P], start=(j == 0), stop=(j == k - 1)),
                                w, M["v"], *rdy, inc=(i == 3 and j == len(ops) - 1))
                    M["pv"] = tok
                    for third in range(3):
                        A["ET", third] = tok
                    for i in range(4):
                        hh = quad * 4 + i
                        z = sg1[:, tb, hh * P:(hh + 1) * P]
                        M["z"] = dve(lambda e, b=b, i=i, tb=tb, z=z, hh=hh: e.scalar_tensor_tensor(
                            out=z, in0=ps[b][:, i * P:(i + 1) * P], scalar=dn1[:, tb, hh:hh + 1], in1=z, op0=ALU.mult, op1=ALU.mult),
                            tok, t_r, M["sg", half])
                    release(b, M["z"])
            return values

        def z_turn(half, j):
            blocks = [sg1[:, tb, (2 * j + i) * P:(2 * j + i + 1) * P] for i in range(2) for tb in range(2)]
            b, tok = xpose(blocks, M["z"])
            M["zT"] = tok
            split_at(half, (8 if half == 0 else 0) + 2 * j, 2, b, tok)

        def mla_half(half):
            att = [attend(list(range(4 * quad, 4 * quad + 4)), (mmask[:, P:256], mmask[:, :]), 192.0 ** -0.5,
                          nm1[:, :, quad * 4:quad * 4 + 4], dn1[:, :, quad * 4:quad * 4 + 4], S, ET, A, mla_scores, mla_values(half, quad))
                   for quad in range(2)]
            turn = [lambda j=j: z_turn(half, j) for j in range(4)]
            return [att[0][0], None, att[0][1], None, att[0][2], att[1][0], turn[0], turn[1], att[1][1], None, att[1][2], None, None, turn[2], turn[3]]

        for k2 in range(2):
            norm_at(1, k2, layer=1, tmp=htmp1)
        side += [lambda k2=k2: norm_at(1, k2, layer=1, tmp=htmp1) for k2 in range(2, 8)]
        gemm(1, range(16), 1024, c_evac)
        side += [None, lambda: c_scale(0), lambda: c_scale(1), lambda: c_turn(0, 0), lambda: c_turn(0, 1), lambda: c_turn(1, 0), lambda: c_turn(1, 1)]
        krope()
        side += [krope_rows, None, kr_turn]
        gemm(1, range(16), 1024, g1_evac(0))
        drain()
        for half in range(2):
            gemm_t(0, range(0, 4), heads_evac("q", qT1, "scores"))
            gemm(0, range(0, 4), 512, qr_evac)
            side += [None] * 3 + [lambda j=j: qr_turn(j) for j in range(2)]
            gemm_t(0, range(4, 8), heads_evac("k", kT1, "scores"))
            gemm(0, range(4, 8), 1024, v1_evac)
            drain()
            side += mla_half(half)
            if half == 0:
                gemm(1, range(16), 1024, g1_evac(1))
                drain()
        Y["tmp"] = qr.rearrange("p a b -> p (a b)")
        fg = qT1.rearrange("p a b -> p (a b)")
        xf = v1.rearrange("p a b -> p (a b)")

        def sums1(tb, c, cs, t):
            i = 2 * tb + c % 2
            o = xf[:, i * 512:i * 512 + 512]
            square(32, tb, c, x[:, tb, cs], S[:, 0, :], t, A["S", 2], N.get("junk1"))
            t = pool(lambda e: e.tensor_tensor(o, x[:, tb, cs], fg[:, cs], ALU.mult), t, t_fg, M["pv"], N.get(("xf", i)))
            square(48, tb, c, o, o, t)
            N["junk1"] = N["sq", 32, tb, c]
            N["xf", i] = N["sq", 48, tb, c]

        for half in range(2):
            for g in range(2):
                gemm(half, range(8, 16) if half == 0 else range(0, 8), 1024, residual(1, g, sums1 if half else None), 1 + g)
            drain()
            if half == 0:
                t_fg = load(9, fg, ins["final_norm_g"].unsqueeze(0).to_broadcast([P, D]), M["scores"], M["pv"])

        r1, r2 = stat[:, 42:44], stat[:, 58:60]
        t1 = mean_square(32)
        t = dve(lambda e: e.tensor_scalar(r2, stat[:, 40:42], EPS / D, EPS * EPS, ALU.mult, ALU.add), t1)
        t2 = mean_square(48)
        t = dve(lambda e: e.scalar_tensor_tensor(out=r2, in0=stat[:, 56:58], scalar=1.0 / D, in1=r2, op0=ALU.mult, op1=ALU.add), t2)
        t = pool(lambda e: e.tensor_tensor(r2, r2, mhalf[:, 0:2], ALU.pow), t, t_mhalf)
        t_r1 = rstd_of(r1, stat[:, 40:42], D, t1)
        gg = stat[:, 0:16]
        t_gg = dve(lambda e: e.tensor_tensor(gg, col("final_g", 0, 16), col("attn_g", 0, 16), ALU.mult), t_cols, N["dgT"])
        diagonals(r2, t)

        def final_x(tb, c):
            cs = slice(c * 1024, c * 1024 + 1024)
            L["x"] = dve(lambda e: e.scalar_tensor_tensor(out=x[:, tb, cs], in0=x[:, tb, cs], scalar=r1[:, tb:tb + 1], in1=fg[:, cs],
                                                          op0=ALU.mult, op1=ALU.mult), N["dgT"], t_r1, t_fg)

        R2 = Region()
        qk = R2(2, 1536)
        qT2 = R2(6, 256)
        kE, kO = R2(6, 256), R2(6, 256)
        v2 = R2(2, 768)
        S2, ET2 = R2(3, 512), R2(3, 512)
        bmask = R2(3, 384)
        yc = R2(2, 768)
        nm2, dn2 = R2(2, 3, 4), R2(2, 3, 4)
        lse, cf, mx, t4 = R2(2, 3, 4), R2(2, 3, 4), R2(2, 4), R2(2, 4)
        hs_, hr = R2(2, 24), R2(2, 24)
        av = ET2.rearrange("p a b -> p (a b)")[:, 0:1024].rearrange("p (a b) -> p a b", a=2)
        au = R2(2, 512)
        wsT = yc.rearrange("p a b -> p (a b)")[:, 0:1024].rearrange("p (a b) -> p a b", a=8)
        sq = S2.rearrange("p a b -> p (a b)")
        Rc = Region()
        Rc.off = 3072 + 1536 + 3072 + 1536 + 1536
        bt, yb, zp = Rc(256), Rc(256), Rc(2, 258)
        qk_flat = qk.rearrange("p a b -> p (a b)")
        zz = qk_flat[:, 0:1536].rearrange("p (a b) -> p a b", a=2)
        bb = qk_flat[:, 1536:3072].rearrange("p (a b) -> p a b", a=2)
        B = {}
        for k2 in range(2):
            norm_at(0, k2, scale=gg)
        side += [lambda k2=k2: norm_at(0, k2, scale=gg) for k2 in range(2, 8)]
        side += [lambda tb=tb, c=c: final_x(tb, c) for tb in range(2) for c in range(2)]

        def small_loads():
            t_ws = load(10, wsT, ins["sgu_wT"], L["x"])
            B["bm"] = t_mask[0] = load(11, bmask, K[:, K_B2:K_B2 + 3 * 384].rearrange("p (a b) -> p a b", a=3), L["x"])
            B["ws"] = pool(lambda e: e.affine_select(out=wsT, in_=wsT, compare_op=ALU.is_ge, fill=0.0, base=0,
                                                     pattern=[[0, 8], [1, P]], channel_multiplier=-1), t_ws)
            pool(lambda e: e.memset(kE, 0.0), at_tok[0][15])
            B["kz"] = pool(lambda e: e.memset(kO, 0.0), at_tok[0][15])

        side.append(small_loads)
        def copies(*moves):
            def evac(banks, toks):
                for tb in range(2):
                    for n in range(2):
                        if (n, tb) not in banks:
                            continue
                        b = banks[n, tb]
                        for mn, cs, dst, name, war in moves:
                            if mn == n:
                                B[name] = t = act(lambda e, b=b, cs=cs, d=dst(tb): e.activation(d, ps[b][:, cs], ACT.Copy),
                                                  toks[n, tb], L["x"], B.get(war))
                        release(b, t)
            return evac

        full = slice(0, 512)

        def head_norm(tb):
            t = dve(lambda e: e.tensor_tensor(sq, qk[:, tb, :], qk[:, tb, :], ALU.mult), B["qk0"], B["qk1"], B["qk2"], B.get("hn"))
            t = dve(lambda e: e.tensor_reduce(hs_[:, tb, :], sq.rearrange("p (h d) -> p h d", h=24), AX_X, ALU.add), t)
            B["hn"] = t
            B["hr", tb] = rstd_of(hr[:, tb, :], hs_[:, tb, :], 64, t)

        def head_scale(tb):
            q3 = qk[:, tb, :].rearrange("p (h d) -> p h d", h=24)
            B["qkn", tb] = dve(lambda e: e.tensor_tensor(q3, q3, hr[:, tb, :].unsqueeze(2).to_broadcast([P, 24, 64]), ALU.mult), B["hr", tb])

        def qk2_turn(j):
            blocks = [qk[:, tb, (2 * j + i) * P:(2 * j + i + 1) * P] for i in range(2) for tb in range(2)]
            b, tok = xpose(blocks, B["qkn", 0], B["qkn", 1])
            B["qkT"] = tok
            if j < 3:
                B["qT"] = t = act(lambda e: e.activation(qT2[:, 2 * j:2 * j + 2, :].rearrange("p a b -> p (a b)"), ps[b][:, :], ACT.Copy,
                                                         scale=col("q_g")), tok)
            else:
                for half, dst in ((slice(0, 64), kE), (slice(64, 128), kO)):
                    B["kT"] = t = act(lambda e, half=half, dst=dst: e.activation(
                        dst[half, 2 * j - 6:2 * j - 4, :].rearrange("p a b -> p (a b)"), ps[b][half, :], ACT.Copy,
                        scale=cols[half, COLS["k_g"][0]:COLS["k_g"][1]]), tok, B["kz"])
            release(b, t)

        def c_scores(h, qs, ks):
            return [(qT2[:, h // 2, qs], (kE, kO)[h % 2][:, h // 2, ks], (B["qT"], B["kT"]))]

        A2 = {}

        def c_values(g):
            def values(parts, rdy):
                b, w = take()
                for tb in range(2):
                    for i in range(4):
                        h = 4 * g + i
                        ops = parts(tb, i)
                        for j, (l, m) in enumerate(ops):
                            tok = pe(lambda e, tb=tb, i=i, l=l, m=m, j=j, k=len(ops), h=h: e.matmul(
                                ps[b][:, tb * 256 + i * 64:tb * 256 + (i + 1) * 64], l, v2[:, m, h * 64:(h + 1) * 64],
                                start=(j == 0), stop=(j == k - 1)), w, B["v0"], B["v1"], *rdy, inc=(tb == 1 and i == 3 and j == 1))
                for third in range(3):
                    A2["ET", third] = tok
                B["yc"] = act(lambda e: e.activation(yc[:, :, g * 256:(g + 1) * 256], ps[b][:, :].rearrange("p (t c) -> p t c", t=2), ACT.Copy), tok)
                release(b, B["yc"])
            return values

        def mixture():
            t = act(lambda e: e.activation(lse, dn2, ACT.Ln), B["yc"])
            t = dve(lambda e: e.tensor_tensor(lse, lse, nm2, ALU.subtract), t)
            t = dve(lambda e: e.tensor_tensor(mx, lse[:, :, 0, :], lse[:, :, 1, :], ALU.max), t)
            t = dve(lambda e: e.tensor_tensor(mx, mx, lse[:, :, 2, :], ALU.max), t)
            for g in range(3):
                t1 = dve(lambda e, g=g: e.tensor_tensor(cf[:, :, g, :], lse[:, :, g, :], mx, ALU.subtract), t)
            t = act(lambda e: e.activation(cf, cf, ACT.Exp), t1)
            t = dve(lambda e: e.tensor_tensor(t4, cf[:, :, 0, :], cf[:, :, 1, :], ALU.add), t)
            t = dve(lambda e: e.tensor_tensor(t4, t4, cf[:, :, 2, :], ALU.add), t)
            for g in range(3):
                t1 = dve(lambda e, g=g: e.tensor_tensor(lse[:, :, g, :], dn2[:, :, g, :], t4, ALU.mult), t)
            t = dve(lambda e: e.reciprocal(lse, lse), t1)
            t = dve(lambda e: e.tensor_tensor(cf, cf, lse, ALU.mult), t)
            for tb in range(2):
                y3 = yc[:, tb, :].rearrange("p (h d) -> p h d", h=12)
                c3 = cf[:, tb, :, :].rearrange("p g i -> p (g i)").unsqueeze(2).to_broadcast([P, 12, 64])
                B["ycn", tb] = dve(lambda e, y3=y3, c3=c3: e.tensor_tensor(y3, y3, c3, ALU.mult), t)

        def yc_turn(j):
            blocks = [yc[:, tb, (2 * j + i) * P:(2 * j + i + 1) * P] for i in range(2) for tb in range(2)]
            b, tok = xpose(blocks, B["ycn", 0], B["ycn", 1])
            split_at(1, 10 + 2 * j, 2, b, tok)

        def gating(tb):
            b, w = take()
            for h in range(8):
                tok = pe(lambda e, h=h: e.matmul(ps[b][:, h * 64:(h + 1) * 64], wsT[:, h, :], av[:, tb, h * 64:(h + 1) * 64], start=True, stop=True),
                         w, B["ws"], B["av"], inc=(h == 7))
            a3 = av[:, tb, :].rearrange("p (h d) -> p h d", h=8)
            b3 = col("sgu_b", 0, 8).unsqueeze(2).to_broadcast([P, 8, 64])
            t = dve(lambda e: e.tensor_tensor(a3, ps[b][:, :].rearrange("p (h d) -> p h d", h=8), b3, ALU.add), tok, t_cols)
            release(b, t)
            B["ya", tb] = dve(lambda e: e.tensor_tensor(au[:, tb, :], au[:, tb, :], av[:, tb, :], ALU.mult), t, B["au"])

        def ya_turn(j):
            blocks = [au[:, tb, (2 * j + i) * P:(2 * j + i + 1) * P] for i in range(2) for tb in range(2)]
            b, tok = xpose(blocks, B["ya", 0], B["ya", 1])
            B["yaT"] = tok
            split_at(1, 2 * j, 2, b, tok)

        def cx_evac(n_c, c_cols, n_x, x_cols, dst_cols, other=None):
            def evac(banks, toks):
                for tb in range(2):
                    bc, bx = banks[n_c, tb], banks[n_x, tb]
                    z = zz[:, tb, dst_cols]
                    t = act(lambda e, bc=bc, z=z: e.activation(z, ps[bc][:, c_cols], ACT.Copy), toks[n_c, tb], B["qkT"])
                    t = dve(lambda e, bx=bx, z=z: e.tensor_tensor(z, z, ps[bx][:, x_cols], ALU.mult), t, toks[n_x, tb])
                    B["z", tb] = t
                    release(bx, t)
                    if n_c != n_x:
                        release(bc, t)
                    if other is not None:
                        bo = banks[1, tb]
                        B["b0"] = act(lambda e, bo=bo, tb=tb: e.activation(bb[:, tb, 0:512], ps[bo][:, :], ACT.Copy), toks[1, tb])
                        release(bo, B["b0"])
            return evac

        def conv_turn(f):
            blocks = [a[:, tb, f * P:(f + 1) * P] for a in (zz, bb) for tb in range(2)]
            b, tok = xpose(blocks, B["z", 0], B["z", 1], B["b0"], B["b1"])
            zq = zp[:, f % 2, :]
            t = act(lambda e: e.activation(zq[:, 2:258], ps[b][:, 0:256], ACT.Copy), tok, B["zp0"], B.get(("zp", f % 2)))
            t = dve(lambda e: e.tensor_scalar(bt, zq[:, 0:256], col("conv", 3 * f), None, ALU.mult), t)
            t = dve(lambda e: e.scalar_tensor_tensor(out=bt, in0=zq[:, 1:257], scalar=col("conv", 3 * f + 1), in1=bt, op0=ALU.mult, op1=ALU.add), t)
            t = dve(lambda e: e.scalar_tensor_tensor(out=bt, in0=zq[:, 2:258], scalar=col("conv", 3 * f + 2), in1=bt, op0=ALU.mult, op1=ALU.add), t)
            B["zp", f % 2] = t
            t = dve(lambda e: e.tensor_tensor(yb, bt, ps[b][:, 256:512], ALU.mult), t, B.get("yb"))
            release(b, t)
            hi, lo = ahi[:, 1, 4 + f, :], alo[:, 1, 4 + f, :]
            t1 = act(lambda e: e.activation(hi, yb, ACT.Copy), t, at_read[1][4 + f])
            at_tok[1][4 + f] = B["yb"] = dve(lambda e: e.tensor_tensor(lo, yb, hi.bitcast(F32), ALU.subtract), t1)

        gemm(0, range(16), 1024, copies((0, full, lambda tb: qk[:, tb, 0:512], "qk0", None), (1, full, lambda tb: qk[:, tb, 512:1024], "qk1", None)))
        gemm(0, range(16), 1024, copies((0, full, lambda tb: qk[:, tb, 1024:1536], "qk2", None), (1, full, lambda tb: v2[:, tb, 0:512], "v0", None)))
        side += [lambda: head_norm(0), lambda: head_norm(1), lambda: head_scale(0), lambda: head_scale(1), None, None, None]
        side += [lambda j=j: qk2_turn(j) for j in range(6)]
        gemm(0, range(16), 1024, copies((0, full, lambda tb: av[:, tb, :], "av", None), (1, full, lambda tb: au[:, tb, :], "au", None)))
        side += [None, lambda: gating(0), lambda: gating(1), None, None, lambda: ya_turn(0), lambda: ya_turn(1)]
        gemm(0, range(16), 512, copies((0, slice(0, 256), lambda tb: bb[:, tb, 512:768], "b1", "qkT"),
                                       (0, slice(256, 512), lambda tb: v2[:, tb, 512:768], "v1", None)))
        drain()
        for third in range(3):
            A2["ET", third] = B["yaT"]
        B["yc"] = B["yaT"]
        for g in range(3):
            a, b, c = attend(list(range(4 * g, 4 * g + 4)), (bmask[:, g, 0:P], bmask[:, g, P:384]), 0.125,
                             nm2[:, :, g, :], dn2[:, :, g, :], S2, ET2, A2, c_scores, c_values(g))
            side += [a, None, b, None, c, None]
        side += [mixture, None, None, None] + [lambda j=j: yc_turn(j) for j in range(3)]
        gemm(0, range(16), 1024, cx_evac(0, full, 1, full, slice(0, 512)))
        gemm(0, range(16), 1024, cx_evac(0, slice(0, 256), 0, slice(256, 512), slice(512, 768), other=True))
        drain()
        B["zp0"] = pool(lambda e: e.memset(zp, 0.0), A2["ET", 2])
        side += [None] + [lambda f=f: conv_turn(f) for f in range(6)]

        Y["x"] = L["x"]

        def add_x(g, final=False, summed=None):
            def evac(banks, toks):
                for tb in range(2):
                    for n in range(2):
                        b = banks[n, tb]
                        cs = slice(g * 1024 + n * 512, g * 1024 + n * 512 + 512)
                        key = ("x", tb, 2 * g + n)
                        Y[key] = L["x"] = dve(lambda e, b=b, cs=cs, tb=tb: e.tensor_tensor(x[:, tb, cs], ps[b][:, :], x[:, tb, cs], ALU.add),
                                              toks[n, tb], Y[key], Y["x"], free=True)
                        release(b, L["x"])
                        if summed:
                            summed(tb, 2 * g + n, cs, L["x"])
                        if final:
                            L["out"] = sp(lambda e, cs=cs, tb=tb: e.dma_start(out[0, tb * P:(tb + 1) * P, cs], x[:, tb, cs]), L["x"], count=s_out)
            return evac

        def sums2(tb, c, cs, t):
            square(16, tb, c, x[:, tb, cs], S2[:, 0, :], t, A2["ET", 2], N.get("junk2"))
            N["junk2"] = N["sq", 16, tb, c]

        order = list(range(0, 4)) + list(range(10, 16)) + list(range(4, 10))
        for g in range(2):
            gemm(1, order, 1024, add_x(g, summed=sums2), 1 + g)
        drain()

        norm_diag(16)
        for k2 in range(2):
            norm_at(0, k2, scale=col("mlp_g", 0, 16))
        side += [lambda k2=k2: norm_at(0, k2, scale=col("mlp_g", 0, 16)) for k2 in range(2, 8)]
        R3 = Region()
        u = R3(2, 2, 1024)
        U = {}

        def u_evac(g):
            def evac(banks, toks):
                for tb in range(2):
                    for n in range(2):
                        b = banks[n, tb]
                        o = u[:, g % 2, tb, n * 512:n * 512 + 512]
                        t = act(lambda e, b=b, o=o: e.activation(o, ps[b][:, :], ACT.Relu), toks[n, tb], U.get(("uT", g % 2)))
                        release(b, t)
                        U["u", g] = dve(lambda e, o=o: e.tensor_tensor(o, o, o, ALU.mult), t)
            return evac

        def u_turn(g, j):
            blocks = [u[:, g % 2, tb, (2 * j + i) * P:(2 * j + i + 1) * P] for i in range(2) for tb in range(2)]
            b, tok = xpose(blocks, U["u", g])
            U["uT", g % 2] = tok
            split_at(1, (g % 2) * 8 + 2 * j, 2, b, tok)

        for g in range(8):
            gemm(0, range(16), 1024, u_evac(g))
            side += [None] * 2 + [lambda g=g, j=j: u_turn(g, j) for j in range(4)]
            if g == 0:
                continue
            for n in range(2):
                gemm(1, range(((g - 1) % 2) * 8, ((g - 1) % 2) * 8 + 8), 1024, add_x(n))
        drain()
        for n in range(2):
            gemm(1, range(8, 16), 1024, add_x(n, final=True), 1 + n)
        assert not side and not urgent and state["used"] == state["w"] and state["next"] == len(plan)
        t_out = L["out"]

        block = ctx.enter_context(nc.Block())

        @block.sync
        def _(eng):
            sp.play(eng)
            eng.wait_ge(t_out[0].handle, t_out[1])

        @block.scalar
        def _(eng):
            act.play(eng)

        @block.vector
        def _(eng):
            dve.play(eng)

        @block.gpsimd
        def _(eng):
            pool.play(eng)

        @block.tensor
        def _(eng):
            pe.play(eng)


def constants():
    k = np.zeros((P, NCONST), np.float32)
    k[:, K_ID:K_ID + P] = np.eye(P, dtype=np.float32)
    i = np.arange(P)
    t = np.arange(256)
    k[:, K_MLA + P:K_MLA + 256] = np.where(i[None, :] <= i[:, None], 0.0, NEG)
    for d, a in ((256, 0), (64, 128)):
        f = 10000.0 ** (-np.arange(0, d, 2, dtype=np.float64) / d)
        k[:, K_FREQ + a:K_FREQ + a + d // 2] = f.astype(np.float32)[None, :]
    for h in range(8):
        lg = np.log1p(-np.exp2(-5.0 - h))
        diff = t[None, :] - i[:, None]
        k[:, K_D + h * 256:K_D + (h + 1) * 256] = np.where(diff >= 0, np.exp(lg * np.maximum(diff, 0)), 0.0) / 16.0
    for g, (w, d) in enumerate(((128, 1), (512, 4), (2048, 16))):
        def mask(q, s):
            gap = q[:, None] - s[None, :]
            return np.where((gap >= 0) & (gap <= w) & (gap % d == 0), 0.0, NEG)
        o = K_B2 + g * 384
        k[:, o:o + P] = mask(i, i)
        k[:, o + P:o + 384] = mask(i + P, t)
    return k


def tiles(w, groups, kbs=None):
    kb = w.shape[0] // P
    w3 = w.reshape(kb, P, w.shape[1])
    parts = []
    for cols in groups:
        a = np.concatenate([w3[:, :, s] for s in cols], axis=2) if len(cols) > 1 else w3[:, :, cols[0]]
        parts.append(a[list(kbs)] if kbs is not None else a)
    return np.ascontiguousarray(np.concatenate(parts, axis=0))


def layout(inp):
    a = {k: np.asarray(v) for k, v in inp.items()}
    sl = slice
    g = {}
    w = a["ret_w_in"][0]
    grp = []
    for p in range(4):
        grp += [[sl(p * 512, p * 512 + 512), sl(2048 + p * 512, 2048 + p * 512 + 512)],
                [sl(4096 + p * 1024, 4096 + (p + 1) * 1024)], [sl(8192 + p * 1024, 8192 + (p + 1) * 1024)]]
    g["ret_in"] = tiles(w, grp)
    two = [[sl(0, 1024)], [sl(1024, 2048)]]
    wo = a["ret_w_out"][0]
    g["ret_out"] = np.concatenate([tiles(wo[0:2048], two), tiles(wo[2048:3072], two), tiles(wo[3072:4096], two)])
    w = a["mla_w_in"][0]
    g["mla_in"] = tiles(w, [[sl(0, 1024)], [sl(1088, 2112)], [sl(2112, 3136)]])
    g["mla_kr"] = np.ascontiguousarray(w[:, 1024:1088].reshape(16, P, 64).transpose(1, 0, 2).reshape(1, P, 1024))
    w = a["mla_w_uq"][0].reshape(512, 16, 192)
    g["uq_n"] = tiles(np.ascontiguousarray(w[:, :, 0:128]).reshape(512, 2048), two)
    g["uq_r"] = tiles(np.ascontiguousarray(w[:, :, 128:192]).reshape(512, 1024), [[sl(0, 512)], [sl(512, 1024)]])
    w = a["mla_w_ukv"][0].reshape(512, 16, 256)
    g["ukv_k"] = tiles(np.ascontiguousarray(w[:, :, 0:128]).reshape(512, 2048), two)
    g["ukv_v"] = tiles(np.ascontiguousarray(w[:, :, 128:256]).reshape(512, 2048), two)
    w = a["mla_w_out"][0]
    g["mla_out"] = np.concatenate([tiles(w[0:1024], two), tiles(w[1024:2048], two)])
    w = a["w_in_2"][0]
    au, av, bb, bc, bx, q, k, v = 0, 512, 1024, 1792, 2560, 3328, 4096, 4864
    g["in2"] = tiles(w, [
        [sl(q, q + 768), sl(k, k + 256)], [sl(k + 256, k + 768), sl(v, v + 512)],
        [sl(av, av + 512), sl(au, au + 512)], [sl(bc, bc + 512), sl(bx, bx + 512)],
        [sl(bc + 512, bc + 768), sl(bx + 512, bx + 768), sl(bb, bb + 512)]])
    g["in2h"] = tiles(w, [[sl(bb + 512, bb + 768), sl(v + 512, v + 768)]])
    g["out2"] = tiles(a["w_out_2"][0], two, list(range(0, 4)) + list(range(10, 16)) + list(range(4, 10)))
    g["mlp1"] = tiles(a["w_mlp_in_2"][0], [[sl(i * 1024, (i + 1) * 1024)] for i in range(8)])
    w = a["w_mlp_out_2"][0]
    g["mlp2"] = np.concatenate([tiles(w[i * 1024:(i + 1) * 1024], two) for i in range(8)])
    w = a["ada_w"].reshape(2, 16, P, 3 * D)
    grp = [[sl(q * 512, q * 512 + 512), sl(D + q * 512, D + q * 512 + 512)] for q in range(4)]
    grp += [[sl(2 * D + i * 1024, 2 * D + (i + 1) * 1024)] for i in range(2)]
    g["ada"] = np.ascontiguousarray(np.stack([np.concatenate([w[..., c] for c in cs], axis=-1) for cs in grp], axis=1))
    def colm(v):
        return v.reshape(-1, P).T
    ab = a["ada_b"]
    parts = [colm(a["c"][0]), colm(ab[0, :2 * D]), colm(ab[1, :2 * D]), colm(a["norm_g"].reshape(-1)), colm(a["ret_gn_g"][0]),
             colm(a["mla_q_norm_g"][0]), colm(a["mla_kv_norm_g"][0]), colm(a["attn_norm_2"][0]), colm(a["mlp_norm_2"][0]), colm(a["final_norm_g"]),
             a["conv_w_2"][0].reshape(3, 6, P).transpose(2, 1, 0).reshape(P, 18), a["sgu_b_2"][0].T,
             np.concatenate([a["q_norm_2"][0]] * 2)[:, None], np.concatenate([a["k_norm_2"][0]] * 2)[:, None]]
    g["cols"] = np.ascontiguousarray(np.concatenate(parts, axis=1))
    g["pos"] = np.ascontiguousarray(a["positions"].reshape(2, P).T)
    g["x"] = a["x"]
    g["ada_b"] = ab
    g["final_norm_g"] = a["final_norm_g"]
    g["sgu_wT"] = np.ascontiguousarray(a["sgu_w_2"][0].transpose(2, 0, 1))
    g["consts"] = constants()
    return g


def kernel(**inputs):
    from concourse import bacc, mybir as mb
    from concourse.bass_utils import run_bass_kernel_spmd

    nc = bacc.Bacc("TRN2", target_bir_lowering=False, num_devices=1)
    arrays, ins = {}, {}
    for name, a in layout(inputs).items():
        arrays[f"in_{name}"] = a
        ins[name] = nc.dram_tensor(f"in_{name}", a.shape, mb.dt.from_np(a.dtype), kind="ExternalInput").ap()
    out = nc.dram_tensor("out_0", (1, 256, D), mb.dt.float32, kind="ExternalOutput").ap()
    fused_blocks(nc, ins, out)
    r = run_bass_kernel_spmd(nc, [arrays], core_ids=[0])
    return r.results[0]["out_0"]
```
